# Optimizing a Trainium2 kernel written in Bass

```python
import jax
import jax.numpy as jnp
from jax import lax
import numpy as np

D_MODEL = 1024
BATCH = 1
SEQ = 256
DEPTH = 2

GRID_W = 64
CTX_LEN = 256
EPS = 1e-6
N_MOD = 6

SSD_HEADS = 16
SSD_HEAD_DIM = 64
SSD_INNER = SSD_HEADS * SSD_HEAD_DIM
SSD_GROUPS = 4
SSD_STATE = 128
SSD_CONV = 5
SSD_CHUNK = 128
SSD_BC = SSD_GROUPS * SSD_STATE
SSD_CONV_DIM = SSD_INNER + 2 * SSD_BC
SSD_STATE_COLS = SSD_CONV_DIM + 2 * SSD_HEADS

CF_CH = 1024
CF_KERNEL = 31

AB_IN = SSD_INNER + SSD_STATE_COLS + 2 * CF_CH
AB_OUT = SSD_INNER + CF_CH

HG_HEADS = 8
HG_DK = 128
HG_DV = D_MODEL // HG_HEADS
HG_KEY = HG_HEADS * HG_DK
HG_VAL = HG_HEADS * HG_DV
HG_CHUNK = 64
HG_IN = HG_KEY + 2 * HG_VAL + 2 * HG_KEY

N_EXPERTS = 16
N_EXPERT_GROUPS = 4
EXPERTS_PER_GROUP = N_EXPERTS // N_EXPERT_GROUPS
TOP_K = 2
D_EXPERT = 512

N_EVEN = (DEPTH + 1) // 2
N_ODD = DEPTH // 2


def rmsnorm(x, g):
    xf = x.astype(jnp.float32)
    y = xf * lax.rsqrt(jnp.mean(xf * xf, axis=-1, keepdims=True) + EPS)
    return (y * g.astype(jnp.float32)).astype(x.dtype)

def layernorm(x, g, b):
    xf = x.astype(jnp.float32)
    mu = jnp.mean(xf, axis=-1, keepdims=True)
    xc = xf - mu
    var = jnp.mean(xc * xc, axis=-1, keepdims=True)
    return (xc * lax.rsqrt(var + EPS) * g.astype(jnp.float32) + b.astype(jnp.float32)).astype(x.dtype)

def modulation(cond, w, b):
    m = jax.nn.silu(cond) @ w + b
    return m.reshape(cond.shape[:-1] + (N_MOD, D_MODEL))

def dwconv(x, w, b):
    k = w.shape[0]
    y = lax.conv_general_dilated(x, w[:, None, :].astype(x.dtype), window_strides=(1,),
                                 padding=[(k // 2, k // 2)], dimension_numbers=("NWC", "WIO", "NWC"),
                                 feature_group_count=x.shape[-1])
    return y + b.astype(y.dtype)

def _flip(t):
    return jnp.flip(t, axis=1)

def _same(t):
    return t

def to_col_major(t, rows):
    b, _, ch = t.shape
    return t.reshape(b, rows, GRID_W, ch).transpose(0, 2, 1, 3).reshape(b, rows * GRID_W, ch)

def from_col_major(t, rows):
    b, _, ch = t.shape
    return t.reshape(b, GRID_W, rows, ch).transpose(0, 2, 1, 3).reshape(b, rows * GRID_W, ch)

def _carry_step(s, inp):
    dec, st = inp
    return dec * s + st, s

def ssd_scan(xs, dt, a_neg, bm, cm, s0, with_output):
    bsz, seqlen, nh, hp = xs.shape
    ng, ns = bm.shape[2], bm.shape[3]
    rep = nh // ng
    nc = seqlen // SSD_CHUNK
    la = (dt * a_neg).reshape(bsz, nc, SSD_CHUNK, ng, rep)
    acum = jnp.cumsum(la, axis=2)
    xdt = (xs.astype(jnp.float32) * dt[..., None]).reshape(bsz, nc, SSD_CHUNK, ng, rep, hp)
    bc = bm.astype(jnp.float32).reshape(bsz, nc, SSD_CHUNK, ng, ns)
    to_end = jnp.exp(acum[:, :, -1:] - acum)
    chunk_states = jnp.einsum("bcsgn,bcsgr,bcsgrp->bcgrpn", bc, to_end, xdt).reshape(bsz, nc, nh, hp, ns)
    chunk_decay = jnp.exp(acum[:, :, -1]).reshape(bsz, nc, nh)[..., None, None]
    s_final, s_in = lax.scan(_carry_step, s0, (jnp.moveaxis(chunk_decay, 1, 0), jnp.moveaxis(chunk_states, 1, 0)))
    if not with_output:
        return None, s_final
    s_in = jnp.moveaxis(s_in, 0, 1).reshape(bsz, nc, ng, rep, hp, ns)
    cc = cm.astype(jnp.float32).reshape(bsz, nc, SSD_CHUNK, ng, ns)
    causal = jnp.tril(jnp.ones((SSD_CHUNK, SSD_CHUNK), dtype=bool))[:, :, None, None]
    seg = acum[:, :, :, None] - acum[:, :, None, :]
    decay = jnp.exp(jnp.where(causal, seg, -jnp.inf))
    cb = jnp.einsum("bclgn,bcsgn->bclsg", cc, bc)
    y_diag = jnp.einsum("bclsg,bclsgr,bcsgrp->bclgrp", cb, decay, xdt)
    y_off = jnp.einsum("bclgn,bcgrpn,bclgr->bclgrp", cc, s_in, jnp.exp(acum))
    return (y_diag + y_off).reshape(bsz, seqlen, nh, hp), s_final

def ssd_inputs(p_state, conv_w, conv_b, dt_bias):
    b, n, _ = p_state.shape
    xbc = jax.nn.silu(dwconv(p_state[..., :SSD_CONV_DIM], conv_w, conv_b))
    xs = xbc[..., :SSD_INNER].reshape(b, n, SSD_HEADS, SSD_HEAD_DIM)
    bm = xbc[..., SSD_INNER:SSD_INNER + SSD_BC].reshape(b, n, SSD_GROUPS, SSD_STATE)
    cm = xbc[..., SSD_INNER + SSD_BC:].reshape(b, n, SSD_GROUPS, SSD_STATE)
    dt_raw = p_state[..., SSD_CONV_DIM:].astype(jnp.float32).reshape(b, n, 2, SSD_HEADS)
    dt = jax.nn.softplus(dt_raw + dt_bias.astype(jnp.float32))
    return xs, bm, cm, dt

def ssd_readout(y, xs, z, d_skip, norm_g):
    b, n = y.shape[0], y.shape[1]
    y = y + d_skip.astype(jnp.float32)[:, None] * xs.astype(jnp.float32)
    y = y.reshape(b, n, SSD_INNER) * jax.nn.silu(z.astype(jnp.float32))
    return rmsnorm(y, norm_g)

def conformer_conv(v, gate, dw_w, dw_b, ln_g, ln_b, rows):
    u = v * jax.nn.sigmoid(gate)
    b, n, ch = u.shape
    if rows is not None:
        u = u.reshape(b * rows, GRID_W, ch)
    u = dwconv(u, dw_w, dw_b).reshape(b, n, ch)
    return jax.nn.silu(layernorm(u, ln_g, ln_b))

def even_mixer(hc, hl, w_in, conv_w, conv_b, dt_bias, a_log, d_skip, ssd_g,
               cf_w, cf_b, cf_lng, cf_lnb, w_out, rows, need_ctx):
    a_neg = -jnp.exp(a_log.astype(jnp.float32))
    s_lo, s_hi = SSD_INNER, SSD_INNER + SSD_STATE_COLS
    pl = hl @ w_in
    if need_ctx:
        pc = hc @ w_in
        pc_state = pc[..., s_lo:s_hi]
    else:
        pc_state = hc @ w_in[:, s_lo:s_hi]
    xs_l, b_l, c_l, dt_l = ssd_inputs(pl[..., s_lo:s_hi], conv_w, conv_b, dt_bias)
    xs_c, b_c, c_c, dt_c = ssd_inputs(pc_state, conv_w, conv_b, dt_bias)
    bsz = hl.shape[0]
    ys_c, ys_l = [], []
    for d in range(2):
        flip = _flip if d else _same
        s0 = jnp.zeros((bsz, SSD_HEADS, SSD_HEAD_DIM, SSD_STATE), jnp.float32)
        y_c, s_ctx = ssd_scan(flip(xs_c), flip(dt_c[:, :, d]), a_neg[d], flip(b_c), flip(c_c), s0, need_ctx)
        y_l, _ = ssd_scan(flip(xs_l), flip(dt_l[:, :, d]), a_neg[d], flip(b_l), flip(c_l), s_ctx, True)
        ys_l.append(flip(y_l))
        if need_ctx:
            ys_c.append(flip(y_c))
    cf0 = SSD_INNER + SSD_STATE_COLS
    o_ssd = ssd_readout(ys_l[0] + ys_l[1], xs_l, pl[..., :SSD_INNER], d_skip, ssd_g)
    o_cf = conformer_conv(pl[..., cf0:cf0 + CF_CH], pl[..., cf0 + CF_CH:], cf_w, cf_b, cf_lng, cf_lnb, rows)
    y_lat = (jnp.concatenate([o_ssd, o_cf.astype(o_ssd.dtype)], axis=-1) @ w_out).astype(hl.dtype)
    y_ctx = None
    if need_ctx:
        oc_ssd = ssd_readout(ys_c[0] + ys_c[1], xs_c, pc[..., :SSD_INNER], d_skip, ssd_g)
        oc_cf = conformer_conv(pc[..., cf0:cf0 + CF_CH], pc[..., cf0 + CF_CH:], cf_w, cf_b, cf_lng, cf_lnb, None)
        y_ctx = (jnp.concatenate([oc_ssd, oc_cf.astype(oc_ssd.dtype)], axis=-1) @ w_out).astype(hc.dtype)
    return y_ctx, y_lat

def hgrn2_scan(q, k, v, logf, s0, with_output):
    bsz, seqlen, nh, dk = k.shape
    dv = v.shape[-1]
    nc = seqlen // HG_CHUNK

    def chunks(t):
        return t.astype(jnp.float32).reshape(bsz, nc, HG_CHUNK, nh, t.shape[-1])

    kc, vc = chunks(k), chunks(v)
    gcum = jnp.cumsum(chunks(logf), axis=2)
    g_end = gcum[:, :, -1]
    k_end = kc * jnp.exp(g_end[:, :, None] - gcum)
    chunk_states = jnp.einsum("bcshk,bcshv->bchkv", k_end, vc)
    s_final, s_in = lax.scan(_carry_step, s0, (jnp.moveaxis(jnp.exp(g_end)[..., None], 1, 0),
                                               jnp.moveaxis(chunk_states, 1, 0)))
    if not with_output:
        return None, s_final
    s_in = jnp.moveaxis(s_in, 0, 1)
    qc = chunks(q)
    g_mid = gcum[:, :, HG_CHUNK // 2 - 1:HG_CHUNK // 2]
    q_rel = qc * jnp.exp(gcum - g_mid)
    k_rel = kc * jnp.exp(g_mid - gcum)
    causal = jnp.tril(jnp.ones((HG_CHUNK, HG_CHUNK), dtype=bool))
    att = jnp.where(causal, jnp.einsum("bclhk,bcshk->bchls", q_rel, k_rel), 0.0)
    o_intra = jnp.einsum("bchls,bcshv->bclhv", att, vc)
    o_inter = jnp.einsum("bclhk,bchkv->bclhv", qc * jnp.exp(gcum), s_in)
    return (o_intra + o_inter).reshape(bsz, seqlen, nh, dv), s_final

def hgrn2_gates(p_state, lb):
    b, n, _ = p_state.shape
    v = p_state[..., :HG_VAL].reshape(b, n, HG_HEADS, HG_DV)
    f_raw = p_state[..., HG_VAL:].astype(jnp.float32).reshape(b, n, 2, HG_HEADS, HG_DK)
    lbh = lb.reshape(HG_HEADS, HG_DK)
    f = lbh + (1.0 - lbh) * jax.nn.sigmoid(f_raw)
    return v, 1.0 - f, jnp.log(f)

def hgrn2_readout(o, g, norm_g):
    b, n = o.shape[0], o.shape[1]
    return rmsnorm(o, norm_g).reshape(b, n, HG_VAL) * jax.nn.silu(g.astype(jnp.float32))

def odd_mixer(hc, hl, w_in, lb, norm_g, w_out, rows, need_ctx):
    st0 = HG_KEY + HG_VAL
    bsz, n_lat = hl.shape[0], hl.shape[1]
    pl = to_col_major(hl, rows) @ w_in
    q_l = jax.nn.silu(pl[..., :HG_KEY]).reshape(bsz, n_lat, HG_HEADS, HG_DK)
    v_l, k_l, lf_l = hgrn2_gates(pl[..., st0:], lb)
    if need_ctx:
        pc = hc @ w_in
        q_c = jax.nn.silu(pc[..., :HG_KEY]).reshape(bsz, hc.shape[1], HG_HEADS, HG_DK)
        pc_state = pc[..., st0:]
    else:
        pc_state = hc @ w_in[:, st0:]
    v_c, k_c, lf_c = hgrn2_gates(pc_state, lb)
    os_c, os_l = [], []
    for d in range(2):
        flip = _flip if d else _same
        s0 = jnp.zeros((bsz, HG_HEADS, HG_DK, HG_DV), jnp.float32)
        qc_d = flip(q_c) if need_ctx else None
        o_c, s_ctx = hgrn2_scan(qc_d, flip(k_c[:, :, d]), flip(v_c), flip(lf_c[:, :, d]), s0, need_ctx)
        o_l, _ = hgrn2_scan(flip(q_l), flip(k_l[:, :, d]), flip(v_l), flip(lf_l[:, :, d]), s_ctx, True)
        os_l.append(flip(o_l))
        if need_ctx:
            os_c.append(flip(o_c))
    y_lat = from_col_major(hgrn2_readout(os_l[0] + os_l[1], pl[..., HG_KEY:st0], norm_g) @ w_out, rows).astype(hl.dtype)
    y_ctx = None
    if need_ctx:
        y_ctx = (hgrn2_readout(os_c[0] + os_c[1], pc[..., HG_KEY:st0], norm_g) @ w_out).astype(hc.dtype)
    return y_ctx, y_lat

def moe(h, router_w, router_b, w_gate, w_up, w_down):
    shp = h.shape
    t = h.reshape(-1, D_MODEL)
    scores = jax.nn.sigmoid((t @ router_w).astype(jnp.float32))
    sel = scores + router_b.astype(jnp.float32)
    grouped = sel.reshape(-1, N_EXPERT_GROUPS, EXPERTS_PER_GROUP)
    group_score = lax.top_k(grouped, TOP_K)[0].sum(-1)
    g_idx = jnp.argmax(group_score, axis=-1)
    idx = jnp.broadcast_to(g_idx[:, None, None], (t.shape[0], 1, EXPERTS_PER_GROUP))
    in_group = jnp.take_along_axis(grouped, idx, axis=1)[:, 0]
    _, local = lax.top_k(in_group, TOP_K)
    expert_idx = g_idx[:, None] * EXPERTS_PER_GROUP + local
    wts = jnp.take_along_axis(scores, expert_idx, axis=1)
    wts = wts / jnp.sum(wts, axis=-1, keepdims=True)
    combine = jnp.sum(jax.nn.one_hot(expert_idx, N_EXPERTS, dtype=jnp.float32) * wts[..., None], axis=1)

    def expert(acc, p):
        wg, wu, wd, gate_col = p
        y = (jax.nn.silu(t @ wg) * (t @ wu)) @ wd
        return acc + gate_col[:, None] * y, None

    out, _ = lax.scan(expert, jnp.zeros(t.shape, jnp.float32), (w_gate, w_up, w_down, combine.T))
    return out.reshape(shp).astype(h.dtype)

def first_inputs(seed: int = 0) -> dict:
    key = jax.random.key(seed)
    ks = jax.random.split(key, 32)
    f32 = jnp.float32

    def dense(k, shape, fan_in, scale=1.0):
        return scale * fan_in ** -0.5 * jax.random.normal(k, shape, f32)

    def gain(k, shape):
        return 1.0 + 0.1 * jax.random.normal(k, shape, f32)

    def small(k, shape, s=0.02):
        return s * jax.random.normal(k, shape, f32)

    dt0 = jnp.exp(jax.random.uniform(ks[14], (N_EVEN, 2, SSD_HEADS), f32, np.log(1e-3), np.log(1e-1)))
    return {
        "x": jax.random.normal(ks[0], (BATCH, SEQ, D_MODEL), f32),
        "c": jax.random.normal(ks[1], (BATCH, D_MODEL), f32),
        "ctx": jax.random.normal(ks[2], (BATCH, CTX_LEN, D_MODEL), f32),
        "c_ctx": jax.random.normal(ks[3], (D_MODEL,), f32),
        "mod_w": dense(ks[4], (DEPTH, D_MODEL, N_MOD * D_MODEL), D_MODEL, 0.5),
        "mod_b": small(ks[5], (DEPTH, N_MOD * D_MODEL)),
        "norm_mix_g": gain(ks[6], (DEPTH, D_MODEL)),
        "norm_ffn_g": gain(ks[7], (DEPTH, D_MODEL)),
        "router_w": dense(ks[8], (D_MODEL, N_EXPERTS), D_MODEL),
        "router_b": small(ks[9], (N_EXPERTS,), 0.01),
        "moe_w_gate": dense(ks[10], (DEPTH, N_EXPERTS, D_MODEL, D_EXPERT), D_MODEL),
        "moe_w_up": dense(ks[11], (DEPTH, N_EXPERTS, D_MODEL, D_EXPERT), D_MODEL),
        "moe_w_down": dense(ks[12], (DEPTH, N_EXPERTS, D_EXPERT, D_MODEL), D_EXPERT),
        "ab_w_in": dense(ks[13], (N_EVEN, D_MODEL, AB_IN), D_MODEL),
        "ssd_conv_w": dense(ks[15], (N_EVEN, SSD_CONV, SSD_CONV_DIM), SSD_CONV),
        "ssd_conv_b": small(ks[16], (N_EVEN, SSD_CONV_DIM)),
        "ssd_dt_bias": dt0 + jnp.log(-jnp.expm1(-dt0)),
        "ssd_a_log": jnp.log(jax.random.uniform(ks[17], (N_EVEN, 2, SSD_HEADS), f32, 1.0, 16.0)),
        "ssd_d": gain(ks[18], (N_EVEN, SSD_HEADS)),
        "ssd_norm_g": gain(ks[19], (N_EVEN, SSD_INNER)),
        "cf_dw_w": dense(ks[20], (N_EVEN, CF_KERNEL, CF_CH), CF_KERNEL),
        "cf_dw_b": small(ks[21], (N_EVEN, CF_CH)),
        "cf_ln_g": gain(ks[22], (N_EVEN, CF_CH)),
        "cf_ln_b": small(ks[23], (N_EVEN, CF_CH)),
        "ab_w_out": dense(ks[24], (N_EVEN, AB_OUT, D_MODEL), AB_OUT),
        "hg_w_in": dense(ks[25], (N_ODD, D_MODEL, HG_IN), D_MODEL),
        "hg_lb": small(ks[26], (DEPTH, HG_KEY), 0.1),
        "hg_norm_g": gain(ks[27], (N_ODD, HG_DV)),
        "hg_w_out": dense(ks[28], (N_ODD, HG_VAL, D_MODEL), HG_VAL),
        "final_norm_g": gain(ks[29], (D_MODEL,)),
    }

def first_block(x, c, ctx, c_ctx, mod_w, mod_b, norm_mix_g, norm_ffn_g, router_w, router_b,
              moe_w_gate, moe_w_up, moe_w_down, ab_w_in, ssd_conv_w, ssd_conv_b, ssd_dt_bias,
              ssd_a_log, ssd_d, ssd_norm_g, cf_dw_w, cf_dw_b, cf_ln_g, cf_ln_b, ab_w_out,
              hg_w_in, hg_lb, hg_norm_g, hg_w_out, final_norm_g):
    rows = x.shape[1] // GRID_W
    lb_all = jnp.cumsum(jax.nn.softmax(hg_lb.astype(jnp.float32), axis=0), axis=0)
    lb_all = lb_all - lb_all[0]
    xl, xc = x, ctx
    for l in range(DEPTH):
        last = l == DEPTH - 1
        j = l // 2
        m_l = modulation(c, mod_w[l], mod_b[l])[:, :, None, :]
        m_c = modulation(c_ctx, mod_w[l], mod_b[l])
        hl = rmsnorm(xl, norm_mix_g[l]) * (1.0 + m_l[:, 1]) + m_l[:, 0]
        hc = rmsnorm(xc, norm_mix_g[l]) * (1.0 + m_c[1]) + m_c[0]
        if l % 2 == 0:
            y_c, y_l = even_mixer(hc, hl, ab_w_in[j], ssd_conv_w[j], ssd_conv_b[j], ssd_dt_bias[j],
                                  ssd_a_log[j], ssd_d[j], ssd_norm_g[j], cf_dw_w[j], cf_dw_b[j],
                                  cf_ln_g[j], cf_ln_b[j], ab_w_out[j], rows, not last)
        else:
            y_c, y_l = odd_mixer(hc, hl, hg_w_in[j], lb_all[l], hg_norm_g[j], hg_w_out[j], rows, not last)
        xl = xl + m_l[:, 2] * y_l
        hl = rmsnorm(xl, norm_ffn_g[l]) * (1.0 + m_l[:, 4]) + m_l[:, 3]
        xl = xl + m_l[:, 5] * moe(hl, router_w, router_b, moe_w_gate[l], moe_w_up[l], moe_w_down[l])
        if not last:
            xc = xc + m_c[2] * y_c
            hc = rmsnorm(xc, norm_ffn_g[l]) * (1.0 + m_c[4]) + m_c[3]
            xc = xc + m_c[5] * moe(hc, router_w, router_b, moe_w_gate[l], moe_w_up[l], moe_w_down[l])
    return rmsnorm(xl, final_norm_g)


ROPE_THETA = 10000.0
NORM_EPS = 1e-6
NEG_INF = -1e30
TINY = 1e-30
D_FF = 2816
Q_BLOCK = 128

MLA_HEADS = 8
MLA_NOPE = 64
MLA_ROPE = 32
MLA_V = 64
MLA_Q_LORA = 256
MLA_KV_LORA = 128

GLA_HEADS = 4
GLA_DK = 64
GLA_DV = 128
GLA_GATE_RANK = 16
GLA_GATE_TAU = 16.0
GLA_CHUNK = 64

NSA_HEADS = 16
NSA_KV_GROUPS = 4
NSA_HEAD_DIM = 64
NSA_CMP_LEN = 32
NSA_CMP_STRIDE = 16
NSA_CMP_HIDDEN = 128
NSA_SEL_LEN = 64
NSA_TOP_N = 16
NSA_WINDOW = 512
NSA_Q_BLOCK = 64
NSA_FORCE_SCORE = 1e4

HY_SPLITS = (MLA_Q_LORA, MLA_KV_LORA, MLA_ROPE, GLA_HEADS * GLA_DK, GLA_HEADS * GLA_DK,
             GLA_HEADS * GLA_DV, GLA_GATE_RANK, GLA_HEADS * GLA_DV)
HY_IN = sum(HY_SPLITS)
HY_OUT = MLA_HEADS * MLA_V + GLA_HEADS * GLA_DV
NSA_KV_WIDTH = NSA_KV_GROUPS * NSA_HEAD_DIM
NSA_SPLITS = (NSA_HEADS * NSA_HEAD_DIM,) + (NSA_KV_WIDTH,) * 6 + (NSA_HEADS * 3,)
NSA_IN = sum(NSA_SPLITS)
NSA_OUT = NSA_HEADS * NSA_HEAD_DIM
N_EVEN_2 = (DEPTH + 1) // 2
N_ODD_2 = DEPTH // 2


def split_cols(h, sizes):
    return jnp.split(h, np.cumsum(sizes)[:-1].tolist(), axis=-1)

def rms_norm(x, g):
    xf = x.astype(jnp.float32)
    y = xf * lax.rsqrt(jnp.mean(xf * xf, axis=-1, keepdims=True) + NORM_EPS)
    return (y * g.astype(jnp.float32)).astype(x.dtype)

def rope(x, pos):
    d = x.shape[-1]
    inv_freq = jnp.power(ROPE_THETA, -jnp.arange(d // 2, dtype=jnp.float32) * (2.0 / d))
    ang = pos.astype(jnp.float32)[..., None] * inv_freq
    cos = jnp.cos(ang)[:, :, None, :]
    sin = jnp.sin(ang)[:, :, None, :]
    xf = x.astype(jnp.float32)
    x1, x2 = xf[..., : d // 2], xf[..., d // 2:]
    return jnp.concatenate([x1 * cos - x2 * sin, x2 * cos + x1 * sin], axis=-1).astype(x.dtype)

def masked_softmax(s, mask):
    s = jnp.where(mask, s.astype(jnp.float32), NEG_INF)
    m = jnp.max(s, axis=-1, keepdims=True)
    p = jnp.where(mask, jnp.exp(s - m), 0.0)
    return p / jnp.maximum(jnp.sum(p, axis=-1, keepdims=True), TINY)

def swiglu(x, w_gate, w_up, w_down):
    return (jax.nn.silu(x @ w_gate) * (x @ w_up)) @ w_down

def causal_block_attention(q, k, v, scale):
    B, S, H, Dk = q.shape
    nb = S // Q_BLOCK
    q_blocks = q.reshape(B, nb, Q_BLOCK, H, Dk).transpose(1, 0, 2, 3, 4)
    key_pos = jnp.arange(S)

    def one_block(args):
        i, qb = args
        s = jnp.einsum('bqhd,bkhd->bhqk', qb, k, preferred_element_type=jnp.float32) * scale
        q_pos = i * Q_BLOCK + jnp.arange(Q_BLOCK)
        p = masked_softmax(s, key_pos[None, :] <= q_pos[:, None])
        return jnp.einsum('bhqk,bkhd->bqhd', p.astype(v.dtype), v)

    out = lax.map(one_block, (jnp.arange(nb), q_blocks))
    return out.transpose(1, 0, 2, 3, 4).reshape(B, S, H, v.shape[-1])

def mla_heads(c_q, c_kv, k_r, positions, q_norm, w_uq, kv_norm, w_ukv):
    B, S, _ = c_q.shape
    q = (rms_norm(c_q, q_norm) @ w_uq).reshape(B, S, MLA_HEADS, MLA_NOPE + MLA_ROPE)
    q_nope, q_rot = q[..., :MLA_NOPE], rope(q[..., MLA_NOPE:], positions)
    kv = (rms_norm(c_kv, kv_norm) @ w_ukv).reshape(B, S, MLA_HEADS, MLA_NOPE + MLA_V)
    k_nope, v = kv[..., :MLA_NOPE], kv[..., MLA_NOPE:]
    k_rot = rope(k_r.reshape(B, S, 1, MLA_ROPE), positions)
    q_full = jnp.concatenate([q_nope, q_rot], axis=-1)
    k_full = jnp.concatenate([k_nope, jnp.broadcast_to(k_rot, (B, S, MLA_HEADS, MLA_ROPE))], axis=-1)
    o = causal_block_attention(q_full, k_full, v, (MLA_NOPE + MLA_ROPE) ** -0.5)
    return o.reshape(B, S, MLA_HEADS * MLA_V)

def gla_heads(h_q, h_k, h_v, h_a, h_r, w_a2, b_a, out_norm):
    B, S, _ = h_q.shape
    H, DK, DV, C = GLA_HEADS, GLA_DK, GLA_DV, GLA_CHUNK
    nc = S // C
    f32 = jnp.float32
    q = h_q.reshape(B, nc, C, H, DK).astype(f32) * DK ** -0.5
    k = h_k.reshape(B, nc, C, H, DK).astype(f32)
    v = h_v.reshape(B, nc, C, H, DV).astype(f32)
    log_a = jax.nn.log_sigmoid((h_a @ w_a2 + b_a).astype(f32)) / GLA_GATE_TAU
    b = jnp.cumsum(log_a.reshape(B, nc, C, H, DK), axis=2)
    b_last = b[:, :, -1:]
    k_dec = k * jnp.exp(b_last - b)
    q_inter = q * jnp.exp(b)
    q_intra = q * jnp.exp(b - b_last)
    causal = jnp.tril(jnp.ones((C, C), dtype=bool))
    A = jnp.where(causal, jnp.einsum('bnihd,bnjhd->bnhij', q_intra, k_dec), 0.0)
    o_intra = jnp.einsum('bnhij,bnjhv->bnihv', A, v)
    kv_chunk = jnp.einsum('bnjhd,bnjhv->nbhdv', k_dec, v)
    decay_chunk = jnp.exp(b[:, :, -1]).transpose(1, 0, 2, 3)

    def step(state, inp):
        dec, kv = inp
        return state * dec[..., None] + kv, state

    _, s_prev = lax.scan(step, jnp.zeros((B, H, DK, DV), f32), (decay_chunk, kv_chunk))
    o_inter = jnp.einsum('bnihd,nbhdv->bnihv', q_inter, s_prev)
    o = rms_norm((o_intra + o_inter).reshape(B, S, H, DV), out_norm)
    o = o * jax.nn.silu(h_r.reshape(B, S, H, DV).astype(f32))
    return o.reshape(B, S, H * DV).astype(h_q.dtype)

def mla_gla_mixer(u, positions, w_in, q_norm, w_uq, kv_norm, w_ukv, w_a2, b_a, out_norm, w_out):
    c_q, c_kv, k_r, g_q, g_k, g_v, g_a, g_r = split_cols(u @ w_in, HY_SPLITS)
    o_mla = mla_heads(c_q, c_kv, k_r, positions, q_norm, w_uq, kv_norm, w_ukv)
    o_gla = gla_heads(g_q, g_k, g_v, g_a, g_r, w_a2, b_a, out_norm)
    return jnp.concatenate([o_mla, o_gla.astype(o_mla.dtype)], axis=-1) @ w_out

def nsa_mixer(u, positions, w_in, pos_k, pos_v, ck_w1, ck_w2, cv_w1, cv_w2, w_out):
    B, S, _ = u.shape
    H, G, Dh = NSA_HEADS, NSA_KV_GROUPS, NSA_HEAD_DIM
    Hg = H // G
    dt = u.dtype
    q, k_c, v_c, k_s, v_s, k_w, v_w, g = split_cols(u @ w_in, NSA_SPLITS)
    q = rope(q.reshape(B, S, H, Dh), positions)
    gates = jax.nn.sigmoid(g.reshape(B, S, H, 3))

    n_cmp = (S - NSA_CMP_LEN) // NSA_CMP_STRIDE + 1
    cmp_start = np.arange(n_cmp) * NSA_CMP_STRIDE
    cmp_end = cmp_start + NSA_CMP_LEN - 1
    cmp_idx = cmp_start[:, None] + np.arange(NSA_CMP_LEN)[None, :]

    def compress(t, pos_emb, w1, w2):
        blocks = t.reshape(B, S, G, Dh)[:, cmp_idx] + pos_emb[None, None, :, None, :]
        flat = blocks.transpose(0, 1, 3, 2, 4).reshape(B, n_cmp, G, NSA_CMP_LEN * Dh)
        return jax.nn.silu(flat @ w1) @ w2

    k_cmp = rope(compress(k_c, pos_k, ck_w1, ck_w2), positions[:, cmp_end])
    v_cmp = compress(v_c, pos_v, cv_w1, cv_w2)
    cmp_end_j = jnp.asarray(cmp_end)

    n_blk = S // NSA_SEL_LEN
    n_pad = max(n_blk, NSA_TOP_N)

    def to_blocks(t):
        tb = t.reshape(B, n_blk, NSA_SEL_LEN, G, Dh).transpose(0, 3, 1, 2, 4)
        return jnp.pad(tb, ((0, 0), (0, 0), (0, n_pad - n_blk), (0, 0), (0, 0)))

    k_sel_all = to_blocks(rope(k_s.reshape(B, S, G, Dh), positions))
    v_sel_all = to_blocks(v_s.reshape(B, S, G, Dh))
    blk_start = np.arange(n_pad) * NSA_SEL_LEN
    ov = np.minimum(cmp_start[:, None] + NSA_CMP_LEN, blk_start[None, :] + NSA_SEL_LEN) - np.maximum(cmp_start[:, None], blk_start[None, :])
    overlap = jnp.asarray(np.clip(ov, 0, None) / NSA_CMP_LEN, dtype=jnp.float32)

    pad_w = ((0, 0), (NSA_WINDOW, 0), (0, 0), (0, 0))
    k_win = jnp.pad(rope(k_w.reshape(B, S, G, Dh), positions), pad_w)
    v_win = jnp.pad(v_w.reshape(B, S, G, Dh), pad_w)

    nq = S // NSA_Q_BLOCK
    q_blocks = q.reshape(B, nq, NSA_Q_BLOCK, G, Hg, Dh).transpose(1, 0, 2, 3, 4, 5)
    g_blocks = gates.reshape(B, nq, NSA_Q_BLOCK, G, Hg, 3).transpose(1, 0, 2, 3, 4, 5)
    bi = jnp.arange(B)[:, None, None, None]
    gi = jnp.arange(G)[None, :, None, None]
    scale = Dh ** -0.5
    span = NSA_Q_BLOCK + NSA_WINDOW

    def one_block(args):
        i, qb, gb = args
        t = i * NSA_Q_BLOCK + jnp.arange(NSA_Q_BLOCK)
        s_c = jnp.einsum('bqghd,bngd->bghqn', qb, k_cmp, preferred_element_type=jnp.float32) * scale
        p_c = masked_softmax(s_c, cmp_end_j[None, :] <= t[:, None])
        o_c = jnp.einsum('bghqn,bngd->bqghd', p_c.astype(dt), v_cmp)
        imp = jnp.einsum('bghqn,nm->bgqm', p_c, overlap)
        blk = jnp.arange(n_pad)[None, :]
        cur = (t // NSA_SEL_LEN)[:, None]
        forced = (blk == 0) | (blk == cur) | (blk == cur - 1)
        score = jnp.where(blk <= cur, jnp.where(forced, NSA_FORCE_SCORE, imp), NEG_INF)
        _, sel = lax.top_k(score, NSA_TOP_N)
        k_sel = k_sel_all[bi, gi, sel].reshape(B, G, NSA_Q_BLOCK, NSA_TOP_N * NSA_SEL_LEN, Dh)
        v_sel = v_sel_all[bi, gi, sel].reshape(B, G, NSA_Q_BLOCK, NSA_TOP_N * NSA_SEL_LEN, Dh)
        kpos = (sel[..., None] * NSA_SEL_LEN + jnp.arange(NSA_SEL_LEN)).reshape(B, G, NSA_Q_BLOCK, -1)
        s_s = jnp.einsum('bqghd,bgqmd->bghqm', qb, k_sel, preferred_element_type=jnp.float32) * scale
        p_s = masked_softmax(s_s, (kpos <= t[None, None, :, None])[:, :, None])
        o_s = jnp.einsum('bghqm,bgqmd->bqghd', p_s.astype(dt), v_sel)
        start = i * NSA_Q_BLOCK
        k_wb = lax.dynamic_slice_in_dim(k_win, start, span, axis=1)
        v_wb = lax.dynamic_slice_in_dim(v_win, start, span, axis=1)
        wpos = (start - NSA_WINDOW + jnp.arange(span))[None, :]
        m_w = (wpos <= t[:, None]) & (wpos > t[:, None] - NSA_WINDOW) & (wpos >= 0)
        s_w = jnp.einsum('bqghd,bkgd->bghqk', qb, k_wb, preferred_element_type=jnp.float32) * scale
        p_w = masked_softmax(s_w, m_w)
        o_w = jnp.einsum('bghqk,bkgd->bqghd', p_w.astype(dt), v_wb)
        return gb[..., 0:1] * o_c + gb[..., 1:2] * o_s + gb[..., 2:3] * o_w

    out = lax.map(one_block, (jnp.arange(nq), q_blocks, g_blocks))
    return out.transpose(1, 0, 2, 3, 4, 5).reshape(B, S, NSA_OUT) @ w_out

def second_inputs(seed: int = 0) -> dict:
    key = jax.random.key(seed)
    ks = iter(jax.random.split(key, 40))
    f32 = jnp.float32

    def w(shape, fan_in):
        return jax.random.normal(next(ks), shape, f32) * fan_in ** -0.5

    def gain(shape):
        return 1.0 + 0.02 * jax.random.normal(next(ks), shape, f32)

    def small(shape, s):
        return s * jax.random.normal(next(ks), shape, f32)

    x = jax.random.normal(next(ks), (BATCH, SEQ, D_MODEL), f32)
    offsets = jax.random.randint(next(ks), (BATCH, 1), 0, 1024)
    positions = (offsets + jnp.arange(SEQ)[None, :]).astype(jnp.int32)
    return {
        'x': x,
        'positions': positions,
        'ffn_norm': gain((DEPTH, 2, D_MODEL)),
        'ffn_w_gate': w((DEPTH, 2, D_MODEL, D_FF), D_MODEL),
        'ffn_w_up': w((DEPTH, 2, D_MODEL, D_FF), D_MODEL),
        'ffn_w_down': w((DEPTH, 2, D_FF, D_MODEL), D_FF),
        'mix_norm': gain((DEPTH, D_MODEL)),
        'hy_w_in': w((N_EVEN_2, D_MODEL, HY_IN), D_MODEL),
        'mla_q_norm': gain((N_EVEN_2, MLA_Q_LORA)),
        'mla_w_uq': w((N_EVEN_2, MLA_Q_LORA, MLA_HEADS * (MLA_NOPE + MLA_ROPE)), MLA_Q_LORA),
        'mla_kv_norm': gain((N_EVEN_2, MLA_KV_LORA)),
        'mla_w_ukv': w((N_EVEN_2, MLA_KV_LORA, MLA_HEADS * (MLA_NOPE + MLA_V)), MLA_KV_LORA),
        'gla_w_a2': w((N_EVEN_2, GLA_GATE_RANK, GLA_HEADS * GLA_DK), GLA_GATE_RANK),
        'gla_b_a': small((N_EVEN_2, GLA_HEADS * GLA_DK), 0.1),
        'gla_out_norm': gain((N_EVEN_2, GLA_DV)),
        'hy_w_out': w((N_EVEN_2, HY_OUT, D_MODEL), HY_OUT),
        'nsa_w_in': w((N_ODD_2, D_MODEL, NSA_IN), D_MODEL),
        'nsa_pos_k': small((N_ODD_2, NSA_CMP_LEN, NSA_HEAD_DIM), 0.1),
        'nsa_pos_v': small((N_ODD_2, NSA_CMP_LEN, NSA_HEAD_DIM), 0.1),
        'nsa_ck_w1': w((N_ODD_2, NSA_CMP_LEN * NSA_HEAD_DIM, NSA_CMP_HIDDEN), NSA_CMP_LEN * NSA_HEAD_DIM),
        'nsa_ck_w2': w((N_ODD_2, NSA_CMP_HIDDEN, NSA_HEAD_DIM), NSA_CMP_HIDDEN),
        'nsa_cv_w1': w((N_ODD_2, NSA_CMP_LEN * NSA_HEAD_DIM, NSA_CMP_HIDDEN), NSA_CMP_LEN * NSA_HEAD_DIM),
        'nsa_cv_w2': w((N_ODD_2, NSA_CMP_HIDDEN, NSA_HEAD_DIM), NSA_CMP_HIDDEN),
        'nsa_w_out': w((N_ODD_2, NSA_OUT, D_MODEL), NSA_OUT),
        'final_norm': gain((D_MODEL,)),
    }

def second_block(x, positions, ffn_norm, ffn_w_gate, ffn_w_up, ffn_w_down, mix_norm,
              hy_w_in, mla_q_norm, mla_w_uq, mla_kv_norm, mla_w_ukv, gla_w_a2, gla_b_a,
              gla_out_norm, hy_w_out, nsa_w_in, nsa_pos_k, nsa_pos_v, nsa_ck_w1, nsa_ck_w2,
              nsa_cv_w1, nsa_cv_w2, nsa_w_out, final_norm):
    h = x
    for layer in range(DEPTH):
        j = layer // 2
        h = h + 0.5 * swiglu(rms_norm(h, ffn_norm[layer, 0]), ffn_w_gate[layer, 0], ffn_w_up[layer, 0], ffn_w_down[layer, 0])
        u = rms_norm(h, mix_norm[layer])
        if layer % 2 == 0:
            mixed = mla_gla_mixer(u, positions, hy_w_in[j], mla_q_norm[j], mla_w_uq[j], mla_kv_norm[j],
                                  mla_w_ukv[j], gla_w_a2[j], gla_b_a[j], gla_out_norm[j], hy_w_out[j])
        else:
            mixed = nsa_mixer(u, positions, nsa_w_in[j], nsa_pos_k[j], nsa_pos_v[j], nsa_ck_w1[j],
                              nsa_ck_w2[j], nsa_cv_w1[j], nsa_cv_w2[j], nsa_w_out[j])
        h = h + mixed.astype(h.dtype)
        h = h + 0.5 * swiglu(rms_norm(h, ffn_norm[layer, 1]), ffn_w_gate[layer, 1], ffn_w_up[layer, 1], ffn_w_down[layer, 1])
    return rms_norm(h, final_norm)


def setup_inputs(seed=0):
    out = dict(first_inputs(seed))
    for name, value in second_inputs(seed + 1).items():
        if name != "x":
            out[name + "_2"] = value
    return out


def reference(
    x, c, ctx, c_ctx, mod_w, mod_b, norm_mix_g, norm_ffn_g, router_w, router_b, moe_w_gate,
    moe_w_up, moe_w_down, ab_w_in, ssd_conv_w, ssd_conv_b, ssd_dt_bias, ssd_a_log, ssd_d,
    ssd_norm_g, cf_dw_w, cf_dw_b, cf_ln_g, cf_ln_b, ab_w_out, hg_w_in, hg_lb, hg_norm_g,
    hg_w_out, final_norm_g, positions_2, ffn_norm_2, ffn_w_gate_2, ffn_w_up_2, ffn_w_down_2,
    mix_norm_2, hy_w_in_2, mla_q_norm_2, mla_w_uq_2, mla_kv_norm_2, mla_w_ukv_2, gla_w_a2_2,
    gla_b_a_2, gla_out_norm_2, hy_w_out_2, nsa_w_in_2, nsa_pos_k_2, nsa_pos_v_2, nsa_ck_w1_2,
    nsa_ck_w2_2, nsa_cv_w1_2, nsa_cv_w2_2, nsa_w_out_2, final_norm_2,
):
    x = first_block(
        x, c, ctx, c_ctx, mod_w, mod_b, norm_mix_g, norm_ffn_g, router_w, router_b, moe_w_gate,
        moe_w_up, moe_w_down, ab_w_in, ssd_conv_w, ssd_conv_b, ssd_dt_bias, ssd_a_log, ssd_d,
        ssd_norm_g, cf_dw_w, cf_dw_b, cf_ln_g, cf_ln_b, ab_w_out, hg_w_in, hg_lb, hg_norm_g,
        hg_w_out, final_norm_g,
    )
    return second_block(
        x, positions_2, ffn_norm_2, ffn_w_gate_2, ffn_w_up_2, ffn_w_down_2, mix_norm_2,
        hy_w_in_2, mla_q_norm_2, mla_w_uq_2, mla_kv_norm_2, mla_w_ukv_2, gla_w_a2_2, gla_b_a_2,
        gla_out_norm_2, hy_w_out_2, nsa_w_in_2, nsa_pos_k_2, nsa_pos_v_2, nsa_ck_w1_2,
        nsa_ck_w2_2, nsa_cv_w1_2, nsa_cv_w2_2, nsa_w_out_2, final_norm_2,
    )


_drawn_inputs = setup_inputs


def setup_inputs(seed=0):
    import zlib

    import numpy as np

    out = dict(_drawn_inputs(seed))
    spreads = {}
    factors = {'hg_lb': 4.181,
     'ffn_norm_2': 3.403,
     'mix_norm_2': 3.073,
     'mla_q_norm_2': 8.0,
     'mla_kv_norm_2': 8.0,
     'gla_b_a_2': 3.239,
     'gla_out_norm_2': 7.05,
     'nsa_pos_k_2': 8.0,
     'final_norm_2': 8.039,
     'nsa_pos_v_2': 8.0}
    for name, (base, spread) in spreads.items():
        noise = np.random.default_rng([zlib.crc32(name.encode()), seed]).standard_normal(out[name].shape)
        drawn = base * np.exp(spread * noise) if base else spread * noise
        out[name] = jnp.asarray(drawn.astype(out[name].dtype))
    for name, factor in factors.items():
        out[name] = (out[name] * factor).astype(out[name].dtype)
    return out
```

```python
from contextlib import ExitStack, contextmanager

import numpy as np

import concourse.bass as bass
from concourse import mybir

F32 = mybir.dt.float32
U32 = mybir.dt.uint32
ALU = mybir.AluOpType
ACT = mybir.ActivationFunctionType
AX = mybir.AxisListType

P = 128
D = 1024
KD = D // P
SEQ = 256
TT = 2 * SEQ
NT = TT // P
EPS = 1e-6

VECTORS = [
    ("norm_mix", 16), ("norm_ffn", 16), ("mod_b", 96), ("conv_b", 16), ("conv_w", 80),
    ("d_skip", 8), ("ssd_g", 8), ("cf_w", 248), ("cf_b", 8), ("cf_lng", 8), ("cf_lnb", 8),
    ("hg_lb", 16), ("hg_g", 1), ("final_g", 8), ("ffn_norm2", 32), ("mix_norm2", 16),
    ("q_norm", 2), ("kv_norm", 1), ("gla_g", 1), ("final_g2", 8), ("cond", 16),
    ("pos_k", 32), ("pos_v", 32), ("gla_ba", 4),
]
VCOL, _n = {}, 0
for _name, _w in VECTORS:
    VCOL[_name] = _n
    _n += _w
NV = _n
ROWS = [("router_b", 64), ("dt_bias", 32), ("a_log", 32), ("pos", SEQ)]
CONSTS = [("ident", P), ("ones", P), ("upper", P), ("lower", P), ("up64", P), ("lo64", P),
          ("xup64", P), ("xlo64", P), ("upper_x", P), ("lower_x", P), ("tie", 16), ("half", 2), ("ropef", 2),
          ("swap_mla", P), ("swap_nsa", P), ("rot_rows", 1), ("causal_add", 2 * P), ("cmp_mask", 32), ("cmp_add", 32)]
CCOL, _n = {}, 0
for _name, _w in CONSTS:
    CCOL[_name] = _n
    _n += _w
NCONST = _n


TWO_PI_PARTS = [6.28125]
TWO_PI_PARTS.append(float(np.round((2 * np.pi - 6.28125) * 2 ** 21) / 2 ** 21))
TWO_PI_PARTS.append(float(np.float32(2 * np.pi - sum(TWO_PI_PARTS))))
PI_BELOW = float(np.nextafter(np.float32(np.pi), np.float32(0)))


class Ring:

    def __init__(self, nc, ctx):
        self.buf, self.landed, self.queue, self.sent, self.used, self.free_at = {}, {}, {}, {}, {}, {}
        for a, n in (("A", 4096), ("B", 4096), ("C", 2048), ("D", 2048)):
            self.buf[a] = ctx.enter_context(nc.sbuf_tensor(f"weights_{a}", [P, n], F32))
            self.landed[a] = ctx.enter_context(nc.semaphore(f"weights_{a}_landed"))
            self.queue[a], self.sent[a], self.used[a] = [], 0, 0
        self.chunk_done = ctx.enter_context(nc.semaphore("pe_chunk_done"))
        self.chunks = 0

    def load(self, sp, area, after):
        i = self.sent[area]
        if i < len(self.queue[area]):
            if after is not None:
                sp.wait_ge(self.chunk_done, after)
            sp.dma_start(self.buf[area][:], self.queue[area][i]).then_inc(self.landed[area], 16)
        self.sent[area] += 1

    def arrived(self, pe, area):
        self.used[area] += 1
        pe.wait_ge(self.landed[area], 16 * self.used[area])


@contextmanager
def stage(nc, names):
    handles = {name: nc.alloc_semaphore(name=f"{name}_{nc.next_id()}") for name in names.split()}
    with nc.Block() as block:
        yield block, handles
    nc.clear_and_free_semaphores(list(handles.values()))
    nc.all_engine_barrier()


def chain(eng, sem, base=0):
    n = [0]

    def link(ins):
        n[0] += 1
        ins.then_inc(sem, 1)
        eng.wait_ge(sem, base + n[0])
        return n[0]
    return link


class Program:
    def __init__(self, nc, ctx, d, out):
        self.nc, self.ctx, self.d, self.out = nc, ctx, d, out
        sb = self.sb
        self.ring = Ring(nc, ctx)
        self.X = sb(ctx, "residual", [P, KD, TT])
        self.H = sb(ctx, "normed", [P, KD, TT])
        self.vec = sb(ctx, "vectors", [P, NV])
        self.cst = sb(ctx, "constants", [P, NCONST])
        self.mod = sb(ctx, "modulation", [P, 2 * 6 * KD, 2])
        self.scale_mod = sb(ctx, "norm_scales", [P, 4, KD, 2])
        self.ps = ctx.enter_context(nc.psum_tensor("ps", [P, 8, 512], F32))
        self.eps = sb(ctx, "eps", [P, 1])
        self.spare = sb(ctx, "spare", [P, 3])

    def sb(self, ctx, name, shape, dt=F32):
        return ctx.enter_context(self.nc.sbuf_tensor(f"{name}_{self.nc.next_id()}", shape, dt))

    def v(self, name, i=0, n=1, p=P):
        c = VCOL[name] + i
        return self.vec[0:p, c:c + n]

    def c(self, name, n=P, p=P, off=0):
        c = CCOL[name] + off
        return self.cst[0:p, c:c + n]

    def plan(self):
        q, d = self.ring.queue, self.d
        for i in range(12):
            q["A"].append(d["mod_w"][2 * i])
            q["B"].append(d["mod_w"][2 * i + 1])
        for i in range(5):
            q["A"].append(d["ab_in"][2 * i])
            q["B"].append(d["ab_in"][2 * i + 1])
        for i in range(2):
            q["A"].append(d["ab_out"][2 * i])
            q["B"].append(d["ab_out"][2 * i + 1])

        def moe(layer):
            for e in range(16):
                q["A"].append(d["moe_gate"][16 * layer + e])
                q["B"].append(d["moe_up"][16 * layer + e])
                q["C"].append(d["moe_down"][2 * (16 * layer + e)])
                q["D"].append(d["moe_down"][2 * (16 * layer + e) + 1])

        def ffn(n):
            for j in range(11):
                q["AB"[j % 2]].append(d["ffn_gu"][11 * n + j])
                q["CD"[j % 2]].append(d["ffn_down"][11 * n + j])
        moe(0)
        for i in range(5):
            q["A"].append(d["hg_in"][2 * i])
            q["B"].append(d["hg_in"][2 * i + 1])
        q["A"].append(d["hg_out"][0])
        q["B"].append(d["hg_out"][1])
        moe(1)
        ffn(0)
        for i in range(4):
            q["BA"[i % 2]].append(d["hy_in"][i])
        q["B"].append(d["hy_out"][0])
        q["A"].append(d["hy_out"][1])
        ffn(1)
        ffn(2)
        for i in range(5):
            q["BA"[i % 2]].append(d["nsa_in"][i])
        q["A"].append(d["nsa_out"][0])
        q["B"].append(d["nsa_out"][1])
        ffn(3)

    def load_inputs(self):
        nc, d = self.nc, self.d
        with stage(nc, "loaded memset") as (block, s):
            @block.sync
            def _(sp):
                for area in "ABCD":
                    self.ring.load(sp, area, None)

            @block.scalar
            def _(act):
                act.dma_start(self.vec[:], d["vectors"]).then_inc(s["loaded"], 16)
                act.dma_start(self.cst[:], d["constants"]).then_inc(s["loaded"], 16)
                act.dma_start(self.X[:].rearrange("p k t -> p (k t)"), d["x"]).then_inc(s["loaded"], 16)
                act.wait_ge(s["loaded"], 48)

            @block.vector
            def _(dve):
                nc.vector.memset(self.eps[:], EPS).then_inc(s["memset"], 1)
                dve.wait_ge(s["memset"], 1)

    def modulation(self):
        nc, ring, ps, mod = self.nc, self.ring, self.ps, self.mod
        rounds = 12
        base = ring.chunks
        with ExitStack() as ctx:
            cond = self.sb(ctx, "cond", [P, KD, 2])
            with stage(nc, "silu_done added scaled") as (block, s):
                @block.scalar
                def _(act):
                    nc.scalar.activation(cond[:], self.v("cond", 0, 16).rearrange("p (k c) -> p k c", c=2),
                                         ACT.Silu).then_inc(s["silu_done"], 1)

                @block.sync
                def _(sp):
                    with sp.Fori(0, rounds - 1) as i:
                        sp.wait_ge(ring.chunk_done, i * 8 + base + 4)
                        sp.dma_start(ring.buf["A"][:], self.d["mod_w"][2 * i + 2]).then_inc(ring.landed["A"], 16)
                        sp.wait_ge(ring.chunk_done, i * 8 + base + 8)
                        sp.dma_start(ring.buf["B"][:], self.d["mod_w"][2 * i + 3]).then_inc(ring.landed["B"], 16)
                    ring.sent["A"] += rounds - 1
                    ring.sent["B"] += rounds - 1
                    ring.load(sp, "A", base + 8 * rounds - 4)
                    ring.load(sp, "B", base + 8 * rounds)

                @block.tensor
                def _(pe):
                    pe.wait_ge(s["silu_done"], 1)
                    with pe.Fori(0, rounds) as i:
                        for half, area in enumerate("AB"):
                            pe.wait_ge(ring.landed[area], i * 16 + 16 * (ring.used[area] + 1))
                            for m in range(4):
                                if m == 0:
                                    pe.wait_ge(s["added"], i * 2 + half + 1)
                                for k in range(KD):
                                    last = nc.tensor.matmul(
                                        ps[:, half, 2 * m:2 * m + 2],
                                        ring.buf[area][:, k * 512 + m * P:k * 512 + (m + 1) * P],
                                        cond[:, k, :], start=(k == 0), stop=(k == KD - 1))
                                last.then_inc(ring.chunk_done, 1)
                    ring.used["A"] += rounds
                    ring.used["B"] += rounds

                @block.vector
                def _(dve):
                    self.credit(nc.vector, s["added"])
                    with dve.Fori(0, rounds) as i:
                        for half in range(2):
                            dve.wait_ge(ring.chunk_done, i * 8 + base + 4 * half + 4)
                            bias = self.vec[:, VCOL["mod_b"]:VCOL["mod_b"] + 96].rearrange(
                                "p (i m) -> p i m", m=4)[:, bass.ds(i * 2 + half, 1), :].rearrange("p i m -> p (i m)")
                            out = mod[:].rearrange("p (i m) c -> p i m c", m=4)[:, bass.ds(i * 2 + half, 1), :, :]
                            nc.vector.tensor_tensor(
                                out.rearrange("p i m c -> p (i m) c"), ps[:, half, 0:8].rearrange("p (m c) -> p m c", c=2),
                                bias.unsqueeze(2).to_broadcast([P, 4, 2]), ALU.add).then_inc(s["added"], 1)
                    dve.wait_ge(s["added"], 2 * rounds + 1)
                    m4 = mod[:].rearrange("p (l j k) c -> p l j k c", l=2, j=6)
                    for n in range(4):
                        layer, kind = n // 2, n % 2
                        g = self.v(("norm_mix", "norm_ffn")[kind], 8 * layer, 8)
                        nc.vector.scalar_tensor_tensor(
                            out=self.scale_mod[:, n, :, :], in0=m4[:, layer, 1 + 3 * kind, :, :], scalar=1.0,
                            in1=g.unsqueeze(2).to_broadcast([P, KD, 2]), op0=ALU.add, op1=ALU.mult).then_inc(s["scaled"], 1)
        ring.chunks += 8 * rounds

    def credit(self, engine, sem, column=1):
        if engine is self.nc.scalar:
            self.nc.scalar.activation(self.spare[:, 0:1], self.eps[:], ACT.Copy).then_inc(sem, 1)
        else:
            self.nc.vector.memset(self.spare[:, column:column + 1], 0.0).then_inc(sem, 1)

    def m(self, layer, kind, k, c):
        return self.mod[:, layer * 48 + kind * 8 + k, c:c + 1]

    def rms_norm(self, src, dst, chunks, tokens, scale, shift=None, permuted=False, eps=None):
        nc, ps = self.nc, self.ps
        halves = [(c, slice(c * SEQ, (c + 1) * SEQ)) for c in range(tokens // SEQ)]
        with ExitStack() as ctx:
            sq = self.sb(ctx, "squares", [P, 2, tokens])
            root = self.sb(ctx, "root", [P, tokens])
            rstd = self.sb(ctx, "rstd", [P, tokens])
            with stage(nc, "squared summed rooted inverted scaled shifted") as (block, s):
                @block.scalar
                def _(act):
                    for k in range(chunks):
                        if k >= 2:
                            act.wait_ge(s["summed"], k - 1)
                        nc.scalar.activation(sq[:, k % 2, :], src(k, slice(0, tokens)), ACT.Square).then_inc(s["squared"], 1)
                    act.wait_ge(s["summed"], chunks)
                    nc.scalar.activation(root[:], ps[:, 0, 0:tokens], ACT.Sqrt, bias=self.eps[:, 0:1],
                                         scale=1.0 / (chunks * P)).then_inc(s["rooted"], 1)
                    if shift is not None:
                        for k in range(chunks):
                            act.wait_ge(s["scaled"], (k + 1) * len(halves))
                            for c, t in halves:
                                nc.scalar.activation(dst(k, t), dst(k, t), ACT.Identity,
                                                     bias=shift(k, c)).then_inc(s["shifted"], 1)

                @block.tensor
                def _(pe):
                    for k in range(chunks):
                        pe.wait_ge(s["squared"], k + 1)
                        nc.tensor.matmul(ps[:, 0, 0:tokens], self.c("ones"), sq[:, k % 2, :],
                                         start=(k == 0), stop=(k == chunks - 1)).then_inc(s["summed"], 1)

                @block.vector
                def _(dve):
                    dve.wait_ge(s["rooted"], 1)
                    nc.vector.reciprocal(rstd[:], root[:]).then_inc(s["inverted"], 1)
                    dve.wait_ge(s["inverted"], 1)
                    for k in range(chunks):
                        for c, t in halves:
                            a, r, o = src(k, t), rstd[:, t], dst(k, t)
                            if permuted and c == 0:
                                a = a.rearrange("p (r w) -> p w r", w=64)
                                r = r.rearrange("p (r w) -> p w r", w=64)
                                o = o.rearrange("p (w r) -> p w r", w=64)
                            nc.vector.scalar_tensor_tensor(out=o, in0=a, scalar=scale(k, c), in1=r,
                                                           op0=ALU.mult, op1=ALU.mult).then_inc(s["scaled"], 1)

    def x_chunk(self, k, t):
        return self.X[:, k, t]

    def h_chunk(self, k, t):
        return self.H[:, k, t]

    def panel_products(self, pe, s_free, area, kchunks, cols, rhs, n0, banks, tokens, free):
        nc, ring = self.nc, self.ring
        ring.arrived(pe, area)
        for m in range(cols // P):
            free(n0 + m)
            for k in range(kchunks):
                last = nc.tensor.matmul(
                    self.ps[:, banks[(n0 + m) % len(banks)], 0:tokens],
                    ring.buf[area][:, k * cols + m * P:k * cols + (m + 1) * P], rhs(k),
                    start=(k == 0), stop=(k == kchunks - 1))
            last.then_inc(ring.chunk_done, 1)

    def out_projection(self, panels, kchunks, rhs, layer, tokens, permuted=False, scale=None):
        nc, ring, ps, X = self.nc, self.ring, self.ps, self.X
        cols = 4096 // kchunks
        per = cols // P
        base = ring.chunks
        halves = [(c, slice(c * SEQ, (c + 1) * SEQ)) for c in range(tokens // SEQ)]
        nh = len(halves)
        with stage(nc, "added") as (block, s):
            @block.tensor
            def _(pe):
                for i, area in enumerate(panels):
                    self.panel_products(pe, None, area, kchunks, cols, rhs, per * i, range(4), tokens,
                                        lambda n: pe.wait_ge(s["added"], nh * (n - 3)) if n >= 4 else None)

            @block.sync
            def _(sp):
                for i, area in enumerate(panels):
                    ring.load(sp, area, base + per * (i + 1))

            @block.vector
            def _(dve):
                for m in range(KD):
                    dve.wait_ge(ring.chunk_done, base + m + 1)
                    for c, t in halves:
                        x, y = X[:, m, t], ps[:, m % 4, t]
                        if permuted:
                            x = x.rearrange("p (r w) -> p w r", w=64)
                            y = y.rearrange("p (w r) -> p w r", w=64)
                        sc = self.m(layer, 2, m, c) if scale is None else scale
                        nc.vector.scalar_tensor_tensor(out=x, in0=y, scalar=sc, in1=x,
                                                       op0=ALU.mult, op1=ALU.add).then_inc(s["added"], 1)
        ring.chunks += KD

    def even_in(self, Z, XBC, U, dt_tok):
        nc, ring, ps, H = self.nc, self.ring, self.ps, self.H
        base = ring.chunks
        areas = "AB" * 5
        with ExitStack() as ctx:
            sig = self.sb(ctx, "gate_sigmoid", [P, 2, TT])
            wdt = self.sb(ctx, "w_dt", [P, KD, 32])
            with stage(nc, "wdt_in act_read dve_read zeroed dt_sum sig_done u_done") as (block, s):
                def bank_counts(n):
                    a = v = 0
                    for j in range(n):
                        pair, what = divmod(j - 24, 4)
                        if j < 8:
                            a = j + 1
                        elif j < 24:
                            v = j - 7
                        elif what < 2:
                            v = 16 + 2 * pair + what + 1
                        else:
                            a = 8 + 2 * pair + what - 1
                    return a, v

                @block.tensor
                def _(pe):
                    def free(n):
                        if n >= 6:
                            a, v = bank_counts(n - 5)
                            pe.wait_ge(s["act_read"], a) if a else None
                            pe.wait_ge(s["dve_read"], v) if v else None
                    for i, area in enumerate(areas):
                        self.panel_products(pe, None, area, KD, 512, lambda k: H[:, k, :], 4 * i, range(6), TT, free)
                    pe.wait_ge(s["wdt_in"], 16)
                    for t in range(NT):
                        for k in range(KD):
                            last = nc.tensor.matmul(ps[:, 6, 32 * t:32 * t + 32], H[:, k, t * P:(t + 1) * P],
                                                    wdt[:, k, :], start=(k == 0), stop=(k == KD - 1))
                    last.then_inc(s["dt_sum"], 1)

                @block.sync
                def _(sp):
                    sp.dma_start(wdt[:].rearrange("p k n -> p (k n)"), self.d["w_dt"]).then_inc(s["wdt_in"], 16)
                    for i, area in enumerate(areas):
                        ring.load(sp, area, base + 4 * (i + 1))

                @block.scalar
                def _(act):
                    for n in range(8):
                        act.wait_ge(ring.chunk_done, base + n + 1)
                        nc.scalar.activation(Z[:, n, :], ps[:, n % 6, :], ACT.Silu).then_inc(s["act_read"], 1)
                    g = 0
                    for n in range(24, 40):
                        if (n - 24) % 4 >= 2:
                            act.wait_ge(ring.chunk_done, base + n + 1)
                            if g >= 2:
                                act.wait_ge(s["dve_read"], 16 + g - 1)
                            nc.scalar.activation(sig[:, g % 2, :], ps[:, n % 6, :], ACT.Sigmoid).then_inc(s["act_read"], 1)
                            g += 1

                @block.gpsimd
                def _(pool):
                    nc.gpsimd.memset(XBC[:], 0.0).then_inc(s["zeroed"], 1)
                    nc.gpsimd.memset(U[:], 0.0).then_inc(s["zeroed"], 1)

                @block.vector
                def _(dve):
                    dve.wait_ge(s["zeroed"], 2)
                    for n in range(8, 24):
                        dve.wait_ge(ring.chunk_done, base + n + 1)
                        nc.vector.tensor_copy(XBC[:, n - 8, :, 2:2 + SEQ],
                                              ps[:, n % 6, :].rearrange("p (s t) -> p s t", s=2)).then_inc(s["dve_read"], 1)
                    g = 0
                    for n in range(24, 40):
                        if (n - 24) % 4 >= 2:
                            dve.wait_ge(s["act_read"], 8 + g + 1)
                            vps = ps[:, (n - 2) % 6, :]
                            ulat = U[:, g, 0:376].rearrange("p (r w) -> p r w", w=94)[:, :, 15:79]
                            nc.vector.tensor_tensor(ulat, vps[:, 0:SEQ].rearrange("p (r w) -> p r w", w=64),
                                                    sig[:, g % 2, 0:SEQ].rearrange("p (r w) -> p r w", w=64),
                                                    ALU.mult).then_inc(s["u_done"], 1)
                            nc.vector.tensor_tensor(U[:, g, 391:391 + SEQ], vps[:, SEQ:TT], sig[:, g % 2, SEQ:TT],
                                                    ALU.mult).then_inc(s["dve_read"], 1)
                            g += 1
                    dve.wait_ge(s["dt_sum"], 1)
                    nc.vector.tensor_copy(dt_tok[:].rearrange("p t n -> p (t n)"), ps[:, 6, 0:128]).then_inc(s["u_done"], 1)
        ring.chunks += 40

    def convolutions(self, XBC, U, dt_tok, LA):
        nc = self.nc
        with ExitStack() as ctx:
            acc = self.sb(ctx, "conv_acc", [P, 2, TT])
            uacc = self.sb(ctx, "cf_acc", [P, 2, TT])
            rows = self.sb(ctx, "ssd_rows", [P, 64])
            aneg = self.sb(ctx, "a_neg", [P, 32])
            raw = self.sb(ctx, "dt_raw", [P, NT, 32])
            mag = self.sb(ctx, "dt_mag", [P, NT, 32])
            with stage(nc, "tap small conv_done xbc_out rows_in u_conv u_out pool_tap prep act_prep") as (block, s):
                @block.sync
                def _(sp):
                    sp.dma_start(rows[:], self.d["ssd_rows"].partition_broadcast(P)).then_inc(s["rows_in"], 16)

                def xsrc(c, tap):
                    return XBC[:, c, :, tap:tap + SEQ]

                sent = [0]

                def taps(dve, jobs, k):
                    for j in range(k):
                        for out, src, w in jobs:
                            if j == 0:
                                ins = nc.vector.tensor_scalar(out, src(j), w(j), None, ALU.mult)
                            else:
                                dve.wait_ge(s["tap"], sent[0] - len(jobs) + 1)
                                ins = nc.vector.scalar_tensor_tensor(out=out, in0=src(j), scalar=w(j), in1=out,
                                                                     op0=ALU.mult, op1=ALU.add)
                            ins.then_inc(s["tap"], 1)
                            sent[0] += 1

                @block.vector
                def _(dve):
                    link = chain(dve, s["small"])
                    dve.wait_ge(s["rows_in"], 16)
                    link(nc.vector.tensor_tensor(raw[:], dt_tok[:], rows[:, 0:32].unsqueeze(1).to_broadcast([P, NT, 32]), ALU.add))
                    link(nc.vector.tensor_scalar(mag[:], raw[:], 0.0, None, ALU.max))
                    nc.vector.scalar_tensor_tensor(out=raw[:], in0=mag[:], scalar=-2.0, in1=raw[:],
                                                   op0=ALU.mult, op1=ALU.add).then_inc(s["prep"], 1)
                    dve.wait_ge(s["act_prep"], 3)
                    nc.vector.tensor_tensor(dt_tok[:], mag[:], raw[:], ALU.add).then_inc(s["prep"], 1)
                    dve.wait_ge(s["prep"], 2)
                    link(nc.vector.scalar_tensor_tensor(
                        out=LA[:], in0=dt_tok[:], scalar=-1.0, in1=aneg[:].unsqueeze(1).to_broadcast([P, NT, 32]),
                        op0=ALU.mult, op1=ALU.mult))
                    for c in range(0, 16, 2):
                        if c >= 2:
                            dve.wait_ge(s["xbc_out"], c)
                        accs = [acc[:, i, :].rearrange("p (s t) -> p s t", s=2) for i in range(2)]
                        taps(dve, [(accs[i], lambda j, i=i: xsrc(c + i, j), lambda j, i=i: self.v("conv_w", 16 * j + c + i))
                                   for i in range(2)], 5)
                        dve.wait_ge(s["tap"], sent[0])
                        for i in range(2):
                            nc.vector.tensor_scalar(accs[i], accs[i], self.v("conv_b", c + i), None, ALU.add).then_inc(s["conv_done"], 1)
                    for c in range(8):
                        if c >= 2:
                            dve.wait_ge(s["u_out"], c - 1)
                        w = lambda j: self.v("cf_w", 8 * j + c)
                        taps(dve, [(uacc[:, c % 2, 0:SEQ].rearrange("p (r w) -> p r w", w=64),
                                    lambda j: U[:, c, 0:376].rearrange("p (r w) -> p r w", w=94)[:, :, j:j + 64], w),
                                   (uacc[:, c % 2, SEQ:TT], lambda j: U[:, c, 376 + j:376 + j + SEQ], w)], 31)
                        dve.wait_ge(s["tap"], sent[0])
                        nc.vector.tensor_scalar(uacc[:, c % 2, :], uacc[:, c % 2, :], self.v("cf_b", c), None,
                                                ALU.add).then_inc(s["u_conv"], 1)

                @block.scalar
                def _(act):
                    act.wait_ge(s["rows_in"], 16)
                    nc.scalar.activation(aneg[:], rows[:, 32:64], ACT.Exp).then_inc(s["act_prep"], 1)
                    act.wait_ge(s["prep"], 1)
                    nc.scalar.activation(raw[:], raw[:], ACT.Exp).then_inc(s["act_prep"], 1)
                    act.wait_ge(s["act_prep"], 2)
                    nc.scalar.activation(raw[:], raw[:], ACT.Ln, bias=1.0).then_inc(s["act_prep"], 1)
                    for c in range(16):
                        act.wait_ge(s["conv_done"], c + 1)
                        nc.scalar.activation(XBC[:, c, :, 2:2 + SEQ], acc[:, c % 2, :].rearrange("p (s t) -> p s t", s=2),
                                             ACT.Silu).then_inc(s["xbc_out"], 1)
                    for c in range(8):
                        act.wait_ge(s["u_conv"], c + 1)
                        nc.scalar.activation(self.H[:, c, :], uacc[:, c % 2, :], ACT.Copy).then_inc(s["u_out"], 1)

    def layer_norm_silu(self):
        nc, ps, H = self.nc, self.ps, self.H
        with ExitStack() as ctx:
            sq = self.sb(ctx, "ln_squares", [P, 2, TT])
            root = self.sb(ctx, "ln_root", [P, TT])
            mean = self.sb(ctx, "ln_mean", [P, TT])
            with stage(nc, "summed mean_done centred squared varied rooted inverted scaled done") as (block, s):
                @block.tensor
                def _(pe):
                    for k in range(KD):
                        last = nc.tensor.matmul(ps[:, 0, :], self.c("ones"), H[:, k, :], start=(k == 0), stop=(k == KD - 1))
                    last.then_inc(s["summed"], 1)
                    for k in range(KD):
                        pe.wait_ge(s["squared"], k + 1)
                        nc.tensor.matmul(ps[:, 1, :], self.c("ones"), sq[:, k % 2, :], start=(k == 0),
                                         stop=(k == KD - 1)).then_inc(s["varied"], 1)

                @block.vector
                def _(dve):
                    dve.wait_ge(s["summed"], 1)
                    nc.vector.tensor_scalar(mean[:], ps[:, 0, :], 1.0 / D, None, ALU.mult).then_inc(s["mean_done"], 1)
                    dve.wait_ge(s["mean_done"], 1)
                    for k in range(KD):
                        nc.vector.tensor_tensor(H[:, k, :], H[:, k, :], mean[:], ALU.subtract).then_inc(s["centred"], 1)
                    dve.wait_ge(s["rooted"], 1)
                    nc.vector.reciprocal(root[:], root[:]).then_inc(s["inverted"], 1)
                    dve.wait_ge(s["inverted"], 1)
                    dve.wait_ge(s["centred"], KD)
                    for k in range(KD):
                        nc.vector.scalar_tensor_tensor(out=H[:, k, :], in0=H[:, k, :], scalar=self.v("cf_lng", k),
                                                       in1=root[:], op0=ALU.mult, op1=ALU.mult).then_inc(s["scaled"], 1)

                @block.scalar
                def _(act):
                    for k in range(KD):
                        act.wait_ge(s["centred"], k + 1)
                        if k >= 2:
                            act.wait_ge(s["varied"], k - 1)
                        nc.scalar.activation(sq[:, k % 2, :], H[:, k, :], ACT.Square).then_inc(s["squared"], 1)
                    act.wait_ge(s["varied"], KD)
                    nc.scalar.activation(root[:], ps[:, 1, :], ACT.Sqrt, bias=self.eps[:, 0:1],
                                         scale=1.0 / D).then_inc(s["rooted"], 1)
                    for k in range(KD):
                        act.wait_ge(s["scaled"], k + 1)
                        nc.scalar.activation(H[:, k, :], H[:, k, :], ACT.Silu, bias=self.v("cf_lnb", k)).then_inc(s["done"], 1)

    def ssd(self, Z, XBC, dt_tok, LA):
        nc, ps = self.nc, self.ps
        H16 = 16

        def xbc(c, tile, p0=0, p1=P):
            return XBC[p0:p1, c, tile // 2, 2 + (tile % 2) * P:2 + (tile % 2) * P + P]
        orders = [[2, 3, 0, 1], [3, 2, 1, 0]]
        steps = [(d, t) for d in range(2) for t in orders[d]]
        with ExitStack() as ctx:
            tok = self.sb(ctx, "xb_tokens", [P, NT, 12, P])
            acum = self.sb(ctx, "acum", [P, NT, 32])
            eend = self.sb(ctx, "exp_end", [P, NT, 32])
            wend = self.sb(ctx, "w_end", [P, NT, 32])
            Y = self.sb(ctx, "y", [P, KD, TT])
            with stage(nc, "transposed copied act_copied sums acum_done diff_done exp_done w_done yinit") as (block, s):
                @block.tensor
                def _(pe):
                    for i in range(12):
                        if i >= 4:
                            pe.wait_ge(s["copied"] if i % 2 == 0 else s["act_copied"], (i - 4) // 2 + 1)
                        for t in range(NT):
                            last = nc.tensor.transpose(ps[:, i % 4, t * P:(t + 1) * P], xbc(i, t), self.c("ident"))
                        last.then_inc(s["transposed"], 1)
                    for t in range(NT):
                        nc.tensor.matmul(ps[:, 4, 32 * t:32 * t + 16], self.c("upper"), LA[:, t, 0:16], start=True, stop=True)
                        nc.tensor.matmul(ps[:, 4, 32 * t + 16:32 * t + 32], self.c("lower"), LA[:, t, 16:32], start=True, stop=True)
                    for t in range(NT):
                        last = nc.tensor.matmul(ps[:, 5, 32 * t:32 * t + 32], self.c("ones"), LA[:, t, :], start=True, stop=True)
                    last.then_inc(s["sums"], 1)

                @block.vector
                def _(dve):
                    for i in range(0, 12, 2):
                        dve.wait_ge(s["transposed"], i + 1)
                        nc.vector.tensor_copy(tok[:, :, i, :], ps[:, i % 4, :].rearrange("p (t c) -> p t c", t=NT)).then_inc(s["copied"], 1)
                    dve.wait_ge(s["sums"], 1)
                    nc.vector.tensor_copy(acum[:].rearrange("p t n -> p (t n)"), ps[:, 4, 0:128]).then_inc(s["acum_done"], 1)
                    dve.wait_ge(s["acum_done"], 1)
                    dve.wait_ge(s["exp_done"], 1)
                    nc.vector.tensor_tensor(wend[:].rearrange("p t n -> p (t n)"), ps[:, 5, 0:128],
                                            acum[:].rearrange("p t n -> p (t n)"), ALU.subtract).then_inc(s["diff_done"], 1)
                    dve.wait_ge(s["exp_done"], 2)
                    nc.vector.tensor_tensor(wend[:], wend[:], dt_tok[:], ALU.mult).then_inc(s["w_done"], 1)
                    for k in range(KD):
                        nc.vector.tensor_scalar(Y[:, k, :].rearrange("p (s t) -> p s t", s=2), XBC[:, k, :, 2:2 + SEQ],
                                                self.v("d_skip", k), None, ALU.mult).then_inc(s["yinit"], 1)

                @block.scalar
                def _(act):
                    for i in range(1, 12, 2):
                        act.wait_ge(s["transposed"], i + 1)
                        nc.scalar.activation(tok[:, :, i, :], ps[:, i % 4, :].rearrange("p (t c) -> p t c", t=NT),
                                             ACT.Copy).then_inc(s["act_copied"], 1)
                    act.wait_ge(s["sums"], 1)
                    nc.scalar.activation(eend[:].rearrange("p t n -> p (t n)"), ps[:, 5, 0:128], ACT.Exp).then_inc(s["exp_done"], 1)
                    act.wait_ge(s["diff_done"], 1)
                    nc.scalar.activation(wend[:], wend[:], ACT.Exp).then_inc(s["exp_done"], 1)

            S = self.sb(ctx, "state", [P, 1024])
            xdt = self.sb(ctx, "x_dt", [P, 1024])
            xw = self.sb(ctx, "x_w", [P, 1024])
            Gm = self.sb(ctx, "cb_masked", [P, 512])
            E = self.sb(ctx, "decay", [P, 2, 512])
            EA = self.sb(ctx, "exp_acum", [P, 2, 512])
            with stage(nc, "cb_done gm_done xdt_done xw_done bcast_done diff_done relu_done exp_done ea_done "
                           "m_done cp_done y_sum y_added s_sum s_scaled s_done cleared") as (block, s):
                units = [(i, g) for i in range(len(steps)) for g in range(4)]

                def banks(u):
                    return 0 + u % 2, 2 + u % 2, 4 + u % 2

                @block.tensor
                def _(pe):
                    def cb(i):
                        d, t = steps[i]
                        if i >= 1:
                            pe.wait_ge(s["gm_done"], i)
                        for g in range(4):
                            last = nc.tensor.matmul(ps[:, 6, g * P:(g + 1) * P], xbc(8 + g, t), xbc(12 + g, t), start=True, stop=True)
                        last.then_inc(s["cb_done"], 1)

                    def bcast(u):
                        i, g = units[u]
                        d, t = steps[i]
                        b = banks(u)[0]
                        if u >= 2:
                            pe.wait_ge(s["diff_done"], u - 1)
                            pe.wait_ge(s["ea_done"], u - 1)
                        for h in range(4):
                            col = 16 * d + 4 * g + h
                            last = nc.tensor.matmul(ps[:, b, h * P:(h + 1) * P], LA[:, t, col:col + 1].to_broadcast([P, P]),
                                                    self.c(("upper", "lower")[d]), start=True, stop=True)
                        last.then_inc(s["bcast_done"], 1)

                    def outputs(u):
                        i, g = units[u]
                        d, t = steps[i]
                        _, yb, sb_ = banks(u)
                        first = i % 4 == 0
                        if u >= 2:
                            pe.wait_ge(s["y_added"], u - 1)
                        pe.wait_ge(s["m_done"], u + 1)
                        pe.wait_ge(s["xdt_done"], i + 1)
                        if not first:
                            pe.wait_ge(s["cp_done"], u + 1)
                            pe.wait_ge(s["s_done"], 4 * (i - 1) + g + 1)
                        for h in range(4):
                            lo = 64 * (h % 2)
                            o = ps[lo:lo + 64, yb, (h // 2) * P:(h // 2 + 1) * P]
                            hc = (4 * g + h) * 64
                            last = nc.tensor.matmul(o, xdt[:, hc:hc + 64], E[:, u % 2, h * P:(h + 1) * P], start=True, stop=first)
                            if not first:
                                last = nc.tensor.matmul(o, S[:, hc:hc + 64], EA[:, u % 2, h * P:(h + 1) * P], start=False, stop=True)
                        last.then_inc(s["y_sum"], 1)
                        if u >= 2:
                            pe.wait_ge(s["s_done"], u - 1)
                        pe.wait_ge(s["xw_done"], i + 1)
                        nc.tensor.matmul(ps[:, sb_, 0:256], tok[:, t, 8 + g, :], xw[:, g * 256:(g + 1) * 256],
                                         start=True, stop=True).then_inc(s["s_sum"], 1)
                    cb(0)
                    bcast(0)
                    for u in range(len(units)):
                        if u + 1 < len(units):
                            if units[u + 1][1] == 0:
                                cb(units[u + 1][0])
                            bcast(u + 1)
                        outputs(u)

                @block.vector
                def _(dve):
                    def prepare(i):
                        d, t = steps[i]
                        dve.wait_ge(s["cb_done"], i + 1)
                        if i >= 1:
                            dve.wait_ge(s["m_done"], 4 * i)
                        nc.vector.tensor_tensor(Gm[:].rearrange("p (g t) -> p g t", g=4), ps[:, 6, :].rearrange("p (g t) -> p g t", g=4),
                                                self.c(("upper", "lower")[d]).unsqueeze(1).to_broadcast([P, 4, P]),
                                                ALU.mult).then_inc(s["gm_done"], 1)
                        if i >= 1:
                            dve.wait_ge(s["y_sum"], 4 * i)
                        x = tok[:, t, 0:8, :].rearrange("p c (h q) -> p (c h) q", h=2)
                        nc.vector.tensor_tensor(xdt[:].rearrange("p (h q) -> p h q", q=64), x,
                                                dt_tok[:, t, 16 * d:16 * d + 16].unsqueeze(2).to_broadcast([P, 16, 64]),
                                                ALU.mult).then_inc(s["xdt_done"], 1)

                    def state(u):
                        i, g = units[u]
                        d, t = steps[i]
                        dve.wait_ge(s["s_sum"], u + 1)
                        Sg = S[:, g * 256:(g + 1) * 256]
                        if i % 4 == 0:
                            nc.vector.tensor_copy(Sg, ps[:, banks(u)[2], 0:256]).then_inc(s["s_done"], 1)
                            return
                        e = eend[:, t, 16 * d + 4 * g:16 * d + 4 * g + 4].unsqueeze(2).to_broadcast([P, 4, 64])
                        nc.vector.tensor_tensor(Sg.rearrange("p (h q) -> p h q", q=64), Sg.rearrange("p (h q) -> p h q", q=64),
                                                e, ALU.mult).then_inc(s["s_scaled"], 1)
                        n_scaled[0] += 1
                        dve.wait_ge(s["s_scaled"], n_scaled[0])
                        nc.vector.tensor_tensor(Sg, Sg, ps[:, banks(u)[2], 0:256], ALU.add).then_inc(s["s_done"], 1)
                    n_scaled = [0]

                    def diff(u):
                        i, g = units[u]
                        d, t = steps[i]
                        dve.wait_ge(s["ea_done"], u + 1)
                        if u >= 2:
                            dve.wait_ge(s["y_sum"], u - 1)
                        a = acum[:, t, 16 * d + 4 * g:16 * d + 4 * g + 4].unsqueeze(2).to_broadcast([P, 4, P])
                        nc.vector.tensor_tensor(E[:, u % 2, :].rearrange("p (h t) -> p h t", h=4), a,
                                                ps[:, banks(u)[0], :].rearrange("p (h t) -> p h t", h=4),
                                                ALU.subtract).then_inc(s["diff_done"], 1)

                    def weight(u):
                        i, g = units[u]
                        dve.wait_ge(s["exp_done"], u + 1)
                        dve.wait_ge(s["gm_done"], i + 1)
                        nc.vector.tensor_tensor(E[:, u % 2, :].rearrange("p (h t) -> p h t", h=4),
                                                E[:, u % 2, :].rearrange("p (h t) -> p h t", h=4),
                                                Gm[:, g * P:(g + 1) * P].unsqueeze(1).to_broadcast([P, 4, P]),
                                                ALU.mult).then_inc(s["m_done"], 1)

                    def add_y(u):
                        i, g = units[u]
                        d, t = steps[i]
                        dve.wait_ge(s["y_sum"], u + 1)
                        y = Y[:, 2 * g:2 * g + 2, t * P:(t + 1) * P]
                        nc.vector.tensor_tensor(y, y, ps[:, banks(u)[1], 0:256].rearrange("p (c t) -> p c t", c=2),
                                                ALU.add).then_inc(s["y_added"], 1)
                    diff(0)
                    prepare(0)
                    for u in range(len(units)):
                        weight(u)
                        if u + 1 < len(units):
                            diff(u + 1)
                        add_y(u)
                        state(u)
                        if u + 1 < len(units) and units[u + 1][1] == 0:
                            prepare(units[u + 1][0])

                @block.scalar
                def _(act):
                    for u in range(len(units)):
                        b = banks(u)[0]
                        act.wait_ge(s["bcast_done"], u + 1)
                        if u >= 2:
                            act.wait_ge(s["cp_done"], u - 1)
                            act.wait_ge(s["y_sum"], u - 1)
                        nc.scalar.activation(EA[:, u % 2, :], ps[:, b, :], ACT.Exp).then_inc(s["ea_done"], 1)
                        act.wait_ge(s["diff_done"], u + 1)
                        nc.scalar.activation(E[:, u % 2, :], E[:, u % 2, :], ACT.Relu).then_inc(s["relu_done"], 1)
                        act.wait_ge(s["relu_done"], u + 1)
                        nc.scalar.activation(E[:, u % 2, :], E[:, u % 2, :], ACT.Exp, scale=-1.0).then_inc(s["exp_done"], 1)

                @block.gpsimd
                def _(pool):
                    for u, (i, g) in enumerate(units):
                        d, t = steps[i]
                        if g == 0:
                            if i >= 1:
                                pool.wait_ge(s["s_sum"], 4 * i)
                            x = tok[:, t, 0:8, :].rearrange("p c (h q) -> p (c h) q", h=2)
                            nc.gpsimd.tensor_tensor(xw[:].rearrange("p (h q) -> p h q", q=64), x,
                                                    wend[:, t, 16 * d:16 * d + 16].unsqueeze(2).to_broadcast([P, 16, 64]),
                                                    ALU.mult).then_inc(s["xw_done"], 1)
                        pool.wait_ge(s["ea_done"], u + 1)
                        nc.gpsimd.tensor_tensor(EA[:, u % 2, :].rearrange("p (h t) -> p h t", h=4),
                                                EA[:, u % 2, :].rearrange("p (h t) -> p h t", h=4),
                                                xbc(12 + g, t).unsqueeze(1).to_broadcast([P, 4, P]),
                                                ALU.mult).then_inc(s["cp_done"], 1)

            with stage(nc, "gated") as (block, s):
                @block.vector
                def _(dve):
                    for k in range(KD):
                        nc.vector.tensor_tensor(Z[:, k, :], Z[:, k, :], Y[:, k, :], ALU.mult).then_inc(s["gated"], 1)

    def even_mixer(self):
        nc = self.nc
        with ExitStack() as ctx:
            Z = self.sb(ctx, "z", [P, KD, TT])
            XBC = self.sb(ctx, "xbc", [P, 16, 2, SEQ + 4])
            dt_tok = self.sb(ctx, "dt", [P, NT, 32])
            LA = self.sb(ctx, "log_decay", [P, NT, 32])
            with ExitStack() as inner:
                U = self.sb(inner, "u", [P, KD, 662])
                self.even_in(Z, XBC, U, dt_tok)
                self.convolutions(XBC, U, dt_tok, LA)
            self.layer_norm_silu()
            self.ssd(Z, XBC, dt_tok, LA)
            z = lambda k, t: Z[:, k, t]
            self.rms_norm(z, z, KD, TT, lambda k, c: self.v("ssd_g", k))
            self.out_projection("ABAB", 16, lambda k: Z[:, k, :] if k < 8 else self.H[:, k - 8, :], 0, TT)

    def route(self, gates, tokens):
        nc, ps, H = self.nc, self.ps, self.H
        nt = tokens // P
        G = 4 * nt
        with ExitStack() as ctx:
            rw = self.sb(ctx, "router_w", [P, KD, 16])
            rb = self.sb(ctx, "router_b", [P, 16])
            sc = self.sb(ctx, "scores", [P, nt, 16])
            sel = self.sb(ctx, "sel", [P, nt, 16])
            gt = self.sb(ctx, "greater", [P, G, 4, 4])
            eq = self.sb(ctx, "equal", [P, G, 4, 4])
            rank = self.sb(ctx, "rank", [P, G, 4])
            gs = self.sb(ctx, "group_score", [P, nt, 4])
            grank = self.sb(ctx, "group_rank", [P, nt, 4])
            tot = self.sb(ctx, "weight_sum", [P, nt])
            comb = self.sb(ctx, "combine", [P, nt, 16])
            combT = self.sb(ctx, "combine_t", [16, tokens])
            with stage(nc, "w_in logits sig_done link comb_done transposed t_copied bcast act_copied dve_copied") as (block, s):
                @block.sync
                def _(sp):
                    sp.dma_start(rw[:].rearrange("p k n -> p (k n)"), self.d["router_w"]).then_inc(s["w_in"], 16)
                    sp.dma_start(rb[:], self.d["router_b"].partition_broadcast(P)).then_inc(s["w_in"], 16)

                @block.tensor
                def _(pe):
                    pe.wait_ge(s["w_in"], 32)
                    for t in range(nt):
                        for k in range(KD):
                            last = nc.tensor.matmul(ps[:, 0, 16 * t:16 * t + 16], H[:, k, t * P:(t + 1) * P], rw[:, k, :],
                                                    start=(k == 0), stop=(k == KD - 1))
                    last.then_inc(s["logits"], 1)
                    pe.wait_ge(s["comb_done"], 1)
                    for t in range(nt):
                        last = nc.tensor.transpose(ps[0:16, 1, t * P:(t + 1) * P], comb[:, t, :], self.c("ident"))
                    last.then_inc(s["transposed"], 1)
                    pe.wait_ge(s["t_copied"], 1)
                    for e in range(16):
                        if e >= 4:
                            pe.wait_ge(s["act_copied"] if e % 2 else s["dve_copied"], (e - 4) // 2 + 1)
                        nc.tensor.matmul(ps[:, 2 + e % 4, 0:tokens], self.cst[0:16, CCOL["ident"] + e:CCOL["ident"] + e + 1].to_broadcast([16, P]),
                                         combT[:], start=True, stop=True).then_inc(s["bcast"], 1)

                @block.scalar
                def _(act):
                    act.wait_ge(s["logits"], 1)
                    nc.scalar.activation(sc[:].rearrange("p t n -> p (t n)"), ps[:, 0, 0:16 * nt], ACT.Sigmoid).then_inc(s["sig_done"], 1)
                    for e in range(1, 16, 2):
                        act.wait_ge(s["bcast"], e + 1)
                        nc.scalar.activation(gates[:, e, 0:tokens], ps[:, 2 + e % 4, 0:tokens], ACT.Copy).then_inc(s["act_copied"], 1)

                @block.vector
                def _(dve):
                    link = chain(dve, s["link"])
                    V = nc.vector
                    dve.wait_ge(s["w_in"], 32)
                    dve.wait_ge(s["sig_done"], 1)
                    link(V.tensor_tensor(sel[:], sc[:], rb[:].unsqueeze(1).to_broadcast([P, nt, 16]), ALU.add))
                    v = sel[:].rearrange("p t (g j) -> p (t g) j", j=4)

                    def ranks(vals, n, out):
                        vi = vals.unsqueeze(3).to_broadcast([P, n, 4, 4])
                        vj = vals.unsqueeze(2).to_broadcast([P, n, 4, 4])
                        link(V.tensor_tensor(gt[:, 0:n], vj, vi, ALU.is_gt))
                        link(V.tensor_tensor(eq[:, 0:n], vj, vi, ALU.is_equal))
                        tie = self.c("tie", 16).rearrange("p (i j) -> p i j", j=4).unsqueeze(1).to_broadcast([P, n, 4, 4])
                        link(V.tensor_tensor(eq[:, 0:n], eq[:, 0:n], tie, ALU.mult))
                        link(V.tensor_tensor(gt[:, 0:n], gt[:, 0:n], eq[:, 0:n], ALU.add))
                        link(V.tensor_reduce(out, gt[:, 0:n], AX.X, ALU.add))

                    ranks(v, G, rank[:])
                    link(V.tensor_scalar(rank[:], rank[:], 2.0, None, ALU.is_lt))
                    link(V.tensor_tensor(eq[:, :, 0, :], v, rank[:], ALU.mult))
                    link(V.tensor_reduce(gs[:].rearrange("p t g -> p (t g)"), eq[:, :, 0, :], AX.X, ALU.add))
                    ranks(gs[:], nt, grank[:])
                    link(V.tensor_scalar(grank[:], grank[:], 1.0, None, ALU.is_lt))
                    link(V.tensor_tensor(rank[:], rank[:], grank[:].rearrange("p t g -> p (t g)").unsqueeze(2).to_broadcast([P, G, 4]), ALU.mult))
                    link(V.tensor_tensor(comb[:], sc[:], rank[:].rearrange("p (t g) j -> p t (g j)", g=4), ALU.mult))
                    link(V.tensor_reduce(tot[:], comb[:], AX.X, ALU.add))
                    link(V.reciprocal(tot[:], tot[:]))
                    V.tensor_tensor(comb[:], comb[:], tot[:].unsqueeze(2).to_broadcast([P, nt, 16]), ALU.mult).then_inc(s["comb_done"], 1)
                    dve.wait_ge(s["transposed"], 1)
                    V.tensor_copy(combT[:], ps[0:16, 1, 0:tokens]).then_inc(s["t_copied"], 1)
                    for e in range(0, 16, 2):
                        dve.wait_ge(s["bcast"], e + 1)
                        V.tensor_copy(gates[:, e, 0:tokens], ps[:, 2 + e % 4, 0:tokens]).then_inc(s["dve_copied"], 1)

    def experts(self, layer, tokens):
        nc, ring, ps, H, X = self.nc, self.ring, self.ps, self.H, self.X
        NE = 16
        base = ring.chunks
        used = {a: ring.used[a] for a in "ABCD"}
        halves = [(c, slice(c * SEQ, (c + 1) * SEQ)) for c in range(tokens // SEQ)]
        nh = len(halves)
        row0 = 16 * layer
        T = slice(0, tokens)
        PER = 16
        with ExitStack() as ctx:
            gates = self.sb(ctx, "gates", [P, NE, tokens])
            self.route(gates, tokens)
            sg = self.sb(ctx, "silu_gate", [P, 2, tokens])
            up = self.sb(ctx, "gated_up", [P, 2, tokens])
            hid = self.sb(ctx, "hidden", [P, 4, tokens])
            with stage(nc, "silu_done up_done hid_done added") as (block, s):
                @block.sync
                def _(sp):
                    with sp.Fori(0, NE - 1) as e:
                        for area, last, src in (("A", 7, self.d["moe_gate"][e + (row0 + 1)]),
                                                ("B", 8, self.d["moe_up"][e + (row0 + 1)]),
                                                ("C", 16, self.d["moe_down"][e * 2 + 2 * (row0 + 1)]),
                                                ("D", 16, self.d["moe_down"][e * 2 + 2 * (row0 + 1) + 1])):
                            sp.wait_ge(ring.chunk_done, e * PER + base + last)
                            sp.dma_start(ring.buf[area][:], src).then_inc(ring.landed[area], 16)
                    for area, last in (("A", 7), ("B", 8), ("C", 16), ("D", 16)):
                        ring.sent[area] += NE - 1
                        ring.load(sp, area, base + PER * (NE - 1) + last)

                @block.tensor
                def _(pe):
                    with pe.Fori(0, NE) as e:
                        for j in range(4):
                            for what, area in enumerate("AB"):
                                if j == 0:
                                    pe.wait_ge(ring.landed[area], e * 16 + 16 * (used[area] + 1))
                                pe.wait_ge(s["silu_done"] if what == 0 else s["up_done"], e * 4 + max(0, j - 1) + 1)
                                for k in range(KD):
                                    last = nc.tensor.matmul(ps[:, 2 * what + j % 2, T],
                                                            ring.buf[area][:, k * 512 + j * P:k * 512 + (j + 1) * P],
                                                            H[:, k, T], start=(k == 0), stop=(k == KD - 1))
                                last.then_inc(ring.chunk_done, 1)
                        for m in range(KD):
                            pe.wait_ge(s["added"], e * (nh * KD) + (nh * (m - 3) if m >= 4 else 0) + 1)
                            for k in range(4):
                                area = "CD"[k // 2]
                                if m == 0:
                                    if k % 2 == 0:
                                        pe.wait_ge(ring.landed[area], e * 16 + 16 * (used[area] + 1))
                                    pe.wait_ge(s["hid_done"], e * 4 + k + 1)
                                last = nc.tensor.matmul(ps[:, 4 + m % 4, T],
                                                        ring.buf[area][:, (k % 2) * 1024 + m * P:(k % 2) * 1024 + (m + 1) * P],
                                                        hid[:, k, T], start=(k == 0), stop=(k == 3))
                            last.then_inc(ring.chunk_done, 1)

                @block.scalar
                def _(act):
                    self.credit(nc.scalar, s["silu_done"])
                    with act.Fori(0, NE) as e:
                        for j in range(4):
                            act.wait_ge(ring.chunk_done, e * PER + base + 2 * j + 1)
                            act.wait_ge(s["up_done"], e * 4 + max(0, j - 1) + 1)
                            nc.scalar.activation(sg[:, j % 2, :], ps[:, j % 2, T], ACT.Silu).then_inc(s["silu_done"], 1)

                @block.vector
                def _(dve):
                    self.credit(nc.vector, s["up_done"])
                    self.credit(nc.vector, s["added"], 2)
                    with dve.Fori(0, NE) as e:
                        for j in range(4):
                            dve.wait_ge(ring.chunk_done, e * PER + base + 2 * j + 2)
                            dve.wait_ge(s["silu_done"], e * 4 + j + 2)
                            nc.vector.tensor_tensor(up[:, j % 2, :], ps[:, 2 + j % 2, T], sg[:, j % 2, :],
                                                    ALU.mult).then_inc(s["up_done"], 1)
                            dve.wait_ge(s["up_done"], e * 4 + j + 2)
                            nc.vector.tensor_tensor(hid[:, j, :], up[:, j % 2, :],
                                                    gates[:, bass.ds(e, 1), :].rearrange("p e t -> p (e t)"),
                                                    ALU.mult).then_inc(s["hid_done"], 1)
                        for m in range(KD):
                            dve.wait_ge(ring.chunk_done, e * PER + base + 8 + m + 1)
                            dve.wait_ge(s["added"], e * (nh * KD) + 1)
                            for c, t in halves:
                                nc.vector.scalar_tensor_tensor(out=X[:, m, t], in0=ps[:, 4 + m % 4, t],
                                                               scalar=self.m(layer, 5, m, c), in1=X[:, m, t],
                                                               op0=ALU.mult, op1=ALU.add).then_inc(s["added"], 1)

        for a in "ABCD":
            ring.used[a] += NE
        ring.chunks += PER * NE

    def odd_in(self, Q, G, V, K, LF):
        nc, ring, ps, H = self.nc, self.ring, self.ps, self.H
        base = ring.chunks
        areas = "AB" * 5
        with ExitStack() as ctx:
            rows = self.sb(ctx, "lb_rows", [P, 2, D])
            top = self.sb(ctx, "lb_max", [P, D])
            with stage(nc, "rows_in link exps act_read dve_read f_scaled f_done k_done ln_done") as (block, s):
                @block.sync
                def _(sp):
                    sp.dma_start(rows[:].rearrange("p l n -> p (l n)"), self.d["lb_rows"].partition_broadcast(P)).then_inc(s["rows_in"], 16)
                    for i, area in enumerate(areas):
                        ring.load(sp, area, base + 4 * (i + 1))

                @block.tensor
                def _(pe):
                    def free(n):
                        if n >= 6:
                            j = n - 6
                            if j < 16:
                                pe.wait_ge(s["act_read"], j + 1)
                            elif j < 24:
                                pe.wait_ge(s["dve_read"], j - 15)
                            else:
                                pe.wait_ge(s["act_read"], j - 7)
                    for i in range(4):
                        self.panel_products(pe, None, areas[i], KD, 512, lambda k: H[:, k, 0:SEQ], 4 * i, range(6), SEQ, free)
                    for i in range(4, 10):
                        area = areas[i]
                        ring.arrived(pe, area)
                        for t in range(NT):
                            free(4 * i + t)
                            for k in range(KD):
                                last = nc.tensor.matmul(ps[:, (4 * i + t) % 6, :], H[:, k, t * P:(t + 1) * P],
                                                        ring.buf[area][:, k * 512:(k + 1) * 512],
                                                        start=(k == 0), stop=(k == KD - 1))
                            last.then_inc(ring.chunk_done, 1)

                @block.scalar
                def _(act):
                    act.wait_ge(s["link"], 2)
                    nc.scalar.activation(rows[:], rows[:], ACT.Exp).then_inc(s["exps"], 1)
                    for n in range(16):
                        act.wait_ge(ring.chunk_done, base + n + 1)
                        dst = Q[:, n, :] if n < 8 else G[:, n - 8, :]
                        nc.scalar.activation(dst, ps[:, n % 6, 0:SEQ], ACT.Silu).then_inc(s["act_read"], 1)
                    for n in range(24, 40):
                        act.wait_ge(ring.chunk_done, base + n + 1)
                        i, t = divmod(n - 24, 4)
                        nc.scalar.activation(K[:, t, i * 512:(i + 1) * 512], ps[:, n % 6, :], ACT.Sigmoid).then_inc(s["act_read"], 1)
                    for t in range(NT):
                        act.wait_ge(s["f_done"], 16)
                        act.wait_ge(s["k_done"], 16)
                        nc.scalar.activation(LF[:, t, :], LF[:, t, :], ACT.Ln).then_inc(s["ln_done"], 1)

                @block.vector
                def _(dve):
                    link = chain(dve, s["link"])
                    dve.wait_ge(s["rows_in"], 16)
                    link(nc.vector.tensor_tensor(top[:], rows[:, 0, :], rows[:, 1, :], ALU.max))
                    link(nc.vector.tensor_tensor(rows[:], rows[:], top[:].unsqueeze(1).to_broadcast([P, 2, D]), ALU.subtract))
                    dve.wait_ge(s["exps"], 1)
                    link(nc.vector.tensor_tensor(top[:], rows[:, 0, :], rows[:, 1, :], ALU.add))
                    link(nc.vector.reciprocal(top[:], top[:]))
                    link(nc.vector.tensor_tensor(rows[:, 1, :], rows[:, 1, :], top[:], ALU.mult))
                    link(nc.vector.tensor_scalar(rows[:, 0, :], rows[:, 1, :], -1.0, 1.0, ALU.mult, ALU.add))
                    for n in range(16, 24):
                        dve.wait_ge(ring.chunk_done, base + n + 1)
                        i, t = divmod(n - 16, 4)
                        nc.vector.tensor_copy(V[:, t, i * 512:(i + 1) * 512], ps[:, n % 6, :]).then_inc(s["dve_read"], 1)
                    for n in range(16):
                        i, t = divmod(n, 4)
                        cols = slice(i * 512, (i + 1) * 512)
                        feats = slice((i % 2) * 512, (i % 2 + 1) * 512)
                        dve.wait_ge(s["act_read"], 16 + n + 1)
                        nc.vector.tensor_tensor(LF[:, t, cols], K[:, t, cols], rows[:, 0, feats], ALU.mult).then_inc(s["f_scaled"], 1)
                        dve.wait_ge(s["f_scaled"], n + 1)
                        nc.vector.tensor_tensor(LF[:, t, cols], LF[:, t, cols], rows[:, 1, feats], ALU.add).then_inc(s["f_done"], 1)

                @block.gpsimd
                def _(pool):
                    for n in range(16):
                        i, t = divmod(n, 4)
                        cols = slice(i * 512, (i + 1) * 512)
                        pool.wait_ge(s["f_done"], n + 1)
                        nc.gpsimd.tensor_scalar(K[:, t, cols], LF[:, t, cols], -1.0, 1.0, ALU.mult, ALU.add).then_inc(s["k_done"], 1)
        ring.chunks += 40

    def recurrence(self, units, lf, kt, kall, q, v, v2, mids, out, context):
        nc, ps, H = self.nc, self.ps, self.H
        N = len(units)
        nt = NT if context else 2
        with ExitStack() as ctx:
            KE = self.sb(ctx, "k_end", [P, 2, nt, P])
            G = self.sb(ctx, "gcum", [P, 2, SEQ])
            Dm = self.sb(ctx, "gcum_mid", [P, 2, SEQ])
            QR = self.sb(ctx, "q_rel", [P, 2, SEQ])
            KR = self.sb(ctx, "k_rel", [P, 2, SEQ])
            E3 = self.sb(ctx, "exp_gcum", [P, 2, SEQ])
            QG = self.sb(ctx, "q_decayed", [P, 2, SEQ])
            VH = self.sb(ctx, "v_halves", [P, 2, 2, 2, P])
            AM = H[:, 4:6, SEQ:TT]

            def S(b, n):
                return H[:, 2 * b + n // 2, SEQ + (n % 2) * P:SEQ + (n % 2 + 1) * P]
            GC, KX, KT, ATT, CS, O, S0 = range(7)
            with stage(nc, "g_sum kx_sum kt_sum att_sum cs_sum o_sum g_copied d_done krel_done ke_done att_masked "
                           "s_chain o_done exp_done qrel_done qg_done vh_done zeroed") as (block, s):
                @block.tensor
                def _(pe):
                    def front(u):
                        h, d = units[u]
                        cum = self.c(("up64", "lo64")[d])
                        after, after_all = self.c(("xlo64", "xup64")[d]), self.c(("lower_x", "upper_x")[d])
                        if u >= 1:
                            pe.wait_ge(s["g_copied"], u)
                        for t in range(2):
                            last = nc.tensor.matmul(ps[:, GC, t * P:(t + 1) * P], lf(u, t), cum, start=True, stop=True)
                        last.then_inc(s["g_sum"], 1)
                        if u >= 1:
                            pe.wait_ge(s["exp_done"], 4 * (u - 1) + 1)
                        for t in range(2):
                            last = nc.tensor.matmul(ps[:, KX, t * P:(t + 1) * P], after, lf(u, t), start=True, stop=True)
                        if context:
                            first, second = (2, 3) if d == 0 else (3, 2)
                            nc.tensor.matmul(ps[:, KX, first * P:(first + 1) * P], after_all, lf(u, first), start=True, stop=False)
                            nc.tensor.matmul(ps[:, KX, first * P:(first + 1) * P], self.c("ones"), lf(u, second), start=False, stop=True)
                            last = nc.tensor.matmul(ps[:, KX, second * P:(second + 1) * P], after_all, lf(u, second),
                                                    start=True, stop=True)
                        last.then_inc(s["kx_sum"], 1)
                        if u >= 1:
                            pe.wait_ge(s["krel_done"], u)
                        for t in range(2):
                            last = nc.tensor.transpose(ps[:, KT, t * P:(t + 1) * P], kt(u, t), self.c("ident"))
                        last.then_inc(s["kt_sum"], 1)

                    def scores_states(u):
                        h, d = units[u]
                        pe.wait_ge(s["krel_done"], u + 1)
                        pe.wait_ge(s["qrel_done"], u + 1)
                        if u >= 1:
                            pe.wait_ge(s["att_masked"], u)
                            pe.wait_ge(s["s_chain"], 4 * u)
                        for t in range(2):
                            last = nc.tensor.matmul(ps[:, ATT, t * P:(t + 1) * P], KR[:, u % 2, t * P:(t + 1) * P],
                                                    QR[:, u % 2, t * P:(t + 1) * P], start=True, stop=True)
                        last.then_inc(s["att_sum"], 1)
                        pe.wait_ge(s["ke_done"], u + 1)
                        pe.wait_ge(s["vh_done"], u + 1)
                        for i, t in enumerate((2, 3) if context else ()):
                            nc.tensor.matmul(ps[:, S0, 0:P], KE[:, u % 2, t, :], v(u, t),
                                             start=(i == 0), stop=(i == 1))
                        for t in range(2):
                            last = nc.tensor.matmul(ps[:, CS, t * SEQ:(t + 1) * SEQ], KE[:, u % 2, t, :],
                                                    VH[:, u % 2, t, :, :].rearrange("p h v -> p (h v)"), start=True, stop=True)
                        last.then_inc(s["cs_sum"], 1)

                    def outputs(u):
                        h, d = units[u]
                        pe.wait_ge(s["att_masked"], u + 1)
                        pe.wait_ge(s["s_chain"], 4 * u + 4)
                        pe.wait_ge(s["qg_done"], u + 1)
                        if u >= 1:
                            pe.wait_ge(s["o_done"], u)
                        for t in range(2):
                            nc.tensor.matmul(ps[:, O, t * P:(t + 1) * P], v(u, t),
                                             AM[:, u % 2, t * P:(t + 1) * P], start=True, stop=False)
                            for half in range(2):
                                c = 2 * t + half
                                n = c if d == 0 else 3 - c
                                last = nc.tensor.matmul(ps[:, O, c * 64:(c + 1) * 64], S(u % 2, n),
                                                        QG[:, u % 2, c * 64:(c + 1) * 64], start=False, stop=(half == 1))
                        last.then_inc(s["o_sum"], 1)
                    front(0)
                    for u in range(N):
                        scores_states(u)
                        if u + 1 < N:
                            front(u + 1)
                        outputs(u)

                @block.scalar
                def _(act):
                    for u in range(N):
                        b = u % 2
                        act.wait_ge(s["kx_sum"], u + 1)
                        if u >= 2:
                            act.wait_ge(s["cs_sum"], u - 1)
                        nc.scalar.activation(KE[:, b, :, :].rearrange("p t k -> p (t k)"), ps[:, KX, 0:nt * P], ACT.Exp).then_inc(s["exp_done"], 1)
                        act.wait_ge(s["d_done"], u + 1)
                        if u >= 2:
                            act.wait_ge(s["att_sum"], u - 1)
                            act.wait_ge(s["s_chain"], 4 * (u - 1))
                            act.wait_ge(s["qg_done"], u - 1)
                        nc.scalar.activation(QR[:, b, :], Dm[:, b, :], ACT.Exp).then_inc(s["exp_done"], 1)
                        nc.scalar.activation(KR[:, b, :], Dm[:, b, :], ACT.Exp, scale=-1.0).then_inc(s["exp_done"], 1)
                        nc.scalar.activation(E3[:, b, :], G[:, b, :], ACT.Exp).then_inc(s["exp_done"], 1)

                @block.gpsimd
                def _(pool):
                    for u, (h, d) in enumerate(units):
                        b = u % 2
                        if u >= 2:
                            pool.wait_ge(s["cs_sum"], u - 1)
                        for half in range(2):
                            ins = nc.gpsimd.tensor_scalar(VH[:, b, :, half, :], v2(u),
                                                          self.c("half", 1, off=half), None, ALU.mult)
                        ins.then_inc(s["vh_done"], 1)
                        pool.wait_ge(s["exp_done"], 4 * u + 2)
                        nc.gpsimd.tensor_tensor(QR[:, b, :], QR[:, b, :], q(u), ALU.mult).then_inc(s["qrel_done"], 1)
                        pool.wait_ge(s["exp_done"], 4 * u + 4)
                        if u >= 2:
                            pool.wait_ge(s["o_sum"], u - 1)
                        nc.gpsimd.tensor_tensor(QG[:, b, :], E3[:, b, :], q(u), ALU.mult).then_inc(s["qg_done"], 1)

                @block.vector
                def _(dve):
                    def gates(u):
                        h, d = units[u]
                        b = u % 2
                        dve.wait_ge(s["g_sum"], u + 1)
                        if u >= 2:
                            dve.wait_ge(s["exp_done"], 4 * (u - 1))
                        nc.vector.tensor_copy(G[:, b, :], ps[:, GC, 0:SEQ]).then_inc(s["g_copied"], 1)
                        dve.wait_ge(s["g_copied"], u + 1)
                        g = G[:, b, :].rearrange("p (c t) -> p c t", t=64)
                        mid = mids[d]
                        nc.vector.tensor_tensor(Dm[:, b, :].rearrange("p (c t) -> p c t", t=64), g,
                                                g[:, :, mid:mid + 1].to_broadcast([P, 4, 64]), ALU.subtract).then_inc(s["d_done"], 1)
                        dve.wait_ge(s["exp_done"], 4 * u + 1)
                        nc.vector.tensor_tensor(KE[:, b, :, :], KE[:, b, :, :], kall(u),
                                                ALU.mult).then_inc(s["ke_done"], 1)
                        dve.wait_ge(s["exp_done"], 4 * u + 3)
                        dve.wait_ge(s["kt_sum"], u + 1)
                        nc.vector.tensor_tensor(KR[:, b, :], KR[:, b, :], ps[:, KT, 0:SEQ], ALU.mult).then_inc(s["krel_done"], 1)

                    def mask_and_states(u):
                        h, d = units[u]
                        b = u % 2
                        dve.wait_ge(s["att_sum"], u + 1)
                        if u >= 2:
                            dve.wait_ge(s["o_sum"], u - 1)
                        nc.vector.copy_predicated(AM[:, b, :].rearrange("p (t l) -> p t l", t=2),
                                                  self.c(("up64", "lo64")[d]).bitcast(U32).unsqueeze(1).to_broadcast([P, 2, P]),
                                                  ps[:, ATT, 0:SEQ].rearrange("p (t l) -> p t l", t=2)).then_inc(s["att_masked"], 1)
                        dve.wait_ge(s["cs_sum"], u + 1)
                        if context:
                            nc.vector.tensor_copy(S(b, 0), ps[:, S0, 0:P]).then_inc(s["s_chain"], 1)
                        else:
                            nc.vector.memset(S(b, 0), 0.0).then_inc(s["s_chain"], 1)
                        dve.wait_ge(s["exp_done"], 4 * u + 4)
                        for n in range(3):
                            c = n if d == 0 else 3 - n
                            end = c * 64 + (63 if d == 0 else 0)
                            dve.wait_ge(s["s_chain"], 4 * u + n + 1)
                            nc.vector.scalar_tensor_tensor(out=S(b, n + 1), in0=S(b, n), scalar=E3[:, b, end:end + 1],
                                                           in1=ps[:, CS, c * P:(c + 1) * P], op0=ALU.mult,
                                                           op1=ALU.add).then_inc(s["s_chain"], 1)

                    def take_outputs(u):
                        h, d = units[u]
                        dve.wait_ge(s["o_sum"], u + 1)
                        if d == 0:
                            nc.vector.tensor_copy(out(u), ps[:, O, 0:SEQ]).then_inc(s["o_done"], 1)
                        else:
                            dve.wait_ge(s["o_done"], u)
                            nc.vector.tensor_tensor(out(u), out(u), ps[:, O, 0:SEQ], ALU.add).then_inc(s["o_done"], 1)
                    nc.vector.memset(AM, 0.0).then_inc(s["zeroed"], 1)
                    dve.wait_ge(s["zeroed"], 1)
                    gates(0)
                    for u in range(N):
                        mask_and_states(u)
                        if u + 1 < N:
                            gates(u + 1)
                        take_outputs(u)

    def head_norm_gate(self, O, pairs, scale, G):
        nc, ps = self.nc, self.ps
        with ExitStack() as ctx:
            sq = self.sb(ctx, "head_squares", [P, pairs, 2, SEQ])
            root = self.sb(ctx, "head_root", [P, pairs, 2, SEQ])
            with stage(nc, "squared summed rooted inverted scaled gated") as (block, s):
                @block.scalar
                def _(act):
                    for j in range(pairs):
                        nc.scalar.activation(sq[:, j, :, :], O(j), ACT.Square).then_inc(s["squared"], 1)
                    for j in range(pairs):
                        act.wait_ge(s["summed"], j + 1)
                        nc.scalar.activation(root[:, j, :, :], ps[:, j, :].rearrange("p (h t) -> p h t", h=2), ACT.Sqrt,
                                             bias=self.eps[:, 0:1], scale=1.0 / P).then_inc(s["rooted"], 1)

                @block.tensor
                def _(pe):
                    for j in range(pairs):
                        pe.wait_ge(s["squared"], j + 1)
                        nc.tensor.matmul(ps[:, j, :], self.c("ones"), sq[:, j, :, :].rearrange("p h t -> p (h t)"),
                                         start=True, stop=True).then_inc(s["summed"], 1)

                @block.vector
                def _(dve):
                    for j in range(pairs):
                        dve.wait_ge(s["rooted"], j + 1)
                        nc.vector.reciprocal(root[:, j, :, :], root[:, j, :, :]).then_inc(s["inverted"], 1)
                        dve.wait_ge(s["inverted"], j + 1)
                        nc.vector.scalar_tensor_tensor(out=O(j), in0=O(j), scalar=scale, in1=root[:, j, :, :],
                                                       op0=ALU.mult, op1=ALU.mult).then_inc(s["scaled"], 1)
                        dve.wait_ge(s["scaled"], j + 1)
                        nc.vector.tensor_tensor(O(j), O(j), G(j), ALU.mult).then_inc(s["gated"], 1)

    def odd_mixer(self):
        with ExitStack() as ctx:
            Q = self.sb(ctx, "q", [P, 8, SEQ])
            G = self.sb(ctx, "g", [P, 8, SEQ])
            V = self.sb(ctx, "v", [P, NT, D])
            K = self.sb(ctx, "k", [P, NT, 2 * D])
            LF = self.sb(ctx, "log_f", [P, NT, 2 * D])
            self.odd_in(Q, G, V, K, LF)
            units = [(h, d) for h in range(8) for d in range(2)]

            def cols(u):
                h, d = units[u]
                return slice(d * D + h * P, d * D + (h + 1) * P)

            def head(u):
                return slice(units[u][0] * P, (units[u][0] + 1) * P)
            self.recurrence(units, lf=lambda u, t: LF[:, t, cols(u)], kt=lambda u, t: K[:, t, cols(u)],
                            kall=lambda u: K[:, :, cols(u)], q=lambda u: Q[:, units[u][0], :],
                            v=lambda u, t: V[:, t, head(u)], v2=lambda u: V[:, 0:2, head(u)], mids=(31, 32),
                            out=lambda u: self.H[:, units[u][0], 0:SEQ], context=True)
            self.head_norm_gate(lambda j: self.H[:, 2 * j:2 * j + 2, 0:SEQ], 4, self.v("hg_g"), lambda j: G[:, 2 * j:2 * j + 2, :])
            self.out_projection("AB", KD, lambda k: self.H[:, k, 0:SEQ], 1, SEQ, permuted=True)

    def feed_forward(self, n):
        nc, ring, ps, H, X, d = self.nc, self.ring, self.ps, self.H, self.X, self.d
        T = slice(0, SEQ)
        self.rms_norm(self.x_chunk, self.h_chunk, KD, SEQ, lambda k, c: self.v("ffn_norm2", 8 * n + k))
        base = ring.chunks
        used = {a: ring.used[a] for a in "ABCD"}
        BLOCKS, PER = 11, 12
        row0 = BLOCKS * n
        pairs = BLOCKS // 2
        with ExitStack() as ctx:
            sg = self.sb(ctx, "silu_gate", [P, 2, SEQ])
            hid = self.sb(ctx, "hidden", [P, 2, 2, SEQ])
            with stage(nc, "silu_done hid_done added") as (block, s):
                @block.sync
                def _(sp):
                    with sp.Fori(0, pairs - 1) as i:
                        for b in range(2):
                            gu, dn = "AB"[b], "CD"[b]
                            sp.wait_ge(ring.chunk_done, i * (2 * PER) + base + PER * b + 4)
                            sp.dma_start(ring.buf[gu][:], d["ffn_gu"][i * 2 + (row0 + b + 2)]).then_inc(ring.landed[gu], 16)
                            sp.wait_ge(ring.chunk_done, i * (2 * PER) + base + PER * (b + 1))
                            sp.dma_start(ring.buf[dn][:], d["ffn_down"][i * 2 + (row0 + b + 2)]).then_inc(ring.landed[dn], 16)
                    for a in "ABCD":
                        ring.sent[a] += pairs - 1
                    for j in range(2 * (pairs - 1), BLOCKS):
                        ring.load(sp, "AB"[j % 2], base + PER * j + 4)
                        ring.load(sp, "CD"[j % 2], base + PER * j + PER)

                @block.tensor
                def _(pe):
                    def one(i, b):
                        gu, dn = "AB"[b], "CD"[b]
                        j2 = i * 4 + 2 * b
                        for c in range(2):
                            for what in range(2):
                                if c == 0 and what == 0:
                                    pe.wait_ge(ring.landed[gu], i * 16 + 16 * (used[gu] + 1))
                                if c == 0:
                                    pe.wait_ge(s["silu_done"] if what == 0 else s["hid_done"], j2 + 1)
                                for k in range(KD):
                                    off = k * 512 + what * 256 + c * P
                                    last = nc.tensor.matmul(ps[:, 2 * what + c, T], ring.buf[gu][:, off:off + P], H[:, k, T],
                                                            start=(k == 0), stop=(k == KD - 1))
                                last.then_inc(ring.chunk_done, 1)
                        for m in range(KD):
                            pe.wait_ge(s["added"], i * 16 + 8 * b + (m - 3 if m >= 4 else 0) + 1)
                            for k in range(2):
                                if m == 0:
                                    if k == 0:
                                        pe.wait_ge(ring.landed[dn], i * 16 + 16 * (used[dn] + 1))
                                    pe.wait_ge(s["hid_done"], j2 + k + 2)
                                last = nc.tensor.matmul(ps[:, 4 + m % 4, T], ring.buf[dn][:, k * D + m * P:k * D + (m + 1) * P],
                                                        hid[:, b, k, :], start=(k == 0), stop=(k == 1))
                            last.then_inc(ring.chunk_done, 1)
                    with pe.Fori(0, pairs) as i:
                        one(i, 0)
                        one(i, 1)
                    one(pairs, 0)

                @block.scalar
                def _(act):
                    def one(i, b):
                        for c in range(2):
                            act.wait_ge(ring.chunk_done, i * (2 * PER) + base + PER * b + 2 * c + 1)
                            act.wait_ge(s["hid_done"], i * 4 + 2 * b + 1)
                            nc.scalar.activation(sg[:, c, :], ps[:, c, T], ACT.Silu).then_inc(s["silu_done"], 1)
                    self.credit(nc.scalar, s["silu_done"])
                    with act.Fori(0, pairs) as i:
                        one(i, 0)
                        one(i, 1)
                    one(pairs, 0)

                @block.vector
                def _(dve):
                    def one(i, b):
                        for c in range(2):
                            dve.wait_ge(ring.chunk_done, i * (2 * PER) + base + PER * b + 2 * c + 2)
                            dve.wait_ge(s["silu_done"], i * 4 + 2 * b + c + 2)
                            nc.vector.tensor_tensor(hid[:, b, c, :], ps[:, 2 + c, T], sg[:, c, :], ALU.mult).then_inc(s["hid_done"], 1)
                        for m in range(KD):
                            dve.wait_ge(ring.chunk_done, i * (2 * PER) + base + PER * b + 4 + m + 1)
                            dve.wait_ge(s["added"], i * 16 + 8 * b + 1)
                            nc.vector.scalar_tensor_tensor(out=X[:, m, T], in0=ps[:, 4 + m % 4, T], scalar=0.5, in1=X[:, m, T],
                                                           op0=ALU.mult, op1=ALU.add).then_inc(s["added"], 1)
                    self.credit(nc.vector, s["hid_done"])
                    self.credit(nc.vector, s["added"], 2)
                    with dve.Fori(0, pairs) as i:
                        one(i, 0)
                        one(i, 1)
                    one(pairs, 0)
        for a, k in (("A", 6), ("B", 5), ("C", 6), ("D", 5)):
            ring.used[a] += k
        ring.chunks += PER * BLOCKS

    def rope_tables(self, cos, sin, column):
        nc = self.nc
        MAGIC = float(1.5 * 2 ** 23)
        parts = TWO_PI_PARTS
        with ExitStack() as ctx:
            pos = self.sb(ctx, "positions", [P, SEQ], mybir.dt.int32)
            ang = self.sb(ctx, "angle", [P, SEQ])
            turns = self.sb(ctx, "turns", [P, SEQ])
            with stage(nc, "pos_in link sines") as (block, s):
                @block.sync
                def _(sp):
                    sp.dma_start(pos[:], self.d["positions"].partition_broadcast(P)).then_inc(s["pos_in"], 16)

                @block.vector
                def _(dve):
                    link = chain(dve, s["link"])
                    V = nc.vector
                    dve.wait_ge(s["pos_in"], 16)
                    link(V.tensor_copy(ang[:], pos[:]))
                    link(V.tensor_scalar(ang[:], ang[:], self.c("ropef", 1, off=column), None, ALU.mult))
                    for out, quarter in ((sin, 0.0), (cos, 0.25)):
                        link(V.tensor_scalar(turns[:], ang[:], float(1 / (2 * np.pi)), quarter, ALU.mult, ALU.add))
                        link(V.tensor_scalar(turns[:], turns[:], MAGIC, None, ALU.add))
                        link(V.tensor_scalar(turns[:], turns[:], MAGIC, None, ALU.subtract))
                        link(V.scalar_tensor_tensor(out=out, in0=turns[:], scalar=-parts[0], in1=ang[:], op0=ALU.mult, op1=ALU.add))
                        for part in parts[1:]:
                            link(V.scalar_tensor_tensor(out=out, in0=turns[:], scalar=-part, in1=out, op0=ALU.mult, op1=ALU.add))
                        if quarter:
                            link(V.tensor_scalar(out, out, float(np.float32(np.pi / 2)), None, ALU.add))
                        link(V.tensor_scalar(out, out, PI_BELOW, -PI_BELOW, ALU.min, ALU.max))

                @block.scalar
                def _(act):
                    act.wait_ge(s["link"], 2 + 7 + 8)
                    nc.scalar.activation(sin, sin, ACT.Sin).then_inc(s["sines"], 1)
                    nc.scalar.activation(cos, cos, ACT.Sin).then_inc(s["sines"], 1)

    def rotate(self, jobs, cos, sin, swap):
        nc, ps = self.nc, self.ps
        with ExitStack() as ctx:
            part = self.sb(ctx, "rotated", [P, 2, 2, SEQ])
            with stage(nc, "swapped sin_done cos_done done") as (block, s):
                def wide(t, n):
                    return t.unsqueeze(1).to_broadcast([P, n, SEQ])

                @block.tensor
                def _(pe):
                    for i, x in enumerate(jobs):
                        n = x.shape[1]
                        if i >= 2:
                            pe.wait_ge(s["sin_done"], i - 1)
                        for c in range(n):
                            last = nc.tensor.matmul(ps[:, i % 2, c * SEQ:(c + 1) * SEQ], swap, x[:, c, :], start=True, stop=True)
                        last.then_inc(s["swapped"], 1)

                @block.vector
                def _(dve):
                    for i, x in enumerate(jobs):
                        n = x.shape[1]
                        dve.wait_ge(s["swapped"], i + 1)
                        if i >= 2:
                            dve.wait_ge(s["done"], i - 1)
                        nc.vector.tensor_tensor(part[:, i % 2, 0:n, :], ps[:, i % 2, 0:n * SEQ].rearrange("p (n t) -> p n t", n=n),
                                                wide(sin, n), ALU.mult).then_inc(s["sin_done"], 1)
                        dve.wait_ge(s["cos_done"], i + 1)
                        dve.wait_ge(s["sin_done"], i + 1)
                        nc.vector.tensor_tensor(x, x, part[:, i % 2, 0:n, :], ALU.add).then_inc(s["done"], 1)

                @block.gpsimd
                def _(pool):
                    for i, x in enumerate(jobs):
                        n = x.shape[1]
                        pool.wait_ge(s["swapped"], i + 1)
                        nc.gpsimd.tensor_tensor(x, x, wide(cos, n), ALU.mult).then_inc(s["cos_done"], 1)

    def attention(self, heads, q, keys, values, scale, out, compressed=None, weights=None):
        nc, ps = self.nc, self.ps
        nb = keys(0).shape[1]
        NC = 15
        comp0 = nb * SEQ
        width = comp0 + (P if compressed else 0)
        na = nb + (1 if compressed else 0)
        units = [(h, t) for h in range(heads) for t in range(2)]
        N = len(units)
        with ExitStack() as ctx:
            PR = self.sb(ctx, "probs", [P, 2, width])
            PT = self.sb(ctx, "probs_t", [P, 2, width])
            negmax = self.sb(ctx, "neg_max", [P, 2, 4])
            total = self.sb(ctx, "total", [P, 2, 4])
            with stage(nc, "scores_done masked maxed exp_done link scaled transposed pt_copied summed o_copied") as (block, s):
                def wide(t):
                    return (t + 1) * P

                def pieces(u):
                    h, t = units[u]
                    all_ = [(b * SEQ + kt * P, values(h, b, kt)) for b in range(nb) for kt in range(t + 1)]
                    if compressed:
                        all_.append((comp0, compressed[1](h)))
                    return all_

                @block.tensor
                def _(pe):
                    def scores(u):
                        h, t = units[u]
                        if u >= 2:
                            pe.wait_ge(s["masked"], u - 1)
                        W = wide(t)
                        for b in range(nb):
                            last = nc.tensor.matmul(ps[:, u % 2, b * SEQ:b * SEQ + W], q(h)[:, t * P:(t + 1) * P],
                                                    keys(h)[:, b, 0:W], start=True, stop=True)
                        if compressed:
                            last = nc.tensor.matmul(ps[:, 2 + u % 2, 0:NC], q(h)[:, t * P:(t + 1) * P], compressed[0](h),
                                                    start=True, stop=True)
                        last.then_inc(s["scores_done"], 1)

                    def transposes(u):
                        pe.wait_ge(s["scaled"], u + 1)
                        if u >= 1:
                            pe.wait_ge(s["pt_copied"], u)
                        for i, (col, _) in enumerate(pieces(u)):
                            last = nc.tensor.transpose(ps[:, 4 + i // 4, (i % 4) * P:(i % 4 + 1) * P],
                                                       PR[:, u % 2, col:col + P], self.c("ident"))
                        last.then_inc(s["transposed"], 1)

                    def product(u):
                        h, t = units[u]
                        pe.wait_ge(s["pt_copied"], u + 1)
                        if u >= 2:
                            pe.wait_ge(s["o_copied"], u - 1)
                        lo = 64 * (h % 2)
                        js = pieces(u)
                        for i, (_, val) in enumerate(js):
                            last = nc.tensor.matmul(ps[lo:lo + 64, 6 + u % 2, 0:P], val, PT[:, u % 2, i * P:(i + 1) * P],
                                                    start=(i == 0), stop=(i == len(js) - 1))
                        last.then_inc(s["summed"], 1)
                    scores(0)
                    scores(1)
                    for u in range(N):
                        transposes(u)
                        if u + 2 < N:
                            scores(u + 2)
                        product(u)

                @block.vector
                def _(dve):
                    V = nc.vector
                    linked = [0]

                    def link(ins):
                        linked[0] += 1
                        ins.then_inc(s["link"], 1)
                        dve.wait_ge(s["link"], linked[0])

                    def mask_and_max(u):
                        h, t = units[u]
                        W, b2 = wide(t), u % 2
                        dve.wait_ge(s["scores_done"], u + 1)
                        if u >= 2:
                            dve.wait_ge(s["transposed"], u - 1)
                        pr = PR[:, b2, 0:comp0].rearrange("p (b k) -> p b k", b=nb)[:, :, 0:W]
                        sc = ps[:, u % 2, 0:comp0].rearrange("p (b k) -> p b k", b=nb)[:, :, 0:W]
                        if compressed:
                            link(V.scalar_tensor_tensor(out=PR[:, b2, comp0:comp0 + NC], in0=ps[:, 2 + u % 2, 0:NC], scalar=scale,
                                                        in1=self.c("cmp_add", NC, off=16 * t), op0=ALU.mult, op1=ALU.add))
                        V.scalar_tensor_tensor(out=pr, in0=sc, scalar=scale,
                                               in1=self.c("causal_add", W, off=P * (1 - t)).unsqueeze(1).to_broadcast([P, nb, W]),
                                               op0=ALU.mult, op1=ALU.add).then_inc(s["masked"], 1)
                        dve.wait_ge(s["masked"], u + 1)
                        if u >= 2:
                            dve.wait_ge(s["exp_done"], na * (u - 1))
                        if compressed:
                            V.tensor_reduce(negmax[:, b2, nb:nb + 1], PR[:, b2, comp0:comp0 + NC], AX.X, ALU.max, negate=True)
                        V.tensor_reduce(negmax[:, b2, 0:nb], pr, AX.X, ALU.max, negate=True).then_inc(s["maxed"], 1)

                    def normalise(u):
                        h, t = units[u]
                        W, b2 = wide(t), u % 2
                        dve.wait_ge(s["exp_done"], na * (u + 1))
                        pr = PR[:, b2, 0:comp0].rearrange("p (b k) -> p b k", b=nb)[:, :, 0:W]
                        tt = total[:, b2, 0:na]
                        if compressed:
                            pc = PR[:, b2, comp0:comp0 + NC]
                            link(V.tensor_tensor(pc, pc, self.c("cmp_mask", NC, off=16 * t), ALU.mult))
                            link(V.tensor_reduce(total[:, b2, nb:nb + 1], pc, AX.X, ALU.add))
                        link(V.tensor_scalar(tt, tt, 1e-30, None, ALU.max))
                        link(V.reciprocal(tt, tt))
                        if weights:
                            link(V.tensor_tensor(tt, tt, weights(h, t), ALU.mult))
                        if compressed:
                            V.tensor_scalar(pc, pc, total[:, b2, nb:nb + 1], None, ALU.mult)
                        V.tensor_tensor(pr, pr, total[:, b2, 0:nb].unsqueeze(2).to_broadcast([P, nb, W]), ALU.mult).then_inc(s["scaled"], 1)
                    if compressed:
                        link(V.memset(PR[:], 0.0))
                    mask_and_max(0)
                    for u in range(N):
                        if u + 1 < N:
                            mask_and_max(u + 1)
                        normalise(u)

                @block.scalar
                def _(act):
                    def exps(u):
                        h, t = units[u]
                        W, b2 = wide(t), u % 2
                        act.wait_ge(s["maxed"], u + 1)
                        if u >= 2:
                            act.wait_ge(s["scaled"], u - 1)
                        for b in range(nb):
                            pr = PR[:, b2, b * SEQ:b * SEQ + W]
                            nc.scalar.activation(pr, pr, ACT.Exp, bias=negmax[:, b2, b:b + 1],
                                                 accum_out=total[:, b2, b:b + 1]).then_inc(s["exp_done"], 1)
                        if compressed:
                            pc = PR[:, b2, comp0:comp0 + NC]
                            nc.scalar.activation(pc, pc, ACT.Exp, bias=negmax[:, b2, nb:nb + 1]).then_inc(s["exp_done"], 1)

                    def copy_transposed(u):
                        n = len(pieces(u))
                        act.wait_ge(s["transposed"], u + 1)
                        if u >= 2:
                            act.wait_ge(s["summed"], u - 1)
                        m = min(n, 4)
                        ins = nc.scalar.activation(PT[:, u % 2, 0:m * P], ps[:, 4, 0:m * P], ACT.Copy)
                        if n > 4:
                            ins = nc.scalar.activation(PT[:, u % 2, 4 * P:5 * P], ps[:, 5, 0:P], ACT.Copy)
                        ins.then_inc(s["pt_copied"], 1)

                    def copy_output(u):
                        h, t = units[u]
                        lo = 64 * (h % 2)
                        act.wait_ge(s["summed"], u + 1)
                        nc.scalar.activation(out(h)[lo:lo + 64, t * P:(t + 1) * P], ps[lo:lo + 64, 6 + u % 2, 0:P],
                                             ACT.Copy).then_inc(s["o_copied"], 1)
                    exps(0)
                    for u in range(N):
                        if u + 1 < N:
                            exps(u + 1)
                        copy_transposed(u)
                        if u >= 1:
                            copy_output(u - 1)
                    copy_output(N - 1)

    def hybrid_mixer(self):
        nc, ring, ps, H = self.nc, self.ring, self.ps, self.H
        base = ring.chunks
        GAC = 3
        with ExitStack() as ctx:
            C = self.sb(ctx, "latents", [P, 4, SEQ])
            GR = self.sb(ctx, "gla_gate", [P, 4, SEQ])
            GQ = self.sb(ctx, "gla_q", [P, 4, SEQ])
            GK = self.sb(ctx, "gla_k", [P, 2, SEQ])
            GV = self.sb(ctx, "gla_v", [P, 2, 512])
            LA = self.sb(ctx, "gla_log_a", [P, 2, SEQ])
            uq = self.sb(ctx, "w_uq", [P, 2, D])
            uk = self.sb(ctx, "w_uk", [P, D])
            uv = self.sb(ctx, "w_uv", [P, 512])
            a2 = self.sb(ctx, "w_a2", [P, SEQ])
            ba = self.sb(ctx, "gla_bias", [P, SEQ])
            mag = self.sb(ctx, "gla_mag", [P, 2, SEQ])
            low = self.sb(ctx, "gla_low", [P, 2, SEQ])
            with stage(nc, "loaded act_read dve_read a_sum link prep") as (block, s):
                areas = "BABA"

                @block.sync
                def _(sp):
                    for dst, name in ((uq[:].rearrange("p k n -> p (k n)"), "w_uq"), (uk[:], "w_uk"), (uv[:], "w_uv"), (a2[:], "w_a2")):
                        sp.dma_start(dst, self.d[name]).then_inc(s["loaded"], 16)
                    sp.dma_start(ba[:], self.d["gla_ba"].partition_broadcast(P)).then_inc(s["loaded"], 16)
                    for i, area in enumerate(areas):
                        ring.load(sp, area, base + (4 * (i + 1) if i < 3 else 14))

                @block.tensor
                def _(pe):
                    for i in range(2):
                        self.panel_products(pe, None, areas[i], KD, 512, lambda k: H[:, k, 0:SEQ], 4 * i, range(8), SEQ, lambda n: None)
                    for i in (2, 3):
                        area = areas[i]
                        ring.arrived(pe, area)
                        if i == 2:
                            for m in range(2):
                                pe.wait_ge(s["dve_read"], m + 1)
                                for k in range(KD):
                                    last = nc.tensor.matmul(ps[:, m, 0:SEQ], ring.buf[area][:, k * 512 + m * P:k * 512 + (m + 1) * P],
                                                            H[:, k, 0:SEQ], start=(k == 0), stop=(k == KD - 1))
                                last.then_inc(ring.chunk_done, 1)
                        cols = slice(SEQ, 512) if i == 2 else slice(0, 512)
                        for t in range(2):
                            bank = 2 + t if i == 2 else 4 + t
                            if i == 2:
                                pe.wait_ge(s["dve_read"], 3 + t)
                            else:
                                pe.wait_ge(s["act_read"], t + 1)
                            for k in range(KD):
                                last = nc.tensor.matmul(ps[:, bank, 0:cols.stop - cols.start], H[:, k, t * P:(t + 1) * P],
                                                        ring.buf[area][:, k * 512 + cols.start:k * 512 + cols.stop],
                                                        start=(k == 0), stop=(k == KD - 1))
                            last.then_inc(ring.chunk_done, 1)
                    pe.wait_ge(s["loaded"], 80)
                    pe.wait_ge(s["dve_read"], 4)
                    pe.wait_ge(s["act_read"], 4)
                    for t in range(2):
                        last = nc.tensor.matmul(ps[:, 6, t * SEQ:(t + 1) * SEQ], C[:, GAC, t * P:(t + 1) * P], a2[:], start=True, stop=True)
                    last.then_inc(s["a_sum"], 1)

                @block.scalar
                def _(act):
                    for m in range(4):
                        act.wait_ge(ring.chunk_done, base + 5 + m)
                        nc.scalar.activation(GR[:, m, :], ps[:, 4 + m, 0:SEQ], ACT.Silu).then_inc(s["act_read"], 1)
                    act.wait_ge(s["prep"], 1)
                    nc.scalar.activation(mag[:], mag[:], ACT.Exp).then_inc(s["prep"], 1)
                    act.wait_ge(s["prep"], 2)
                    nc.scalar.activation(mag[:], mag[:], ACT.Ln, bias=1.0).then_inc(s["prep"], 1)

                @block.vector
                def _(dve):
                    link = chain(dve, s["link"])
                    V = nc.vector
                    for m in range(4):
                        dve.wait_ge(ring.chunk_done, base + m + 1)
                        V.tensor_copy(C[:, m, :], ps[:, m, 0:SEQ]).then_inc(s["dve_read"], 1)
                    for m in range(2):
                        dve.wait_ge(ring.chunk_done, base + 9 + m)
                        for half in range(2):
                            V.tensor_scalar(GQ[:, 2 * m + half, :], ps[:, m, 0:SEQ], self.c("half", 1, off=half), 0.125,
                                            ALU.mult, ALU.mult).then_inc(s["dve_read"], 1)
                    for t in range(2):
                        dve.wait_ge(ring.chunk_done, base + 11 + t)
                        V.tensor_copy(GK[:, t, :], ps[:, 2 + t, 0:SEQ]).then_inc(s["dve_read"], 1)
                    for t in range(2):
                        dve.wait_ge(ring.chunk_done, base + 13 + t)
                        V.tensor_copy(GV[:, t, :], ps[:, 4 + t, :]).then_inc(s["dve_read"], 1)
                    dve.wait_ge(s["loaded"], 80)
                    dve.wait_ge(s["a_sum"], 1)
                    link(V.tensor_tensor(LA[:], ps[:, 6, :].rearrange("p (t n) -> p t n", t=2),
                                         ba[:].unsqueeze(1).to_broadcast([P, 2, SEQ]), ALU.add))
                    link(V.tensor_scalar(low[:], LA[:], 0.0, None, ALU.min))
                    V.scalar_tensor_tensor(out=mag[:], in0=low[:], scalar=2.0, in1=LA[:], op0=ALU.mult,
                                           op1=ALU.subtract).then_inc(s["prep"], 1)
                    dve.wait_ge(s["prep"], 3)
                    link(V.tensor_tensor(LA[:], low[:], mag[:], ALU.subtract))
                    link(V.tensor_scalar(LA[:], LA[:], 1.0 / 16.0, None, ALU.mult))
            ring.chunks += 14

            with ExitStack() as gla:
                spec = dict(units=[(h, 0) for h in range(4)], lf=lambda u, t: LA[:, t, (u // 2) * P:(u // 2 + 1) * P],
                            kt=lambda u, t: GK[:, t, (u // 2) * P:(u // 2 + 1) * P],
                            kall=lambda u: GK[:, 0:2, (u // 2) * P:(u // 2 + 1) * P],
                            q=lambda u: GQ[:, u, :], v=lambda u, t: GV[:, t, u * P:(u + 1) * P],
                            v2=lambda u: GV[:, 0:2, u * P:(u + 1) * P], mids=(63, 0), out=lambda u: H[:, 4 + u, 0:SEQ], context=False)
                self.recurrence(**spec)
            self.head_norm_gate(lambda j: H[:, 4 + 2 * j:6 + 2 * j, 0:SEQ], 2, self.v("gla_g"), lambda j: GR[:, 2 * j:2 * j + 2, :])

            cq = lambda k, t: C[:, k, t]
            self.rms_norm(cq, cq, 2, SEQ, lambda k, c: self.v("q_norm", k))
            ckv = lambda k, t: C[:, 2, t]
            self.rms_norm(ckv, ckv, 1, SEQ, lambda k, c: self.v("kv_norm"))
            Q = self.sb(ctx, "mla_q", [P, 8, SEQ])
            K = self.sb(ctx, "mla_k", [P, 8, SEQ])
            V_ = self.sb(ctx, "mla_v", [P, 2, 512])
            KR = self.sb(ctx, "mla_k_rot", [P, 1, SEQ])
            cos = self.sb(ctx, "cos", [P, SEQ])
            sin = self.sb(ctx, "sin", [P, SEQ])
            with stage(nc, "products act_read dve_read kr_done") as (block, s):
                @block.tensor
                def _(pe):
                    for h in range(8):
                        for j in range(2):
                            bank = 2 * (h % 2) + j
                            if h >= 2:
                                pe.wait_ge(s["act_read"] if j == 0 else s["dve_read"], h - 1)
                            if j == 0:
                                for k in range(2):
                                    last = nc.tensor.matmul(ps[:, bank, 0:SEQ], uq[:, k, h * P:(h + 1) * P], C[:, k, :],
                                                            start=(k == 0), stop=(k == 1))
                            else:
                                last = nc.tensor.matmul(ps[:, bank, 0:SEQ], uk[:, h * P:(h + 1) * P], C[:, 2, :], start=True, stop=True)
                            last.then_inc(s["products"], 1)
                    for t in range(2):
                        nc.tensor.matmul(ps[:, 4 + t, :], C[:, 2, t * P:(t + 1) * P], uv[:], start=True, stop=True).then_inc(s["products"], 1)

                @block.scalar
                def _(act):
                    for h in range(8):
                        act.wait_ge(s["products"], 2 * h + 1)
                        nc.scalar.activation(Q[:, h, :], ps[:, 2 * (h % 2), 0:SEQ], ACT.Copy).then_inc(s["act_read"], 1)

                @block.vector
                def _(dve):
                    nc.vector.tensor_scalar(KR[:, 0, :], C[:, GAC, :], self.c("rot_rows", 1), None, ALU.mult).then_inc(s["kr_done"], 1)
                    for h in range(8):
                        dve.wait_ge(s["products"], 2 * h + 2)
                        nc.vector.tensor_copy(K[:, h, :], ps[:, 2 * (h % 2) + 1, 0:SEQ]).then_inc(s["dve_read"], 1)
                    for t in range(2):
                        dve.wait_ge(s["products"], 17 + t)
                        nc.vector.tensor_copy(V_[:, t, :], ps[:, 4 + t, :]).then_inc(s["dve_read"], 1)
            self.rope_tables(cos[:], sin[:], 0)
            self.rotate([Q[:, 2 * j:2 * j + 2, :] for j in range(4)] + [KR[:]], cos[:], sin[:], self.c("swap_mla"))
            with stage(nc, "added") as (block, s):
                @block.vector
                def _(dve):
                    nc.vector.tensor_tensor(K[:], K[:], KR[:].to_broadcast([P, 8, SEQ]), ALU.add).then_inc(s["added"], 1)
            self.attention(8, lambda h: Q[:, h, :], lambda h: K[:, h:h + 1, :],
                           lambda h, b, kt: V_[:, kt, h * 64:(h + 1) * 64], float(np.float32(96.0) ** np.float32(-0.5)),
                           lambda h: H[:, h // 2, 0:SEQ])
            self.out_projection("BA", KD, lambda k: H[:, k, 0:SEQ], 0, SEQ, scale=1.0)

    def sparse_mixer(self):
        nc, ring, ps, H = self.nc, self.ring, self.ps, self.H
        base = ring.chunks
        areas = "BABAB"
        NC = 15
        with ExitStack() as ctx:
            Q = self.sb(ctx, "nsa_q", [P, 16, SEQ])
            K = self.sb(ctx, "nsa_k", [P, 4, SEQ])
            V = self.sb(ctx, "nsa_v", [P, 2, 512])
            KC = self.sb(ctx, "key_cmp", [P, 4, NC])
            VC = self.sb(ctx, "value_cmp", [P, 4, 64])
            GT = self.sb(ctx, "branch_gates", [P, 2, 48])
            cos = self.sb(ctx, "cos", [P, SEQ])
            sin = self.sb(ctx, "sin", [P, SEQ])
            self.rope_tables(cos[:], sin[:], 1)
            with ExitStack() as inner:
                QR = self.sb(inner, "nsa_q_raw", [P, 8, SEQ])
                wg = self.sb(inner, "w_branch_gates", [P, KD, 48])
                W1 = self.sb(inner, "w_cmp1", [P, 2, 4096])
                W2 = self.sb(inner, "w_cmp2", [P, 2, P])
                CM = self.sb(inner, "cmp_masked", [P, 2, 4, SEQ])
                with stage(nc, "w_in act_read dve_read g_sum g_done") as (block, s):
                    def dve_count(j):
                        return j - 7 if j < 12 else 4 + 2 * (j - 11)

                    @block.sync
                    def _(sp):
                        sp.dma_start(wg[:].rearrange("p k n -> p (k n)"), self.d["nsa_g"]).then_inc(s["w_in"], 16)
                        sp.dma_start(W1[:].rearrange("p b n -> p (b n)"), self.d["cmp_w1"]).then_inc(s["w_in"], 16)
                        sp.dma_start(W2[:].rearrange("p b n -> p (b n)"), self.d["cmp_w2"]).then_inc(s["w_in"], 16)
                        for i, area in enumerate(areas):
                            ring.load(sp, area, base + (4 * (i + 1) if i < 4 else 18))
                        sp.wait_ge(s["w_in"], 48)

                    @block.tensor
                    def _(pe):
                        def free(n):
                            if 6 <= n:
                                j = n - 6
                                if j < 8:
                                    pe.wait_ge(s["act_read"], j + 1)
                                else:
                                    pe.wait_ge(s["dve_read"], dve_count(j))
                        for i in range(4):
                            self.panel_products(pe, None, areas[i], KD, 512, lambda k: H[:, k, 0:SEQ], 4 * i, range(6), SEQ, free)
                        area = areas[4]
                        ring.arrived(pe, area)
                        for t in range(2):
                            free(16 + t)
                            for k in range(KD):
                                last = nc.tensor.matmul(ps[:, (16 + t) % 6, :], H[:, k, t * P:(t + 1) * P],
                                                        ring.buf[area][:, k * 512:(k + 1) * 512], start=(k == 0), stop=(k == KD - 1))
                            last.then_inc(ring.chunk_done, 1)
                        pe.wait_ge(s["w_in"], 48)
                        for t in range(2):
                            for k in range(KD):
                                last = nc.tensor.matmul(ps[:, 6, 48 * t:48 * t + 48], H[:, k, t * P:(t + 1) * P], wg[:, k, :],
                                                        start=(k == 0), stop=(k == KD - 1))
                        last.then_inc(s["g_sum"], 1)

                    @block.scalar
                    def _(act):
                        for n in range(8):
                            act.wait_ge(ring.chunk_done, base + n + 1)
                            nc.scalar.activation(QR[:, n, :], ps[:, n % 6, 0:SEQ], ACT.Copy).then_inc(s["act_read"], 1)
                        act.wait_ge(s["g_sum"], 1)
                        nc.scalar.activation(GT[:].rearrange("p t n -> p (t n)"), ps[:, 6, 0:96], ACT.Sigmoid).then_inc(s["g_done"], 1)

                    @block.vector
                    def _(dve):
                        for n in range(8, 16):
                            dve.wait_ge(ring.chunk_done, base + n + 1)
                            if n < 12:
                                branch, pair = divmod(n - 8, 2)
                                nc.vector.tensor_copy(K[:, 2 * pair + branch, :], ps[:, n % 6, 0:SEQ]).then_inc(s["dve_read"], 1)
                            else:
                                kv, pair = divmod(n - 12, 2)
                                for half in range(2):
                                    nc.vector.tensor_scalar(CM[:, kv, 2 * pair + half, :], ps[:, n % 6, 0:SEQ],
                                                            self.c("half", 1, off=half), None, ALU.mult).then_inc(s["dve_read"], 1)
                        for t in range(2):
                            dve.wait_ge(ring.chunk_done, base + 17 + t)
                            nc.vector.tensor_copy(V[:, t, :], ps[:, (16 + t) % 6, :]).then_inc(s["dve_read"], 1)
                ring.chunks += 18
                self.rotate([QR[:, 2 * j:2 * j + 2, :] for j in range(4)] + [K[:, 2 * j:2 * j + 2, :] for j in range(2)],
                            cos[:], sin[:], self.c("swap_nsa"))

                FL = self.sb(inner, "windows", [P, 2, 4, NC, 32])
                hid = self.sb(inner, "cmp_hidden", [P, 2, 4 * NC])
                kraw = self.sb(inner, "cmp_key_raw", [P, 4 * NC])
                part = self.sb(inner, "cmp_key_part", [P, 4 * NC])
                with stage(nc, "windows hidden silu_done k_sum v_sum k_copied swapped link q_masked vc_zero") as (block, s):
                    @block.vector
                    def _(dve):
                        link = chain(dve, s["link"])
                        nc.vector.memset(VC[:], 0.0).then_inc(s["vc_zero"], 1)
                        for kv in range(2):
                            pe_ = self.v(("pos_k", "pos_v")[kv], 0, 32)
                            for g in range(4):
                                x = CM[:, kv, g, :].rearrange("p (m r) -> p m r", r=16)
                                for part_ in range(2):
                                    pos = pe_[:, 16 * part_:16 * part_ + 16].unsqueeze(1).to_broadcast([P, NC, 16])
                                    o = FL[:, kv, g, :, 16 * part_:16 * part_ + 16]
                                    nc.vector.scalar_tensor_tensor(out=o, in0=pos, scalar=self.c("half", 1, off=g % 2),
                                                                   in1=x[:, part_:part_ + NC, :], op0=ALU.mult,
                                                                   op1=ALU.add).then_inc(s["windows"], 1)
                        dve.wait_ge(s["k_sum"], 1)
                        nc.vector.tensor_copy(kraw[:], ps[:, 2, 0:4 * NC]).then_inc(s["k_copied"], 1)
                        dve.wait_ge(s["swapped"], 1)
                        ends = lambda t: t.rearrange("p (m r) -> p m r", r=16)[:, 1:16, 15].unsqueeze(1).to_broadcast([P, 4, NC])
                        as_gn = lambda t: t.rearrange("p (g n) -> p g n", g=4)
                        link(nc.vector.tensor_tensor(as_gn(part[:]), as_gn(ps[:, 4, 0:4 * NC]), ends(sin[:]), ALU.mult))
                        dve.wait_ge(s["k_copied"], 1)
                        link(nc.vector.tensor_tensor(KC[:], as_gn(kraw[:]), ends(cos[:]), ALU.mult))
                        link(nc.vector.tensor_tensor(KC[:], KC[:], as_gn(part[:]), ALU.add))
                        dve.wait_ge(s["v_sum"], 1)
                        dve.wait_ge(s["vc_zero"], 1)
                        nc.vector.tensor_copy(VC[0:NC, :, :], ps[0:NC, 3, 0:256].rearrange("p (g n) -> p g n", g=4)).then_inc(s["k_copied"], 1)

                    @block.tensor
                    def _(pe):
                        for kv in range(2):
                            pe.wait_ge(s["windows"], 8 * (kv + 1))
                            for pos in range(32):
                                last = nc.tensor.matmul(ps[:, kv, 0:4 * NC], W1[:, kv, pos * P:(pos + 1) * P],
                                                        FL[:, kv, :, :, pos].rearrange("p g n -> p (g n)"), start=(pos == 0), stop=(pos == 31))
                            last.then_inc(s["hidden"], 1)
                        pe.wait_ge(s["silu_done"], 1)
                        nc.tensor.matmul(ps[:, 2, 0:4 * NC], W2[:, 0, :], hid[:, 0, :], start=True, stop=True).then_inc(s["k_sum"], 1)
                        pe.wait_ge(s["silu_done"], 2)
                        for g in range(4):
                            last = nc.tensor.matmul(ps[0:NC, 3, g * 64:(g + 1) * 64], hid[:, 1, g * NC:(g + 1) * NC], W2[:, 1, 0:64],
                                                    start=True, stop=True)
                        last.then_inc(s["v_sum"], 1)
                        pe.wait_ge(s["k_copied"], 1)
                        nc.tensor.matmul(ps[:, 4, 0:4 * NC], self.c("swap_nsa"), kraw[:], start=True, stop=True).then_inc(s["swapped"], 1)

                    @block.scalar
                    def _(act):
                        for kv in range(2):
                            act.wait_ge(s["hidden"], kv + 1)
                            nc.scalar.activation(hid[:, kv, :], ps[:, kv, 0:4 * NC], ACT.Silu).then_inc(s["silu_done"], 1)

                    @block.gpsimd
                    def _(pool):
                        for h in range(16):
                            g = h // 4
                            nc.gpsimd.tensor_scalar(Q[:, h, :], QR[:, (g // 2) * 4 + h % 4, :], self.c("half", 1, off=g % 2), None,
                                                    ALU.mult).then_inc(s["q_masked"], 1)
            self.attention(16, lambda h: Q[:, h, :], lambda h: K[:, 2 * (h // 8):2 * (h // 8) + 2, :],
                           lambda h, b, kt: V[:, kt, b * SEQ + (h // 4) * 64:b * SEQ + (h // 4 + 1) * 64], 0.125,
                           lambda h: H[:, h // 2, 0:SEQ],
                           compressed=(lambda h: KC[:, h // 4, :], lambda h: VC[:, h // 4, :]),
                           weights=lambda h, t: GT[:, t, 3 * h:3 * h + 3])
            self.out_projection("AB", KD, lambda k: H[:, k, 0:SEQ], 1, SEQ, scale=1.0)

    def finish(self):
        nc = self.nc
        self.rms_norm(self.x_chunk, self.h_chunk, KD, SEQ, lambda k, c: self.v("final_g2", k))
        with stage(nc, "stored") as (block, s):
            @block.sync
            def _(sp):
                sp.dma_start(self.out.rearrange("p (k t) -> p k t", k=KD), self.H[:, :, 0:SEQ]).then_inc(s["stored"], 16)
                sp.wait_ge(s["stored"], 16)

    def dump(self):
        with stage(self.nc, "stored") as (block, s):
            @block.sync
            def _(sp):
                sp.dma_start(self.out, self.X[:].rearrange("p k t -> p (k t)")).then_inc(s["stored"], 16)
                sp.wait_ge(s["stored"], 16)


def pack_panels(w, cols):
    k, n = w.shape
    return np.ascontiguousarray(w.reshape(k // P, P, n // cols, cols).transpose(2, 1, 0, 3)).reshape(n // cols, P, -1)


def cols_of(v):
    v = np.ascontiguousarray(v).reshape(-1, P)
    return v.T


def constants():
    c = np.zeros((P, NCONST), np.float32)
    i = np.arange(P)

    def put(name, a):
        c[:a.shape[0], CCOL[name]:CCOL[name] + a.shape[1]] = a
    blk = (i[:, None] // 64) == (i[None, :] // 64)
    put("ident", np.eye(P))
    put("ones", np.ones((P, P)))
    put("upper", i[:, None] <= i[None, :])
    put("lower", i[:, None] >= i[None, :])
    put("up64", (i[:, None] <= i[None, :]) & blk)
    put("lo64", (i[:, None] >= i[None, :]) & blk)
    put("xup64", (i[:, None] < i[None, :]) & blk)
    put("xlo64", (i[:, None] > i[None, :]) & blk)
    put("upper_x", i[:, None] < i[None, :])
    put("lower_x", i[:, None] > i[None, :])
    j = np.arange(4)
    put("tie", np.tile((j[None, :] < j[:, None]).reshape(1, 16), (P, 1)))
    put("half", np.stack([i < 64, i >= 64], 1))
    theta = np.float32(10000.0)
    freq = lambda n: np.power(theta, -np.arange(n, dtype=np.float32) * np.float32(1.0 / n)).astype(np.float32)
    rot = (i >= 64) & (i < 96)
    f = np.zeros((P, 2), np.float32)
    f[rot, 0] = np.tile(freq(16), 2)
    f[:, 1] = np.tile(freq(32), 4)
    put("ropef", f)
    put("rot_rows", rot[:, None])
    for name, starts, half in (("swap_mla", (64,), 16), ("swap_nsa", (0, 64), 32)):
        s = np.zeros((P, P), np.float32)
        for at in starts:
            for m in range(half):
                s[at + m + half, at + m] = -1.0
                s[at + m, at + m + half] = 1.0
        put(name, s)
    tri = np.where(i[None, :] <= i[:, None], 0.0, -1e30)
    put("causal_add", np.concatenate([np.zeros((P, P)), tri], 1))
    n = np.arange(16)
    seen = np.concatenate([(16 * n[None, :] + 31 <= i[:, None] + P * t) & (n < 15)[None, :] for t in range(2)], 1)
    put("cmp_mask", seen)
    put("cmp_add", np.where(seen, 0.0, -1e30))
    return c


def arrays_of(x):
    a = {}
    tok = lambda v: np.ascontiguousarray(np.asarray(v)[0].T.reshape(KD, P, SEQ).transpose(1, 0, 2))
    a["x"] = np.concatenate([tok(x["x"]), tok(x["ctx"])], 2).reshape(P, KD * TT)
    a["constants"] = constants()
    vec = {
        "norm_mix": x["norm_mix_g"], "norm_ffn": x["norm_ffn_g"], "mod_b": x["mod_b"], "conv_b": x["ssd_conv_b"],
        "conv_w": x["ssd_conv_w"], "d_skip": np.repeat(np.asarray(x["ssd_d"])[0], 64), "ssd_g": x["ssd_norm_g"],
        "cf_w": x["cf_dw_w"], "cf_b": x["cf_dw_b"], "cf_lng": x["cf_ln_g"], "cf_lnb": x["cf_ln_b"],
        "hg_lb": x["hg_lb"], "hg_g": x["hg_norm_g"], "final_g": x["final_norm_g"], "ffn_norm2": x["ffn_norm_2"],
        "mix_norm2": x["mix_norm_2"], "q_norm": x["mla_q_norm_2"], "kv_norm": x["mla_kv_norm_2"],
        "gla_g": x["gla_out_norm_2"], "final_g2": x["final_norm_2"],
        "cond": np.stack([np.asarray(x["c"])[0], np.asarray(x["c_ctx"])], 1).reshape(KD, P, 2).transpose(0, 2, 1),
    }
    v = np.zeros((P, NV), np.float32)
    for name, value in vec.items():
        c = cols_of(np.asarray(value))
        if name == "cond":
            c = c.reshape(P, KD * 2)
        v[:, VCOL[name]:VCOL[name] + c.shape[1]] = c
    for name, key in (("pos_k", "nsa_pos_k_2"), ("pos_v", "nsa_pos_v_2")):
        v[:, VCOL[name]:VCOL[name] + 32] = np.tile(np.asarray(x[key])[0].T, (2, 1))
    v[:64, VCOL["gla_ba"]:VCOL["gla_ba"] + 4] = np.asarray(x["gla_b_a_2"])[0].reshape(4, 64).T
    a["vectors"] = v
    w = np.asarray(x["mod_w"])
    a["mod_w"] = np.concatenate([pack_panels(w[i], 512) for i in range(2)])
    w = np.asarray(x["ab_w_in"])[0]
    vg = np.concatenate([w[:, 3104:4128].reshape(D, 4, 1, 256), w[:, 4128:5152].reshape(D, 4, 1, 256)], 2).reshape(D, 2048)
    a["ab_in"] = pack_panels(np.concatenate([w[:, :3072], vg], 1), 512)
    a["w_dt"] = np.ascontiguousarray(w[:, 3072:3104].reshape(KD, P, 32).transpose(1, 0, 2)).reshape(P, KD * 32)
    a["ssd_rows"] = np.concatenate([np.asarray(x["ssd_dt_bias"])[0].reshape(-1), np.asarray(x["ssd_a_log"])[0].reshape(-1)])
    a["ab_out"] = pack_panels(np.asarray(x["ab_w_out"])[0], 256)
    a["router_w"] = np.ascontiguousarray(np.asarray(x["router_w"]).reshape(KD, P, 16).transpose(1, 0, 2)).reshape(P, KD * 16)
    a["router_b"] = np.asarray(x["router_b"])
    packs = lambda w, cols: np.ascontiguousarray(
        w.reshape(-1, w.shape[-2] // P, P, w.shape[-1]).transpose(0, 2, 1, 3)).reshape(-1, P, w.shape[-2] // P * w.shape[-1])
    a["moe_gate"] = packs(np.asarray(x["moe_w_gate"]), 512)
    a["moe_up"] = packs(np.asarray(x["moe_w_up"]), 512)
    a["moe_down"] = packs(np.asarray(x["moe_w_down"]).reshape(64, 256, D), D)
    a["lb_rows"] = np.asarray(x["hg_lb"]).reshape(-1)
    a["hg_in"] = pack_panels(np.asarray(x["hg_w_in"])[0], 512)
    a["hg_out"] = pack_panels(np.asarray(x["hg_w_out"])[0], 512)
    g = np.asarray(x["ffn_w_gate_2"]).reshape(4, KD, P, 11, 1, 256)
    u = np.asarray(x["ffn_w_up_2"]).reshape(4, KD, P, 11, 1, 256)
    a["ffn_gu"] = np.concatenate([g, u], 4).transpose(0, 3, 2, 1, 4, 5).reshape(44, P, 4096)
    a["ffn_down"] = packs(np.asarray(x["ffn_w_down_2"]).reshape(44, 256, D), D)
    w = np.asarray(x["hy_w_in_2"])[0]
    pad = lambda n: np.zeros((D, n), np.float32)
    a["hy_in"] = pack_panels(np.concatenate(
        [w[:, :384], w[:, 1440:1456], pad(48), w[:, 384:416], pad(32), w[:, 1456:1968], w[:, 416:928], w[:, 928:1440]], 1), 512)
    a["hy_out"] = pack_panels(np.asarray(x["hy_w_out_2"])[0], 512)
    w = np.asarray(x["mla_w_uq_2"])[0].reshape(2, P, 8, 96)
    a["w_uq"] = np.concatenate([w, np.zeros((2, P, 8, 32), np.float32)], 3).transpose(1, 0, 2, 3).reshape(P, 2048)
    w = np.asarray(x["mla_w_ukv_2"])[0].reshape(P, 8, 2, 64)
    a["w_uk"] = np.concatenate([w[:, :, 0], np.zeros((P, 8, 64), np.float32)], 2).reshape(P, D)
    a["w_uv"] = np.ascontiguousarray(w[:, :, 1]).reshape(P, 512)
    a["w_a2"] = np.concatenate([np.asarray(x["gla_w_a2_2"])[0], np.zeros((P - 16, SEQ), np.float32)], 0)
    a["gla_ba"] = np.asarray(x["gla_b_a_2"]).reshape(-1)
    a["positions"] = np.asarray(x["positions_2"])[0]
    w1 = [np.asarray(x[n])[0].reshape(32, 64, P).transpose(1, 0, 2).reshape(64, 4096) for n in ("nsa_ck_w1_2", "nsa_cv_w1_2")]
    a["cmp_w1"] = np.concatenate([np.concatenate([w, w], 0) for w in w1], 1)
    w2 = [np.asarray(x[n])[0] for n in ("nsa_ck_w2_2", "nsa_cv_w2_2")]
    a["cmp_w2"] = np.concatenate([np.concatenate([w, w], 1) for w in w2], 1)
    w = np.asarray(x["nsa_w_in_2"])[0]
    wq = w[:, :1024].reshape(D, 2, 2, 4, 64).transpose(0, 1, 3, 2, 4).reshape(D, 1024)
    a["nsa_in"] = pack_panels(np.concatenate(
        [wq, w[:, 1536:1792], w[:, 2048:2304], w[:, 1024:1536], w[:, 1792:2048], w[:, 2304:2560]], 1), 512)
    a["nsa_g"] = np.ascontiguousarray(w[:, 2560:2608].reshape(D, 16, 3)[:, :, [1, 2, 0]].reshape(KD, P, 48).transpose(1, 0, 2)).reshape(P, KD * 48)
    a["nsa_out"] = pack_panels(np.asarray(x["nsa_w_out_2"])[0], 512)
    return a


def build(nc, d, out, stages=None):
    with ExitStack() as ctx:
        p = Program(nc, ctx, d, out)
        p.plan()
        everything(p, stages)


def everything(p, stop=None):
    p.load_inputs()
    p.modulation()
    x, h = p.x_chunk, p.h_chunk
    p.rms_norm(x, h, KD, TT, lambda k, c: p.scale_mod[:, 0, k, c:c + 1], lambda k, c: p.m(0, 0, k, c))
    p.even_mixer()
    if stop == "mix0":
        return p.dump()
    p.rms_norm(x, h, KD, TT, lambda k, c: p.scale_mod[:, 1, k, c:c + 1], lambda k, c: p.m(0, 3, k, c))
    p.experts(0, TT)
    if stop == "moe0":
        return p.dump()
    p.rms_norm(x, h, KD, TT, lambda k, c: p.scale_mod[:, 2, k, c:c + 1], lambda k, c: p.m(1, 0, k, c), permuted=True)
    p.odd_mixer()
    if stop == "mix1":
        return p.dump()
    p.rms_norm(x, h, KD, SEQ, lambda k, c: p.scale_mod[:, 3, k, c:c + 1], lambda k, c: p.m(1, 3, k, c))
    p.experts(1, SEQ)
    if stop == "moe1":
        return p.dump()
    p.rms_norm(x, x, KD, SEQ, lambda k, c: p.v("final_g", k))
    p.feed_forward(0)
    if stop == "f0a":
        return p.dump()
    p.rms_norm(x, h, KD, SEQ, lambda k, c: p.v("mix_norm2", k))
    p.hybrid_mixer()
    if stop == "m0":
        return p.dump()
    p.feed_forward(1)
    p.feed_forward(2)
    if stop == "f1a":
        return p.dump()
    p.rms_norm(x, h, KD, SEQ, lambda k, c: p.v("mix_norm2", 8 + k))
    p.sparse_mixer()
    if stop == "m1":
        return p.dump()
    p.feed_forward(3)
    p.finish()


def kernel(**inputs):
    import concourse.bacc as _bacc
    from concourse.bass_utils import run_bass_kernel_spmd as _run

    nc = _bacc.Bacc("TRN2", target_bir_lowering=False, num_devices=1)
    arrays = {f"in_{k}": np.ascontiguousarray(v) for k, v in arrays_of(inputs).items()}
    d = {k[3:]: nc.dram_tensor(k, v.shape, mybir.dt.from_np(v.dtype), kind="ExternalInput").ap() for k, v in arrays.items()}
    out = nc.dram_tensor("out", (P, KD * SEQ), F32, kind="ExternalOutput").ap()
    build(nc, d, out)
    r = _run(nc, [arrays], core_ids=[0]).results[0]["out"]
    return np.ascontiguousarray(np.asarray(r).reshape(P, KD, SEQ).transpose(2, 1, 0)).reshape(1, SEQ, D)
```

```python
from contextlib import ExitStack, contextmanager

import numpy as np

import concourse.bass as bass
from concourse import mybir

F32 = mybir.dt.float32
F32R = mybir.dt.float32r
U32 = mybir.dt.uint32
ALU = mybir.AluOpType
ACT = mybir.ActivationFunctionType
AX = mybir.AxisListType

P = 128
D = 1024
KD = D // P
SEQ = 256
TT = 2 * SEQ
NT = TT // P
EPS = 1e-6

VECTORS = [
    ("norm_mix", 16), ("norm_ffn", 16), ("mod_b", 96), ("conv_b", 16), ("conv_w", 80),
    ("d_skip", 8), ("ssd_g", 8), ("cf_w", 248), ("cf_b", 8), ("cf_lng", 8), ("cf_lnb", 8),
    ("hg_lb", 16), ("hg_g", 1), ("final_g", 8), ("ffn_norm2", 32), ("mix_norm2", 16),
    ("q_norm", 2), ("kv_norm", 1), ("gla_g", 1), ("final_g2", 8), ("cond", 16),
    ("pos_k", 32), ("pos_v", 32), ("gla_ba", 4),
]
VCOL, _n = {}, 0
for _name, _w in VECTORS:
    VCOL[_name] = _n
    _n += _w
NV = _n
ROWS = [("router_b", 64), ("dt_bias", 32), ("a_log", 32), ("pos", SEQ)]
CONSTS = [("ident", P), ("ones", P), ("upper", P), ("lower", P), ("up64", P), ("lo64", P),
          ("xup64", P), ("xlo64", P), ("upper_x", P), ("lower_x", P), ("tie", 16), ("half", 2), ("ropef", 2),
          ("swap_mla", P), ("swap_nsa", P), ("rot_rows", 1), ("causal_add", 2 * P), ("cmp_mask", 32), ("cmp_add", 32)]
CCOL, _n = {}, 0
for _name, _w in CONSTS:
    CCOL[_name] = _n
    _n += _w
NCONST = _n


TWO_PI_PARTS = [6.28125]
TWO_PI_PARTS.append(float(np.round((2 * np.pi - 6.28125) * 2 ** 21) / 2 ** 21))
TWO_PI_PARTS.append(float(np.float32(2 * np.pi - sum(TWO_PI_PARTS))))
PI_BELOW = float(np.nextafter(np.float32(np.pi), np.float32(0)))


class Ring:

    def __init__(self, nc, ctx):
        self.buf, self.landed, self.queue, self.sent, self.used, self.free_at = {}, {}, {}, {}, {}, {}
        for a, n in (("A", 4096), ("B", 4096), ("C", 2048), ("D", 2048)):
            self.buf[a] = ctx.enter_context(nc.sbuf_tensor(f"weights_{a}", [P, n], F32))
            self.landed[a] = ctx.enter_context(nc.semaphore(f"weights_{a}_landed"))
            self.queue[a], self.sent[a], self.used[a] = [], 0, 0
        self.chunk_done = ctx.enter_context(nc.semaphore("pe_chunk_done"))
        self.chunks = 0

    def load(self, sp, area, after, sem=None):
        i = self.sent[area]
        if i < len(self.queue[area]):
            if after is not None:
                sp.wait_ge(self.chunk_done if sem is None else sem, after)
            sp.dma_start(self.buf[area][:], self.queue[area][i]).then_inc(self.landed[area], 16)
        self.sent[area] += 1

    def arrived(self, pe, area):
        self.used[area] += 1
        pe.wait_ge(self.landed[area], 16 * self.used[area])


@contextmanager
def stage(nc, names):
    handles = {name: nc.alloc_semaphore(name=f"{name}_{nc.next_id()}") for name in names.split()}
    with nc.Block() as block:
        yield block, handles
    nc.clear_and_free_semaphores(list(handles.values()))
    nc.all_engine_barrier()


def chain(eng, sem, base=0):
    n = [0]

    def link(ins):
        n[0] += 1
        ins.then_inc(sem, 1)
        eng.wait_ge(sem, base + n[0])
        return n[0]
    return link


class Program:
    def __init__(self, nc, ctx, d, out):
        self.nc, self.ctx, self.d, self.out = nc, ctx, d, out
        sb = self.sb
        self.ring = Ring(nc, ctx)
        self.X = sb(ctx, "residual", [P, KD, TT])
        self.H = sb(ctx, "normed", [P, KD, TT])
        self.vec = sb(ctx, "vectors", [P, NV])
        self.cst = sb(ctx, "constants", [P, NCONST])
        self.mod = sb(ctx, "modulation", [P, 2 * 6 * KD, 2])
        self.scale_mod = sb(ctx, "norm_scales", [P, 4, KD, 2])
        self.ps = ctx.enter_context(nc.psum_tensor("ps", [P, 8, 512], F32))
        self.eps = sb(ctx, "eps", [P, 1])
        self.spare = sb(ctx, "spare", [P, 3])

    def sb(self, ctx, name, shape, dt=F32):
        return ctx.enter_context(self.nc.sbuf_tensor(f"{name}_{self.nc.next_id()}", shape, dt))

    def v(self, name, i=0, n=1, p=P):
        c = VCOL[name] + i
        return self.vec[0:p, c:c + n]

    def c(self, name, n=P, p=P, off=0):
        c = CCOL[name] + off
        return self.cst[0:p, c:c + n]

    def plan(self):
        q, d = self.ring.queue, self.d
        for i in range(12):
            q["A"].append(d["mod_w"][2 * i])
            q["B"].append(d["mod_w"][2 * i + 1])
        for i in range(5):
            q["A"].append(d["ab_in"][2 * i])
            q["B"].append(d["ab_in"][2 * i + 1])
        for i in range(2):
            q["A"].append(d["ab_out"][2 * i])
            q["B"].append(d["ab_out"][2 * i + 1])

        def moe(layer):
            for e in range(16):
                q["A"].append(d["moe_gate"][16 * layer + e])
                q["B"].append(d["moe_up"][16 * layer + e])
                q["C"].append(d["moe_down"][2 * (16 * layer + e)])
                q["D"].append(d["moe_down"][2 * (16 * layer + e) + 1])

        def ffn(n):
            for j in range(11):
                q["AB"[j % 2]].append(d["ffn_gu"][11 * n + j])
                q["CD"[j % 2]].append(d["ffn_down"][11 * n + j])
        moe(0)
        for i in range(5):
            q["A"].append(d["hg_in"][2 * i])
            q["B"].append(d["hg_in"][2 * i + 1])
        q["A"].append(d["hg_out"][0])
        q["B"].append(d["hg_out"][1])
        moe(1)
        ffn(0)
        for i in range(4):
            q["BA"[i % 2]].append(d["hy_in"][i])
        q["B"].append(d["hy_out"][0])
        q["A"].append(d["hy_out"][1])
        ffn(1)
        ffn(2)
        for i in range(5):
            q["BA"[i % 2]].append(d["nsa_in"][i])
        q["A"].append(d["nsa_out"][0])
        q["B"].append(d["nsa_out"][1])
        ffn(3)

    def load_inputs(self):
        nc, d = self.nc, self.d
        with stage(nc, "loaded memset") as (block, s):
            @block.sync
            def _(sp):
                for area in "ABCD":
                    self.ring.load(sp, area, None)

            @block.scalar
            def _(act):
                act.dma_start(self.vec[:], d["vectors"]).then_inc(s["loaded"], 16)
                act.dma_start(self.cst[:], d["constants"]).then_inc(s["loaded"], 16)
                act.dma_start(self.X[:].rearrange("p k t -> p (k t)"), d["x"]).then_inc(s["loaded"], 16)
                act.wait_ge(s["loaded"], 48)

            @block.vector
            def _(dve):
                nc.vector.memset(self.eps[:], EPS).then_inc(s["memset"], 1)
                dve.wait_ge(s["memset"], 1)

    def modulation(self):
        nc, ring, ps, mod = self.nc, self.ring, self.ps, self.mod
        rounds = 12
        with ExitStack() as ctx:
            cond = self.sb(ctx, "cond", [P, KD, 2])
            rows = self.sb(ctx, "modulation_rows", [2, 2, 512])
            ch = self.sb(ctx, "cond_hi", [P, KD, 2], F32R)
            cl = self.sb(ctx, "cond_lo", [P, KD, 2], F32R)
            wh = self.sb(ctx, "w_hi", [P, 4, 1024], F32R)
            wl = self.sb(ctx, "w_lo", [P, 4, 1024], F32R)
            with stage(nc, "silu_done cond_split hi_done lo_done pieces_used rows_copied turned added scaled") as (block, s):
                def before(i, half):
                    return (i, 0) if half else (i - 1, 1)

                @block.scalar
                def _(act):
                    nc.scalar.activation(cond[:], self.v("cond", 0, 16).rearrange("p (k c) -> p k c", c=2),
                                         ACT.Silu).then_inc(s["silu_done"], 1)
                    act.wait_ge(s["silu_done"], 1)
                    nc.scalar.activation(ch[:], cond[:], ACT.Copy).then_inc(s["cond_split"], 1)
                    self.credit(nc.scalar, s["rows_copied"])

                    def copy_rows(n):
                        act.wait_ge(s["pieces_used"], n[0] * 8 + 4 * n[1] + 8)
                        nc.scalar.activation(rows[:, n[1], :], ps[0:2, n[1], :], ACT.Copy).then_inc(s["rows_copied"], 1)

                    def one_round(i, first):
                        for half, area in enumerate("AB"):
                            act.wait_ge(ring.landed[area], i * 16 + 16 * (ring.used[area] + 1))
                            for p in range(4):
                                act.wait_ge(s["pieces_used"], i * 8 + 4 * half + p + 1)
                                nc.scalar.activation(wh[:, p, :], ring.buf[area][:, p * 1024:(p + 1) * 1024],
                                                     ACT.Copy).then_inc(s["hi_done"], 1)
                                if p == 1 and not (first and half == 0):
                                    copy_rows(before(i, half))
                    one_round(0, True)
                    with act.Fori(1, rounds) as i:
                        one_round(i, False)
                    copy_rows((rounds - 1, 1))

                @block.sync
                def _(sp):
                    with sp.Fori(0, rounds - 1) as i:
                        sp.wait_ge(s["lo_done"], i * 8 + 4)
                        sp.dma_start(ring.buf["A"][:], self.d["mod_w"][2 * i + 2]).then_inc(ring.landed["A"], 16)
                        sp.wait_ge(s["lo_done"], i * 8 + 8)
                        sp.dma_start(ring.buf["B"][:], self.d["mod_w"][2 * i + 3]).then_inc(ring.landed["B"], 16)
                    ring.sent["A"] += rounds - 1
                    ring.sent["B"] += rounds - 1
                    ring.load(sp, "A", 8 * rounds - 4, s["lo_done"])
                    ring.load(sp, "B", 8 * rounds, s["lo_done"])

                @block.tensor
                def _(pe):
                    pe.wait_ge(s["cond_split"], 2)

                    def turn(n):
                        pe.wait_ge(s["rows_copied"], n[0] * 2 + n[1] + 2)
                        pe.wait_ge(s["added"], n[0] * 2 + n[1] + 1)
                        for m in range(4):
                            last = nc.tensor.matmul(ps[:, 2 + n[1], 2 * m:2 * m + 2], rows[:, n[1], m * P:(m + 1) * P],
                                                    self.c("ident", 2, 2), start=True, stop=True)
                        last.then_inc(s["turned"], 1)

                    def one_round(i, first):
                        for half in range(2):
                            for p in range(4):
                                pe.wait_ge(s["lo_done"], i * 8 + 4 * half + p + 1)
                                for k in (2 * p, 2 * p + 1):
                                    cols = slice((k % 2) * 512, (k % 2 + 1) * 512)
                                    last = self.product(ps[0:2, half, :], ch[:, k, :], cl[:, k, :],
                                                        wh[:, p, cols], wl[:, p, cols], k == 0, k == KD - 1)
                                last.then_inc(s["pieces_used"], 1)
                                if p == 2 and not (first and half == 0):
                                    turn(before(i, half))
                    one_round(0, True)
                    with pe.Fori(1, rounds) as i:
                        one_round(i, False)
                    turn((rounds - 1, 1))
                    ring.used["A"] += rounds
                    ring.used["B"] += rounds

                @block.vector
                def _(dve):
                    nc.vector.memset(self.spare[:, 2:3], 0.0).then_inc(s["pieces_used"], 4)
                    self.credit(nc.vector, s["added"])
                    dve.wait_ge(s["cond_split"], 1)
                    nc.vector.tensor_tensor(cl[:], cond[:], ch[:].bitcast(F32), ALU.subtract).then_inc(s["cond_split"], 1)

                    def add_bias(n):
                        dve.wait_ge(s["turned"], n[0] * 2 + n[1] + 1)
                        panel = bass.ds(n[0] * 2 + n[1], 1)
                        bias = self.vec[:, VCOL["mod_b"]:VCOL["mod_b"] + 96].rearrange(
                            "p (i m) -> p i m", m=4)[:, panel, :].rearrange("p i m -> p (i m)")
                        out = mod[:].rearrange("p (i m) c -> p i m c", m=4)[:, panel, :, :]
                        nc.vector.tensor_tensor(
                            out.rearrange("p i m c -> p (i m) c"),
                            ps[:, 2 + n[1], 0:8].rearrange("p (m c) -> p m c", c=2),
                            bias.unsqueeze(2).to_broadcast([P, 4, 2]), ALU.add).then_inc(s["added"], 1)

                    def one_round(i, first):
                        for half, area in enumerate("AB"):
                            for p in range(4):
                                dve.wait_ge(s["hi_done"], i * 8 + 4 * half + p + 1)
                                nc.vector.tensor_tensor(wl[:, p, :], ring.buf[area][:, p * 1024:(p + 1) * 1024],
                                                        wh[:, p, :].bitcast(F32), ALU.subtract).then_inc(s["lo_done"], 1)
                            if not (first and half == 0):
                                add_bias(before(i, half))
                    one_round(0, True)
                    with dve.Fori(1, rounds) as i:
                        one_round(i, False)
                    add_bias((rounds - 1, 1))
                    dve.wait_ge(s["added"], 2 * rounds + 1)
                    m4 = mod[:].rearrange("p (l j k) c -> p l j k c", l=2, j=6)
                    for n in range(4):
                        layer, kind = n // 2, n % 2
                        g = self.v(("norm_mix", "norm_ffn")[kind], 8 * layer, 8)
                        nc.vector.scalar_tensor_tensor(
                            out=self.scale_mod[:, n, :, :], in0=m4[:, layer, 1 + 3 * kind, :, :], scalar=1.0,
                            in1=g.unsqueeze(2).to_broadcast([P, KD, 2]), op0=ALU.add, op1=ALU.mult).then_inc(s["scaled"], 1)

    def credit(self, engine, sem, column=1):
        if engine is self.nc.scalar:
            self.nc.scalar.activation(self.spare[:, 0:1], self.eps[:], ACT.Copy).then_inc(sem, 1)
        else:
            self.nc.vector.memset(self.spare[:, column:column + 1], 0.0).then_inc(sem, 1)

    def m(self, layer, kind, k, c):
        return self.mod[:, layer * 48 + kind * 8 + k, c:c + 1]

    def rms_norm(self, src, dst, chunks, tokens, scale, shift=None, permuted=False, eps=None):
        nc, ps = self.nc, self.ps
        halves = [(c, slice(c * SEQ, (c + 1) * SEQ)) for c in range(tokens // SEQ)]
        with ExitStack() as ctx:
            sq = self.sb(ctx, "squares", [P, 2, tokens])
            root = self.sb(ctx, "root", [P, tokens])
            rstd = self.sb(ctx, "rstd", [P, tokens])
            with stage(nc, "squared summed rooted inverted scaled shifted") as (block, s):
                @block.scalar
                def _(act):
                    for k in range(chunks):
                        if k >= 2:
                            act.wait_ge(s["summed"], k - 1)
                        nc.scalar.activation(sq[:, k % 2, :], src(k, slice(0, tokens)), ACT.Square).then_inc(s["squared"], 1)
                    act.wait_ge(s["summed"], chunks)
                    nc.scalar.activation(root[:], ps[:, 0, 0:tokens], ACT.Sqrt, bias=self.eps[:, 0:1],
                                         scale=1.0 / (chunks * P)).then_inc(s["rooted"], 1)
                    if shift is not None:
                        for k in range(chunks):
                            act.wait_ge(s["scaled"], (k + 1) * len(halves))
                            for c, t in halves:
                                nc.scalar.activation(dst(k, t), dst(k, t), ACT.Identity,
                                                     bias=shift(k, c)).then_inc(s["shifted"], 1)

                @block.tensor
                def _(pe):
                    for k in range(chunks):
                        pe.wait_ge(s["squared"], k + 1)
                        nc.tensor.matmul(ps[:, 0, 0:tokens], self.c("ones"), sq[:, k % 2, :],
                                         start=(k == 0), stop=(k == chunks - 1)).then_inc(s["summed"], 1)

                @block.vector
                def _(dve):
                    dve.wait_ge(s["rooted"], 1)
                    nc.vector.reciprocal(rstd[:], root[:]).then_inc(s["inverted"], 1)
                    dve.wait_ge(s["inverted"], 1)
                    for k in range(chunks):
                        for c, t in halves:
                            a, r, o = src(k, t), rstd[:, t], dst(k, t)
                            if permuted and c == 0:
                                a = a.rearrange("p (r w) -> p w r", w=64)
                                r = r.rearrange("p (r w) -> p w r", w=64)
                                o = o.rearrange("p (w r) -> p w r", w=64)
                            nc.vector.scalar_tensor_tensor(out=o, in0=a, scalar=scale(k, c), in1=r,
                                                           op0=ALU.mult, op1=ALU.mult).then_inc(s["scaled"], 1)

    def x_chunk(self, k, t):
        return self.X[:, k, t]

    def h_chunk(self, k, t):
        return self.H[:, k, t]

    def panel_products(self, pe, s_free, area, kchunks, cols, rhs, n0, banks, tokens, free):
        nc, ring = self.nc, self.ring
        ring.arrived(pe, area)
        for m in range(cols // P):
            free(n0 + m)
            for k in range(kchunks):
                last = nc.tensor.matmul(
                    self.ps[:, banks[(n0 + m) % len(banks)], 0:tokens],
                    ring.buf[area][:, k * cols + m * P:k * cols + (m + 1) * P], rhs(k),
                    start=(k == 0), stop=(k == kchunks - 1))
            last.then_inc(ring.chunk_done, 1)

    def out_projection(self, panels, kchunks, rhs, layer, tokens, permuted=False, scale=None):
        nc, ring, ps, X = self.nc, self.ring, self.ps, self.X
        per = 4096 // kchunks // P
        SLOTS, AHEAD, PK = 4, 3, 8
        parts = kchunks // PK
        pieces = KD * parts
        base = ring.chunks
        used = {a: ring.used[a] for a in panels}
        halves = [(c, slice(c * SEQ, (c + 1) * SEQ)) for c in range(tokens // SEQ)]
        nh = len(halves)

        def raw(p):
            n, part = divmod(p, parts)
            w = ring.buf[panels[n // per]][:].rearrange("p (k n) -> p k n", k=kchunks)
            return w[:, PK * part:PK * (part + 1), (n % per) * P:(n % per + 1) * P]

        with ExitStack() as ctx:
            xh = self.sb(ctx, "x_hi", [P, kchunks, tokens], F32R)
            xl = self.sb(ctx, "x_lo", [P, kchunks, tokens], F32R)
            wh = self.sb(ctx, "w_hi", [P, SLOTS, PK * P], F32R)
            wl = self.sb(ctx, "w_lo", [P, SLOTS, PK * P], F32R)
            with stage(nc, "x_hi x_lo hi_done lo_done pieces_used added") as (block, s):
                @block.tensor
                def _(pe):
                    for p in range(pieces):
                        n, part = divmod(p, parts)
                        pe.wait_ge(s["lo_done"], p + 1)
                        if n >= 4 and part == 0:
                            pe.wait_ge(s["added"], nh * (n - 3))
                        for j in range(PK):
                            k = PK * part + j
                            if n == 0:
                                pe.wait_ge(s["x_lo"], k + 1)
                            w = slice(j * P, (j + 1) * P)
                            last = self.product(ps[:, n % 4, 0:tokens], wh[:, p % SLOTS, w], wl[:, p % SLOTS, w],
                                                xh[:, k, :], xl[:, k, :], k == 0, k == kchunks - 1)
                        last.then_inc(ring.chunk_done if part == parts - 1 else s["pieces_used"], 1)

                @block.sync
                def _(sp):
                    for i, area in enumerate(panels):
                        ring.load(sp, area, per * parts * (i + 1), s["lo_done"])

                @block.scalar
                def _(act):
                    def hi(p):
                        i, first = divmod(p, per * parts)
                        if first == 0:
                            act.wait_ge(ring.landed[panels[i]], 16 * (used[panels[i]] + panels[:i].count(panels[i]) + 1))
                        if p >= SLOTS:
                            n, part = divmod(p - SLOTS, parts)
                            if part == parts - 1:
                                act.wait_ge(ring.chunk_done, base + n + 1)
                            else:
                                act.wait_ge(s["pieces_used"], n + 1)
                        nc.scalar.activation(wh[:, p % SLOTS, :].rearrange("p (k n) -> p k n", k=PK), raw(p),
                                             ACT.Copy).then_inc(s["hi_done"], 1)

                    hi(0)
                    for k in range(kchunks):
                        nc.scalar.activation(xh[:, k, :], rhs(k), ACT.Copy).then_inc(s["x_hi"], 1)
                        if k == 7 and parts == 2:
                            hi(1)
                    for p in range(parts, pieces):
                        hi(p)

                @block.vector
                def _(dve):
                    def lo(p):
                        dve.wait_ge(s["hi_done"], p + 1)
                        nc.vector.tensor_tensor(wl[:, p % SLOTS, :].rearrange("p (k n) -> p k n", k=PK), raw(p),
                                                wh[:, p % SLOTS, :].bitcast(F32).rearrange("p (k n) -> p k n", k=PK),
                                                ALU.subtract).then_inc(s["lo_done"], 1)

                    lo(0)
                    for k in range(kchunks):
                        dve.wait_ge(s["x_hi"], k + 1)
                        nc.vector.tensor_tensor(xl[:, k, :], rhs(k), xh[:, k, :].bitcast(F32), ALU.subtract).then_inc(s["x_lo"], 1)
                        if k == 7 and parts == 2:
                            lo(1)
                    for p in range(parts, AHEAD):
                        lo(p)
                    for p in range(pieces):
                        if p + AHEAD < pieces:
                            lo(p + AHEAD)
                        m, part = divmod(p, parts)
                        for c, t in halves if part == parts - 1 else ():
                            if c == 0:
                                dve.wait_ge(ring.chunk_done, base + m + 1)
                            x, y = X[:, m, t], ps[:, m % 4, t]
                            if permuted:
                                x = x.rearrange("p (r w) -> p w r", w=64)
                                y = y.rearrange("p (w r) -> p w r", w=64)
                            sc = self.m(layer, 2, m, c) if scale is None else scale
                            nc.vector.scalar_tensor_tensor(out=x, in0=y, scalar=sc, in1=x,
                                                           op0=ALU.mult, op1=ALU.add).then_inc(s["added"], 1)
        for a in panels:
            ring.used[a] += 1
        ring.chunks += KD

    def even_in(self, Z, XBC, U, dt_tok):
        nc, ring, ps, H = self.nc, self.ring, self.ps, self.H
        base = ring.chunks
        areas = "AB" * 5
        with ExitStack() as ctx:
            sig = self.sb(ctx, "gate_sigmoid", [P, 2, TT])
            wdt = self.sb(ctx, "w_dt", [P, KD, 32])
            xh = self.sb(ctx, "x_hi", [P, KD, TT], F32R)
            xl = self.sb(ctx, "x_lo", [P, KD, TT], F32R)
            self.split_input(TT, xh, xl)
            SLOTS, AHEAD = 2, 1
            wh = self.sb(ctx, "w_hi", [P, SLOTS, 512], F32R)
            wl = self.sb(ctx, "w_lo", [P, SLOTS, 512], F32R)
            used = {a: ring.used[a] for a in "AB"}

            def raw(p):
                n, half = divmod(p, 2)
                w = ring.buf[areas[n // 4]][:].rearrange("p (k n) -> p k n", k=KD)
                return w[:, 4 * half:4 * half + 4, (n % 4) * P:(n % 4 + 1) * P]

            def hi(act, p):
                if p % 8 == 0:
                    act.wait_ge(ring.landed[areas[p // 8]], 16 * (used[areas[p // 8]] + p // 16 + 1))
                if p >= SLOTS:
                    n, half = divmod(p - SLOTS, 2)
                    act.wait_ge(s["pieces_used"] if half == 0 else ring.chunk_done, n + 1 + (base if half else 0))
                nc.scalar.activation(wh[:, p % SLOTS, :].rearrange("p (k n) -> p k n", k=4), raw(p), ACT.Copy).then_inc(s["hi_done"], 1)

            def lo(dve, p):
                dve.wait_ge(s["hi_done"], p + 1)
                nc.vector.tensor_tensor(wl[:, p % SLOTS, :].rearrange("p (k n) -> p k n", k=4), raw(p),
                                        wh[:, p % SLOTS, :].bitcast(F32).rearrange("p (k n) -> p k n", k=4),
                                        ALU.subtract).then_inc(s["lo_done"], 1)

            for a in "AB":
                ring.used[a] += 5
            with stage(nc, "hi_done lo_done pieces_used wdt_in act_read dve_read zeroed dt_sum sig_done u_done") as (block, s):
                def bank_counts(n):
                    a = v = 0
                    for j in range(n):
                        pair, what = divmod(j - 24, 4)
                        if j < 8:
                            a = j + 1
                        elif j < 24:
                            v = j - 7
                        elif what < 2:
                            v = 16 + 2 * pair + what + 1
                        else:
                            a = 8 + 2 * pair + what - 1
                    return a, v

                @block.tensor
                def _(pe):
                    def free(n):
                        if n >= 6:
                            a, v = bank_counts(n - 5)
                            pe.wait_ge(s["act_read"], a) if a else None
                            pe.wait_ge(s["dve_read"], v) if v else None
                    for n in range(40):
                        free(n)
                        for half in range(2):
                            p = 2 * n + half
                            pe.wait_ge(s["lo_done"], p + 1)
                            for j in range(4):
                                k, cols = 4 * half + j, slice(j * P, (j + 1) * P)
                                last = self.product(ps[:, n % 6, :], wh[:, p % SLOTS, cols], wl[:, p % SLOTS, cols],
                                                    xh[:, k, :], xl[:, k, :], k == 0, k == KD - 1)
                            last.then_inc(s["pieces_used"] if half == 0 else ring.chunk_done, 1)
                    pe.wait_ge(s["wdt_in"], 16)
                    for t in range(NT):
                        for k in range(KD):
                            last = nc.tensor.matmul(ps[:, 6, 32 * t:32 * t + 32], H[:, k, t * P:(t + 1) * P],
                                                    wdt[:, k, :], start=(k == 0), stop=(k == KD - 1))
                    last.then_inc(s["dt_sum"], 1)

                @block.sync
                def _(sp):
                    sp.dma_start(wdt[:].rearrange("p k n -> p (k n)"), self.d["w_dt"]).then_inc(s["wdt_in"], 16)
                    for i, area in enumerate(areas):
                        ring.load(sp, area, 8 * (i + 1), s["lo_done"])

                @block.scalar
                def _(act):
                    for p in range(AHEAD):
                        hi(act, p)
                    g = 0
                    for n in range(40):
                        for p in (2 * n + AHEAD, 2 * n + AHEAD + 1):
                            if p < 80:
                                hi(act, p)
                        if n < 8:
                            act.wait_ge(ring.chunk_done, base + n + 1)
                            nc.scalar.activation(Z[:, n, :], ps[:, n % 6, :], ACT.Silu).then_inc(s["act_read"], 1)
                        if n >= 24 and (n - 24) % 4 >= 2:
                            act.wait_ge(ring.chunk_done, base + n + 1)
                            if g >= 2:
                                act.wait_ge(s["dve_read"], 16 + g - 1)
                            nc.scalar.activation(sig[:, g % 2, :], ps[:, n % 6, :], ACT.Sigmoid).then_inc(s["act_read"], 1)
                            g += 1

                @block.gpsimd
                def _(pool):
                    nc.gpsimd.memset(XBC[:], 0.0).then_inc(s["zeroed"], 1)
                    nc.gpsimd.memset(U[:], 0.0).then_inc(s["zeroed"], 1)

                @block.vector
                def _(dve):
                    for p in range(AHEAD):
                        lo(dve, p)
                    dve.wait_ge(s["zeroed"], 2)
                    g = 0
                    for n in range(40):
                        for p in (2 * n + AHEAD, 2 * n + AHEAD + 1):
                            if p < 80:
                                lo(dve, p)
                        if 8 <= n < 24:
                            dve.wait_ge(ring.chunk_done, base + n + 1)
                            nc.vector.tensor_copy(XBC[:, n - 8, :, 2:2 + SEQ],
                                                  ps[:, n % 6, :].rearrange("p (s t) -> p s t", s=2)).then_inc(s["dve_read"], 1)
                        if n >= 24 and (n - 24) % 4 >= 2:
                            dve.wait_ge(s["act_read"], 8 + g + 1)
                            vps = ps[:, (n - 2) % 6, :]
                            ulat = U[:, g, 0:376].rearrange("p (r w) -> p r w", w=94)[:, :, 15:79]
                            nc.vector.tensor_tensor(ulat, vps[:, 0:SEQ].rearrange("p (r w) -> p r w", w=64),
                                                    sig[:, g % 2, 0:SEQ].rearrange("p (r w) -> p r w", w=64),
                                                    ALU.mult).then_inc(s["u_done"], 1)
                            nc.vector.tensor_tensor(U[:, g, 391:391 + SEQ], vps[:, SEQ:TT], sig[:, g % 2, SEQ:TT],
                                                    ALU.mult).then_inc(s["dve_read"], 1)
                            g += 1
                    dve.wait_ge(s["dt_sum"], 1)
                    nc.vector.tensor_copy(dt_tok[:].rearrange("p t n -> p (t n)"), ps[:, 6, 0:128]).then_inc(s["u_done"], 1)
        ring.chunks += 40

    def convolutions(self, XBC, U, dt_tok, LA):
        nc, ps, H = self.nc, self.ps, self.H
        on_pe, K5, K31 = 5, 5, 31
        with ExitStack() as ctx:
            acc = self.sb(ctx, "conv_acc", [P, 2, TT])
            diag = self.sb(ctx, "tap_diagonals", [P, 8, P])
            rows = self.sb(ctx, "ssd_rows", [P, 64])
            aneg = self.sb(ctx, "a_neg", [P, 32])
            raw = self.sb(ctx, "dt_raw", [P, NT, 32])
            mag = self.sb(ctx, "dt_mag", [P, NT, 32])
            with stage(nc, "tap small xbc_out rows_in prep act_prep diag_made diag_used copied") as (block, s):
                @block.sync
                def _(sp):
                    sp.dma_start(rows[:], self.d["ssd_rows"].partition_broadcast(P)).then_inc(s["rows_in"], 16)

                def xsrc(c, tap):
                    return XBC[:, c, :, tap:tap + SEQ]

                def urows(c, j):
                    return U[:, c, 0:376].rearrange("p (r w) -> p r w", w=94)[:, :, j:j + 64]

                def ucols(c, j):
                    return U[:, c, 376 + j:376 + j + SEQ]

                def taps(dve, jobs, k, start):
                    for j in range(k):
                        for i, (out, src, w, b) in enumerate(jobs):
                            if j == 0:
                                ins = nc.vector.tensor_scalar(out, src(j), w(j), b, ALU.mult, ALU.add)
                            else:
                                dve.wait_ge(s["tap"], start + len(jobs) * (j - 1) + i + 1)
                                ins = nc.vector.scalar_tensor_tensor(out=out, in0=src(j), scalar=w(j), in1=out,
                                                                     op0=ALU.mult, op1=ALU.add)
                            ins.then_inc(s["tap"], 1)

                @block.vector
                def _(dve):
                    link = chain(dve, s["small"])
                    dve.wait_ge(s["rows_in"], 16)
                    link(nc.vector.tensor_tensor(raw[:], dt_tok[:], rows[:, 0:32].unsqueeze(1).to_broadcast([P, NT, 32]), ALU.add))
                    link(nc.vector.tensor_scalar(mag[:], raw[:], 0.0, None, ALU.max))
                    nc.vector.scalar_tensor_tensor(out=raw[:], in0=mag[:], scalar=-2.0, in1=raw[:],
                                                   op0=ALU.mult, op1=ALU.add).then_inc(s["prep"], 1)
                    dve.wait_ge(s["act_prep"], 3)
                    nc.vector.tensor_tensor(dt_tok[:], mag[:], raw[:], ALU.add).then_inc(s["prep"], 1)
                    dve.wait_ge(s["prep"], 2)
                    link(nc.vector.scalar_tensor_tensor(
                        out=LA[:], in0=dt_tok[:], scalar=-1.0, in1=aneg[:].unsqueeze(1).to_broadcast([P, NT, 32]),
                        op0=ALU.mult, op1=ALU.mult))
                    for c in range(0, 16, 2):
                        if c >= 2:
                            dve.wait_ge(s["xbc_out"], c)
                        accs = [acc[:, i, :].rearrange("p (s t) -> p s t", s=2) for i in range(2)]
                        taps(dve, [(accs[i], lambda j, i=i: xsrc(c + i, j), lambda j, i=i: self.v("conv_w", 16 * j + c + i),
                                    self.v("conv_b", c + i)) for i in range(2)], K5, K5 * c)
                    for c in range(on_pe, KD):
                        w, b = lambda j: self.v("cf_w", KD * j + c), self.v("cf_b", c)
                        taps(dve, [(H[:, c, 0:SEQ].rearrange("p (r w) -> p r w", w=64), lambda j: urows(c, j), w, b),
                                   (H[:, c, SEQ:TT], lambda j: ucols(c, j), w, b)], K31,
                             16 * K5 + 2 * K31 * (c - on_pe))

                @block.tensor
                def _(pe):
                    for c in range(on_pe):
                        for j in range(K31):
                            n = K31 * c + j
                            pe.wait_ge(s["diag_made"], n + 1)
                            if c >= 4 and j == 0:
                                pe.wait_ge(s["copied"], c - 3)
                            nc.tensor.matmul(ps[:, 2 * (c % 4), 0:SEQ], diag[:, n % 8, :], urows(c, j),
                                             start=(j == 0), stop=(j == K31 - 1))
                            nc.tensor.matmul(ps[:, 2 * (c % 4) + 1, 0:SEQ], diag[:, n % 8, :], ucols(c, j),
                                             start=(j == 0), stop=(j == K31 - 1)).then_inc(s["diag_used"], 1)

                @block.scalar
                def _(act):
                    act.wait_ge(s["rows_in"], 16)
                    nc.scalar.activation(aneg[:], rows[:, 32:64], ACT.Exp).then_inc(s["act_prep"], 1)
                    act.wait_ge(s["prep"], 1)
                    nc.scalar.activation(raw[:], raw[:], ACT.Exp).then_inc(s["act_prep"], 1)
                    act.wait_ge(s["act_prep"], 2)
                    nc.scalar.activation(raw[:], raw[:], ACT.Ln, bias=1.0).then_inc(s["act_prep"], 1)

                    def diagonal(n):
                        c, j = divmod(n, K31)
                        if n >= 8:
                            act.wait_ge(s["diag_used"], n - 7)
                        nc.scalar.activation(diag[:, n % 8, :], self.c("ident"), ACT.Copy,
                                             scale=self.v("cf_w", KD * j + c)).then_inc(s["diag_made"], 1)

                    def silu(c):
                        act.wait_ge(s["tap"], K5 * (c - c % 2) + 2 * (K5 - 1) + c % 2 + 1)
                        nc.scalar.activation(XBC[:, c, :, 2:2 + SEQ], acc[:, c % 2, :].rearrange("p (s t) -> p s t", s=2),
                                             ACT.Silu).then_inc(s["xbc_out"], 1)

                    def copy(c):
                        act.wait_ge(s["diag_used"], K31 * (c + 1))
                        nc.scalar.activation(H[:, c, :].rearrange("p (h t) -> p h t", h=2),
                                             ps[:, 2 * (c % 4):2 * (c % 4) + 2, 0:SEQ], ACT.Identity,
                                             bias=self.v("cf_b", c)).then_inc(s["copied"], 1)

                    for n in range(K31 * on_pe):
                        diagonal(n)
                        if n % 4 == 3 and n // 4 < 16:
                            silu(n // 4)
                        if n >= K31 and n % K31 == 8:
                            copy(n // K31 - 1)
                    copy(on_pe - 1)

    def layer_norm_silu(self):
        nc, ps, H = self.nc, self.ps, self.H
        with ExitStack() as ctx:
            sq = self.sb(ctx, "ln_squares", [P, 2, TT])
            root = self.sb(ctx, "ln_root", [P, TT])
            mean = self.sb(ctx, "ln_mean", [P, TT])
            with stage(nc, "summed mean_done centred squared varied rooted inverted scaled done") as (block, s):
                @block.tensor
                def _(pe):
                    for k in range(KD):
                        last = nc.tensor.matmul(ps[:, 0, :], self.c("ones"), H[:, k, :], start=(k == 0), stop=(k == KD - 1))
                    last.then_inc(s["summed"], 1)
                    for k in range(KD):
                        pe.wait_ge(s["squared"], k + 1)
                        nc.tensor.matmul(ps[:, 1, :], self.c("ones"), sq[:, k % 2, :], start=(k == 0),
                                         stop=(k == KD - 1)).then_inc(s["varied"], 1)

                @block.vector
                def _(dve):
                    dve.wait_ge(s["summed"], 1)
                    nc.vector.tensor_scalar(mean[:], ps[:, 0, :], 1.0 / D, None, ALU.mult).then_inc(s["mean_done"], 1)
                    dve.wait_ge(s["mean_done"], 1)
                    for k in range(KD):
                        nc.vector.tensor_tensor(H[:, k, :], H[:, k, :], mean[:], ALU.subtract).then_inc(s["centred"], 1)
                    dve.wait_ge(s["rooted"], 1)
                    nc.vector.reciprocal(root[:], root[:]).then_inc(s["inverted"], 1)
                    dve.wait_ge(s["inverted"], 1)
                    dve.wait_ge(s["centred"], KD)
                    for k in range(KD):
                        nc.vector.scalar_tensor_tensor(out=H[:, k, :], in0=H[:, k, :], scalar=self.v("cf_lng", k),
                                                       in1=root[:], op0=ALU.mult, op1=ALU.mult).then_inc(s["scaled"], 1)

                @block.scalar
                def _(act):
                    for k in range(KD):
                        act.wait_ge(s["centred"], k + 1)
                        if k >= 2:
                            act.wait_ge(s["varied"], k - 1)
                        nc.scalar.activation(sq[:, k % 2, :], H[:, k, :], ACT.Square).then_inc(s["squared"], 1)
                    act.wait_ge(s["varied"], KD)
                    nc.scalar.activation(root[:], ps[:, 1, :], ACT.Sqrt, bias=self.eps[:, 0:1],
                                         scale=1.0 / D).then_inc(s["rooted"], 1)
                    for k in range(KD):
                        act.wait_ge(s["scaled"], k + 1)
                        nc.scalar.activation(H[:, k, :], H[:, k, :], ACT.Silu, bias=self.v("cf_lnb", k)).then_inc(s["done"], 1)

    def ssd(self, Z, XBC, dt_tok, LA):
        nc, ps = self.nc, self.ps
        H16 = 16

        def xbc(c, tile, p0=0, p1=P):
            return XBC[p0:p1, c, tile // 2, 2 + (tile % 2) * P:2 + (tile % 2) * P + P]
        orders = [[2, 3, 0, 1], [3, 2, 1, 0]]
        steps = [(d, t) for d in range(2) for t in orders[d]]
        with ExitStack() as ctx:
            tok = self.sb(ctx, "xb_tokens", [P, NT, 12, P])
            acum = self.sb(ctx, "acum", [P, NT, 32])
            eend = self.sb(ctx, "exp_end", [P, NT, 32])
            wend = self.sb(ctx, "w_end", [P, NT, 32])
            Y = self.sb(ctx, "y", [P, KD, TT])
            with stage(nc, "transposed copied act_copied sums acum_done diff_done exp_done w_done yinit") as (block, s):
                @block.tensor
                def _(pe):
                    for i in range(12):
                        if i >= 4:
                            pe.wait_ge(s["copied"] if i % 2 == 0 else s["act_copied"], (i - 4) // 2 + 1)
                        for t in range(NT):
                            last = nc.tensor.transpose(ps[:, i % 4, t * P:(t + 1) * P], xbc(i, t), self.c("ident"))
                        last.then_inc(s["transposed"], 1)
                    for t in range(NT):
                        nc.tensor.matmul(ps[:, 4, 32 * t:32 * t + 16], self.c("upper"), LA[:, t, 0:16], start=True, stop=True)
                        nc.tensor.matmul(ps[:, 4, 32 * t + 16:32 * t + 32], self.c("lower"), LA[:, t, 16:32], start=True, stop=True)
                    for t in range(NT):
                        last = nc.tensor.matmul(ps[:, 5, 32 * t:32 * t + 32], self.c("ones"), LA[:, t, :], start=True, stop=True)
                    last.then_inc(s["sums"], 1)

                @block.vector
                def _(dve):
                    for i in range(0, 12, 2):
                        dve.wait_ge(s["transposed"], i + 1)
                        nc.vector.tensor_copy(tok[:, :, i, :], ps[:, i % 4, :].rearrange("p (t c) -> p t c", t=NT)).then_inc(s["copied"], 1)
                    dve.wait_ge(s["sums"], 1)
                    nc.vector.tensor_copy(acum[:].rearrange("p t n -> p (t n)"), ps[:, 4, 0:128]).then_inc(s["acum_done"], 1)
                    dve.wait_ge(s["acum_done"], 1)
                    dve.wait_ge(s["exp_done"], 1)
                    nc.vector.tensor_tensor(wend[:].rearrange("p t n -> p (t n)"), ps[:, 5, 0:128],
                                            acum[:].rearrange("p t n -> p (t n)"), ALU.subtract).then_inc(s["diff_done"], 1)
                    dve.wait_ge(s["exp_done"], 2)
                    nc.vector.tensor_tensor(wend[:], wend[:], dt_tok[:], ALU.mult).then_inc(s["w_done"], 1)
                    for k in range(KD):
                        nc.vector.tensor_scalar(Y[:, k, :].rearrange("p (s t) -> p s t", s=2), XBC[:, k, :, 2:2 + SEQ],
                                                self.v("d_skip", k), None, ALU.mult).then_inc(s["yinit"], 1)

                @block.scalar
                def _(act):
                    for i in range(1, 12, 2):
                        act.wait_ge(s["transposed"], i + 1)
                        nc.scalar.activation(tok[:, :, i, :], ps[:, i % 4, :].rearrange("p (t c) -> p t c", t=NT),
                                             ACT.Copy).then_inc(s["act_copied"], 1)
                    act.wait_ge(s["sums"], 1)
                    nc.scalar.activation(eend[:].rearrange("p t n -> p (t n)"), ps[:, 5, 0:128], ACT.Exp).then_inc(s["exp_done"], 1)
                    act.wait_ge(s["diff_done"], 1)
                    nc.scalar.activation(wend[:], wend[:], ACT.Exp).then_inc(s["exp_done"], 1)

            S = self.sb(ctx, "state", [P, 1024])
            xdt = self.sb(ctx, "x_dt", [P, 1024])
            xw = self.sb(ctx, "x_w", [P, 1024])
            Gm = self.sb(ctx, "cb_masked", [P, 512])
            E = self.sb(ctx, "decay", [P, 2, 512])
            EA = self.sb(ctx, "exp_acum", [P, 2, 512])
            with stage(nc, "cb_done gm_done xdt_done xw_done bcast_done diff_done relu_done exp_done ea_done "
                           "m_done cp_done y_sum y_added s_sum s_scaled s_done cleared") as (block, s):
                units = [(i, g) for i in range(len(steps)) for g in range(4)]

                def banks(u):
                    return 0 + u % 2, 2 + u % 2, 4 + u % 2

                @block.tensor
                def _(pe):
                    def cb(i):
                        d, t = steps[i]
                        if i >= 1:
                            pe.wait_ge(s["gm_done"], i)
                        for g in range(4):
                            last = nc.tensor.matmul(ps[:, 6, g * P:(g + 1) * P], xbc(8 + g, t), xbc(12 + g, t), start=True, stop=True)
                        last.then_inc(s["cb_done"], 1)

                    def bcast(u):
                        i, g = units[u]
                        d, t = steps[i]
                        b = banks(u)[0]
                        if u >= 2:
                            pe.wait_ge(s["diff_done"], u - 1)
                            pe.wait_ge(s["ea_done"], u - 1)
                        for h in range(4):
                            col = 16 * d + 4 * g + h
                            last = nc.tensor.matmul(ps[:, b, h * P:(h + 1) * P], LA[:, t, col:col + 1].to_broadcast([P, P]),
                                                    self.c(("upper", "lower")[d]), start=True, stop=True)
                        last.then_inc(s["bcast_done"], 1)

                    def outputs(u):
                        i, g = units[u]
                        d, t = steps[i]
                        _, yb, sb_ = banks(u)
                        first = i % 4 == 0
                        if u >= 2:
                            pe.wait_ge(s["y_added"], u - 1)
                        pe.wait_ge(s["m_done"], u + 1)
                        pe.wait_ge(s["xdt_done"], i + 1)
                        if not first:
                            pe.wait_ge(s["cp_done"], u + 1)
                            pe.wait_ge(s["s_done"], 4 * (i - 1) + g + 1)
                        for h in range(4):
                            lo = 64 * (h % 2)
                            o = ps[lo:lo + 64, yb, (h // 2) * P:(h // 2 + 1) * P]
                            hc = (4 * g + h) * 64
                            last = nc.tensor.matmul(o, xdt[:, hc:hc + 64], E[:, u % 2, h * P:(h + 1) * P], start=True, stop=first)
                            if not first:
                                last = nc.tensor.matmul(o, S[:, hc:hc + 64], EA[:, u % 2, h * P:(h + 1) * P], start=False, stop=True)
                        last.then_inc(s["y_sum"], 1)
                        if u >= 2:
                            pe.wait_ge(s["s_done"], u - 1)
                        pe.wait_ge(s["xw_done"], i + 1)
                        nc.tensor.matmul(ps[:, sb_, 0:256], tok[:, t, 8 + g, :], xw[:, g * 256:(g + 1) * 256],
                                         start=True, stop=True).then_inc(s["s_sum"], 1)
                    cb(0)
                    bcast(0)
                    for u in range(len(units)):
                        if u + 1 < len(units):
                            if units[u + 1][1] == 0:
                                cb(units[u + 1][0])
                            bcast(u + 1)
                        outputs(u)

                @block.vector
                def _(dve):
                    def prepare(i):
                        d, t = steps[i]
                        dve.wait_ge(s["cb_done"], i + 1)
                        if i >= 1:
                            dve.wait_ge(s["m_done"], 4 * i)
                        nc.vector.tensor_tensor(Gm[:].rearrange("p (g t) -> p g t", g=4), ps[:, 6, :].rearrange("p (g t) -> p g t", g=4),
                                                self.c(("upper", "lower")[d]).unsqueeze(1).to_broadcast([P, 4, P]),
                                                ALU.mult).then_inc(s["gm_done"], 1)
                        if i >= 1:
                            dve.wait_ge(s["y_sum"], 4 * i)
                        x = tok[:, t, 0:8, :].rearrange("p c (h q) -> p (c h) q", h=2)
                        nc.vector.tensor_tensor(xdt[:].rearrange("p (h q) -> p h q", q=64), x,
                                                dt_tok[:, t, 16 * d:16 * d + 16].unsqueeze(2).to_broadcast([P, 16, 64]),
                                                ALU.mult).then_inc(s["xdt_done"], 1)

                    def state(u):
                        i, g = units[u]
                        d, t = steps[i]
                        dve.wait_ge(s["s_sum"], u + 1)
                        Sg = S[:, g * 256:(g + 1) * 256]
                        if i % 4 == 0:
                            nc.vector.tensor_copy(Sg, ps[:, banks(u)[2], 0:256]).then_inc(s["s_done"], 1)
                            return
                        e = eend[:, t, 16 * d + 4 * g:16 * d + 4 * g + 4].unsqueeze(2).to_broadcast([P, 4, 64])
                        nc.vector.tensor_tensor(Sg.rearrange("p (h q) -> p h q", q=64), Sg.rearrange("p (h q) -> p h q", q=64),
                                                e, ALU.mult).then_inc(s["s_scaled"], 1)
                        n_scaled[0] += 1
                        dve.wait_ge(s["s_scaled"], n_scaled[0])
                        nc.vector.tensor_tensor(Sg, Sg, ps[:, banks(u)[2], 0:256], ALU.add).then_inc(s["s_done"], 1)
                    n_scaled = [0]

                    def diff(u):
                        i, g = units[u]
                        d, t = steps[i]
                        dve.wait_ge(s["ea_done"], u + 1)
                        if u >= 2:
                            dve.wait_ge(s["y_sum"], u - 1)
                        a = acum[:, t, 16 * d + 4 * g:16 * d + 4 * g + 4].unsqueeze(2).to_broadcast([P, 4, P])
                        nc.vector.tensor_tensor(E[:, u % 2, :].rearrange("p (h t) -> p h t", h=4), a,
                                                ps[:, banks(u)[0], :].rearrange("p (h t) -> p h t", h=4),
                                                ALU.subtract).then_inc(s["diff_done"], 1)

                    def weight(u):
                        i, g = units[u]
                        dve.wait_ge(s["exp_done"], u + 1)
                        dve.wait_ge(s["gm_done"], i + 1)
                        nc.vector.tensor_tensor(E[:, u % 2, :].rearrange("p (h t) -> p h t", h=4),
                                                E[:, u % 2, :].rearrange("p (h t) -> p h t", h=4),
                                                Gm[:, g * P:(g + 1) * P].unsqueeze(1).to_broadcast([P, 4, P]),
                                                ALU.mult).then_inc(s["m_done"], 1)

                    def add_y(u):
                        i, g = units[u]
                        d, t = steps[i]
                        dve.wait_ge(s["y_sum"], u + 1)
                        y = Y[:, 2 * g:2 * g + 2, t * P:(t + 1) * P]
                        nc.vector.tensor_tensor(y, y, ps[:, banks(u)[1], 0:256].rearrange("p (c t) -> p c t", c=2),
                                                ALU.add).then_inc(s["y_added"], 1)
                    diff(0)
                    prepare(0)
                    for u in range(len(units)):
                        weight(u)
                        if u + 1 < len(units):
                            diff(u + 1)
                        add_y(u)
                        state(u)
                        if u + 1 < len(units) and units[u + 1][1] == 0:
                            prepare(units[u + 1][0])

                @block.scalar
                def _(act):
                    for u in range(len(units)):
                        b = banks(u)[0]
                        act.wait_ge(s["bcast_done"], u + 1)
                        if u >= 2:
                            act.wait_ge(s["cp_done"], u - 1)
                            act.wait_ge(s["y_sum"], u - 1)
                        nc.scalar.activation(EA[:, u % 2, :], ps[:, b, :], ACT.Exp).then_inc(s["ea_done"], 1)
                        act.wait_ge(s["diff_done"], u + 1)
                        nc.scalar.activation(E[:, u % 2, :], E[:, u % 2, :], ACT.Relu).then_inc(s["relu_done"], 1)
                        act.wait_ge(s["relu_done"], u + 1)
                        nc.scalar.activation(E[:, u % 2, :], E[:, u % 2, :], ACT.Exp, scale=-1.0).then_inc(s["exp_done"], 1)

                @block.gpsimd
                def _(pool):
                    for u, (i, g) in enumerate(units):
                        d, t = steps[i]
                        if g == 0:
                            if i >= 1:
                                pool.wait_ge(s["s_sum"], 4 * i)
                            x = tok[:, t, 0:8, :].rearrange("p c (h q) -> p (c h) q", h=2)
                            nc.gpsimd.tensor_tensor(xw[:].rearrange("p (h q) -> p h q", q=64), x,
                                                    wend[:, t, 16 * d:16 * d + 16].unsqueeze(2).to_broadcast([P, 16, 64]),
                                                    ALU.mult).then_inc(s["xw_done"], 1)
                        pool.wait_ge(s["ea_done"], u + 1)
                        nc.gpsimd.tensor_tensor(EA[:, u % 2, :].rearrange("p (h t) -> p h t", h=4),
                                                EA[:, u % 2, :].rearrange("p (h t) -> p h t", h=4),
                                                xbc(12 + g, t).unsqueeze(1).to_broadcast([P, 4, P]),
                                                ALU.mult).then_inc(s["cp_done"], 1)

            with stage(nc, "gated") as (block, s):
                @block.vector
                def _(dve):
                    for k in range(KD):
                        nc.vector.tensor_tensor(Z[:, k, :], Z[:, k, :], Y[:, k, :], ALU.mult).then_inc(s["gated"], 1)

    def even_mixer(self):
        with ExitStack() as ctx:
            Z = self.sb(ctx, "z", [P, KD, TT])
            with ExitStack() as middle:
                XBC = self.sb(middle, "xbc", [P, 16, 2, SEQ + 4])
                dt_tok = self.sb(middle, "dt", [P, NT, 32])
                LA = self.sb(middle, "log_decay", [P, NT, 32])
                with ExitStack() as inner:
                    U = self.sb(inner, "u", [P, KD, 662])
                    self.even_in(Z, XBC, U, dt_tok)
                    self.convolutions(XBC, U, dt_tok, LA)
                self.layer_norm_silu()
                self.ssd(Z, XBC, dt_tok, LA)
            z = lambda k, t: Z[:, k, t]
            self.rms_norm(z, z, KD, TT, lambda k, c: self.v("ssd_g", k))
            self.out_projection("ABAB", 16, lambda k: Z[:, k, :] if k < 8 else self.H[:, k - 8, :], 0, TT)

    def route(self, gates, tokens):
        nc, ps, H = self.nc, self.ps, self.H
        nt = tokens // P
        G = 4 * nt
        with ExitStack() as ctx:
            rw = self.sb(ctx, "router_w", [P, KD, 16])
            rb = self.sb(ctx, "router_b", [P, 16])
            sc = self.sb(ctx, "scores", [P, nt, 16])
            sel = self.sb(ctx, "sel", [P, nt, 16])
            gt = self.sb(ctx, "greater", [P, G, 4, 4])
            eq = self.sb(ctx, "equal", [P, G, 4, 4])
            rank = self.sb(ctx, "rank", [P, G, 4])
            gs = self.sb(ctx, "group_score", [P, nt, 4])
            grank = self.sb(ctx, "group_rank", [P, nt, 4])
            tot = self.sb(ctx, "weight_sum", [P, nt])
            comb = self.sb(ctx, "combine", [P, nt, 16])
            combT = self.sb(ctx, "combine_t", [16, tokens])
            scT = self.sb(ctx, "scores_t", [16, tokens])
            with stage(nc, "w_in logits sig_done link comb_done transposed t_copied bcast act_copied dve_copied") as (block, s):
                @block.sync
                def _(sp):
                    sp.dma_start(rw[:].rearrange("p k n -> p (k n)"), self.d["router_w"]).then_inc(s["w_in"], 16)
                    sp.dma_start(rb[:], self.d["router_b"].partition_broadcast(P)).then_inc(s["w_in"], 16)

                @block.tensor
                def _(pe):
                    pe.wait_ge(s["w_in"], 32)
                    for k in range(KD):
                        last = nc.tensor.matmul(ps[0:16, 0, 0:tokens], rw[:, k, :], H[:, k, 0:tokens],
                                                start=(k == 0), stop=(k == KD - 1))
                    last.then_inc(s["logits"], 1)
                    pe.wait_ge(s["sig_done"], 1)
                    for t in range(nt):
                        last = nc.tensor.transpose(ps[:, 6, 16 * t:16 * t + 16], scT[:, t * P:(t + 1) * P],
                                                   self.c("ident", 16, p=16))
                    last.then_inc(s["logits"], 1)
                    pe.wait_ge(s["comb_done"], 1)
                    for t in range(nt):
                        last = nc.tensor.transpose(ps[0:16, 1, t * P:(t + 1) * P], comb[:, t, :], self.c("ident"))
                    last.then_inc(s["transposed"], 1)
                    pe.wait_ge(s["t_copied"], 1)
                    for e in range(16):
                        if e >= 4:
                            pe.wait_ge(s["act_copied"] if e % 2 else s["dve_copied"], (e - 4) // 2 + 1)
                        nc.tensor.matmul(ps[:, 2 + e % 4, 0:tokens], self.cst[0:16, CCOL["ident"] + e:CCOL["ident"] + e + 1].to_broadcast([16, P]),
                                         combT[:], start=True, stop=True).then_inc(s["bcast"], 1)

                @block.scalar
                def _(act):
                    act.wait_ge(s["logits"], 1)
                    nc.scalar.activation(scT[:], ps[0:16, 0, 0:tokens], ACT.Sigmoid).then_inc(s["sig_done"], 1)
                    for e in range(1, 16, 2):
                        act.wait_ge(s["bcast"], e + 1)
                        nc.scalar.activation(gates[:, e, 0:tokens], ps[:, 2 + e % 4, 0:tokens], ACT.Copy).then_inc(s["act_copied"], 1)

                @block.vector
                def _(dve):
                    link = chain(dve, s["link"])
                    V = nc.vector
                    dve.wait_ge(s["w_in"], 32)
                    dve.wait_ge(s["logits"], 2)
                    link(V.tensor_copy(sc[:].rearrange("p t n -> p (t n)"), ps[:, 6, 0:16 * nt]))
                    link(V.tensor_tensor(sel[:], sc[:], rb[:].unsqueeze(1).to_broadcast([P, nt, 16]), ALU.add))
                    v = sel[:].rearrange("p t (g j) -> p (t g) j", j=4)

                    def ranks(vals, n, out):
                        vi = vals.unsqueeze(3).to_broadcast([P, n, 4, 4])
                        vj = vals.unsqueeze(2).to_broadcast([P, n, 4, 4])
                        link(V.tensor_tensor(gt[:, 0:n], vj, vi, ALU.is_gt))
                        link(V.tensor_tensor(eq[:, 0:n], vj, vi, ALU.is_equal))
                        tie = self.c("tie", 16).rearrange("p (i j) -> p i j", j=4).unsqueeze(1).to_broadcast([P, n, 4, 4])
                        link(V.tensor_tensor(eq[:, 0:n], eq[:, 0:n], tie, ALU.mult))
                        link(V.tensor_tensor(gt[:, 0:n], gt[:, 0:n], eq[:, 0:n], ALU.add))
                        link(V.tensor_reduce(out, gt[:, 0:n], AX.X, ALU.add))

                    ranks(v, G, rank[:])
                    link(V.tensor_scalar(rank[:], rank[:], 2.0, None, ALU.is_lt))
                    link(V.tensor_tensor(eq[:, :, 0, :], v, rank[:], ALU.mult))
                    link(V.tensor_reduce(gs[:].rearrange("p t g -> p (t g)"), eq[:, :, 0, :], AX.X, ALU.add))
                    ranks(gs[:], nt, grank[:])
                    link(V.tensor_scalar(grank[:], grank[:], 1.0, None, ALU.is_lt))
                    link(V.tensor_tensor(rank[:], rank[:], grank[:].rearrange("p t g -> p (t g)").unsqueeze(2).to_broadcast([P, G, 4]), ALU.mult))
                    link(V.tensor_tensor(comb[:], sc[:], rank[:].rearrange("p (t g) j -> p t (g j)", g=4), ALU.mult))
                    link(V.tensor_reduce(tot[:], comb[:], AX.X, ALU.add))
                    link(V.reciprocal(tot[:], tot[:]))
                    V.tensor_tensor(comb[:], comb[:], tot[:].unsqueeze(2).to_broadcast([P, nt, 16]), ALU.mult).then_inc(s["comb_done"], 1)
                    dve.wait_ge(s["transposed"], 1)
                    V.tensor_copy(combT[:], ps[0:16, 1, 0:tokens]).then_inc(s["t_copied"], 1)
                    for e in range(0, 16, 2):
                        dve.wait_ge(s["bcast"], e + 1)
                        V.tensor_copy(gates[:, e, 0:tokens], ps[:, 2 + e % 4, 0:tokens]).then_inc(s["dve_copied"], 1)


    def split_input(self, tokens, hi, lo):
        nc, H = self.nc, self.H
        with stage(nc, "hi_done lo_done") as (block, s):
            @block.scalar
            def _(act):
                for k in range(KD):
                    nc.scalar.activation(hi[:, k, :], H[:, k, 0:tokens], ACT.Copy).then_inc(s["hi_done"], 1)

            @block.vector
            def _(dve):
                for k in range(KD):
                    dve.wait_ge(s["hi_done"], k + 1)
                    nc.vector.tensor_tensor(lo[:, k, :], H[:, k, 0:tokens], hi[:, k, :].bitcast(F32), ALU.subtract).then_inc(s["lo_done"], 1)

    def product(self, out, w_hi, w_lo, x_hi, x_lo, first, last):
        nc = self.nc
        nc.tensor.matmul(out, w_hi, x_hi, start=first, stop=False)
        nc.tensor.matmul(out, w_hi, x_lo, start=False, stop=False)
        return nc.tensor.matmul(out, w_lo, x_hi, start=False, stop=last)

    def experts(self, layer, tokens):
        nc, ring, ps, X = self.nc, self.ring, self.ps, self.X
        NE, NP, PER = 16, 12, 16
        AHEAD = 3
        base = ring.chunks
        used = {a: ring.used[a] for a in "ABCD"}
        halves = [(c, slice(c * SEQ, (c + 1) * SEQ)) for c in range(tokens // SEQ)]
        nh = len(halves)
        row0 = 16 * layer
        T = slice(0, tokens)

        def done(p):
            return p + 1 if p < 8 else 8 + 2 * (p - 7)
        with ExitStack() as ctx:
            xh = self.sb(ctx, "x_hi", [P, KD, tokens], F32R)
            xl = self.sb(ctx, "x_lo", [P, KD, tokens], F32R)
            self.split_input(tokens, xh, xl)
            gates = self.sb(ctx, "gates", [P, 16, tokens])
            self.route(gates, tokens)
            wh = self.sb(ctx, "w_hi", [P, 4, 1024], F32R)
            wl = self.sb(ctx, "w_lo", [P, 4, 1024], F32R)
            sg, hraw = self.H[:, 0:2, T], self.H[:, 2, T]
            hh = self.sb(ctx, "hidden_hi", [P, 4, tokens], F32R)
            hl = self.sb(ctx, "hidden_lo", [P, 4, tokens], F32R)

            def raw(p):
                if p < 8:
                    area = "AB"[p % 2]
                    j = p // 2
                    src = ring.buf[area][:].rearrange("p (k n) -> p k n", k=KD)[:, :, j * P:(j + 1) * P]
                    return [(area, src, lambda w: w[:, p % 4, :].rearrange("p (k n) -> p k n", k=KD))]
                r = p - 8
                out = []
                for i, area in enumerate("CD"):
                    src = ring.buf[area][:].rearrange("p (k n) -> p k n", k=2)[:, :, r * 256:(r + 1) * 256]
                    out.append((area, src, lambda w, i=i: w[:, p % 4, 512 * i:512 * i + 512].rearrange("p (k n) -> p k n", k=2)))
                return out

            with stage(nc, "hi_done lo_done silu_done up_done hraw_done hh_done hid_done added") as (block, s):
                @block.sync
                def _(sp):
                    with sp.Fori(0, NE - 1) as e:
                        for area, last, src in (("A", 6, self.d["moe_gate"][e + (row0 + 1)]),
                                                ("B", 7, self.d["moe_up"][e + (row0 + 1)]),
                                                ("C", 11, self.d["moe_down"][e * 2 + 2 * (row0 + 1)]),
                                                ("D", 11, self.d["moe_down"][e * 2 + 2 * (row0 + 1) + 1])):
                            sp.wait_ge(s["lo_done"], e * NP + last + 1)
                            sp.dma_start(ring.buf[area][:], src).then_inc(ring.landed[area], 16)
                    for area, last in (("A", 6), ("B", 7), ("C", 11), ("D", 11)):
                        ring.sent[area] += NE - 1
                        ring.load(sp, area, NP * (NE - 1) + last + 1, s["lo_done"])

                @block.scalar
                def _(act):
                    def hi(e, p):
                        if p >= 4:
                            act.wait_ge(ring.chunk_done, e * PER + base + done(p - 4))
                        else:
                            act.wait_ge(ring.chunk_done, e * PER + base - PER + done(p + 8))
                        for area, src, dst in raw(p):
                            if p in (0, 1, 8):
                                act.wait_ge(ring.landed[area], e * 16 + 16 * (used[area] + 1))
                            ins = nc.scalar.activation(dst(wh), src, ACT.Copy)
                        ins.then_inc(s["hi_done"], 1)

                    def one(e, last):
                        for p in range(NP):
                            q = p + AHEAD
                            if q < NP:
                                hi(e, q)
                            elif not last:
                                hi(e + 1, q - NP)
                            if p < 8 and p % 2 == 0:
                                j = p // 2
                                act.wait_ge(ring.chunk_done, e * PER + base + done(p))
                                act.wait_ge(s["up_done"], e * 4 + max(0, j - 1) + 1)
                                nc.scalar.activation(sg[:, j % 2, :], ps[:, j % 2, T], ACT.Silu).then_inc(s["silu_done"], 1)
                    self.credit(nc.scalar, s["silu_done"])
                    for p in range(AHEAD):
                        hi(0, p)
                    with act.Fori(0, NE - 1) as e:
                        one(e, False)
                    one(NE - 1, True)

                @block.vector
                def _(dve):
                    def lo(e, p):
                        dve.wait_ge(s["hi_done"], e * NP + p + 1)
                        for area, src, dst in raw(p):
                            ins = nc.vector.tensor_tensor(dst(wl), src, dst(wh).bitcast(F32), ALU.subtract)
                        ins.then_inc(s["lo_done"], 1)

                    def hidden(e, j):
                        dve.wait_ge(ring.chunk_done, e * PER + base + done(2 * j + 1))
                        dve.wait_ge(s["silu_done"], e * 4 + j + 2)
                        nc.vector.tensor_tensor(sg[:, j % 2, :], ps[:, 2 + j % 2, T], sg[:, j % 2, :], ALU.mult).then_inc(s["hraw_done"], 1)
                        dve.wait_ge(s["hraw_done"], e * 4 + j + 1)
                        nc.vector.tensor_tensor(hraw, sg[:, j % 2, :], gates[:, bass.ds(e, 1), :].rearrange("p e t -> p (e t)"),
                                                ALU.mult).then_inc(s["up_done"], 1)
                        dve.wait_ge(s["up_done"], e * 4 + j + 2)
                        nc.vector.tensor_copy(hh[:, j, :], hraw).then_inc(s["hh_done"], 1)
                        dve.wait_ge(s["hh_done"], e * 4 + j + 1)
                        nc.vector.tensor_tensor(hl[:, j, :], hraw, hh[:, j, :].bitcast(F32), ALU.subtract).then_inc(s["hid_done"], 1)

                    def one(e, last):
                        for p in range(NP):
                            q = p + AHEAD
                            if q < NP:
                                lo(e, q)
                            elif not last:
                                lo(e + 1, q - NP)
                            if p < 8 and p % 2:
                                hidden(e, p // 2)
                            for m in ((2 * (p - 8), 2 * (p - 8) + 1) if p >= 8 else ()):
                                dve.wait_ge(ring.chunk_done, e * PER + base + 8 + m + 1)
                                dve.wait_ge(s["added"], e * (nh * KD) + 1)
                                for c, t in halves:
                                    nc.vector.scalar_tensor_tensor(out=X[:, m, t], in0=ps[:, 4 + m % 4, t],
                                                                   scalar=self.m(layer, 5, m, c), in1=X[:, m, t],
                                                                   op0=ALU.mult, op1=ALU.add).then_inc(s["added"], 1)
                    self.credit(nc.vector, s["up_done"])
                    self.credit(nc.vector, s["added"], 2)
                    for p in range(AHEAD):
                        lo(0, p)
                    with dve.Fori(0, NE - 1) as e:
                        one(e, False)
                    one(NE - 1, True)

                @block.tensor
                def _(pe):
                    with pe.Fori(0, NE) as e:
                        for p in range(8):
                            j, what = divmod(p, 2)
                            pe.wait_ge(s["lo_done"], e * NP + p + 1)
                            pe.wait_ge(s["silu_done"] if what == 0 else s["up_done"], e * 4 + max(0, j - 1) + 1)
                            for k in range(KD):
                                last = self.product(ps[:, 2 * what + j % 2, T], wh[:, p % 4, k * P:(k + 1) * P],
                                                    wl[:, p % 4, k * P:(k + 1) * P], xh[:, k, :], xl[:, k, :], k == 0, k == KD - 1)
                            last.then_inc(ring.chunk_done, 1)
                        for p in range(8, NP):
                            pe.wait_ge(s["lo_done"], e * NP + p + 1)
                            for half in range(2):
                                m = 2 * (p - 8) + half
                                pe.wait_ge(s["added"], e * (nh * KD) + (nh * (m - 3) if m >= 4 else 0) + 1)
                                for k in range(4):
                                    if m == 0:
                                        pe.wait_ge(s["hid_done"], e * 4 + k + 1)
                                    w = slice(k * 256 + half * P, k * 256 + (half + 1) * P)
                                    last = self.product(ps[:, 4 + m % 4, T], wh[:, p % 4, w], wl[:, p % 4, w],
                                                        hh[:, k, :], hl[:, k, :], k == 0, k == 3)
                                last.then_inc(ring.chunk_done, 1)
        for a in "ABCD":
            ring.used[a] += NE
        ring.chunks += PER * NE

    def odd_in(self, Q, G, V, K, LF):
        nc, ring, ps, H = self.nc, self.ring, self.ps, self.H
        base = ring.chunks
        areas = "AB" * 5
        with ExitStack() as ctx:
            rows = self.sb(ctx, "lb_rows", [P, 2, D])
            top = self.sb(ctx, "lb_max", [P, D])
            with stage(nc, "rows_in link exps act_read dve_read f_scaled f_done k_done ln_done") as (block, s):
                @block.sync
                def _(sp):
                    sp.dma_start(rows[:].rearrange("p l n -> p (l n)"), self.d["lb_rows"].partition_broadcast(P)).then_inc(s["rows_in"], 16)
                    for i, area in enumerate(areas):
                        ring.load(sp, area, base + 4 * (i + 1))

                @block.tensor
                def _(pe):
                    def free(n):
                        if n >= 6:
                            j = n - 6
                            if j < 16:
                                pe.wait_ge(s["act_read"], j + 1)
                            elif j < 24:
                                pe.wait_ge(s["dve_read"], j - 15)
                            else:
                                pe.wait_ge(s["act_read"], j - 7)
                    for i in range(4):
                        self.panel_products(pe, None, areas[i], KD, 512, lambda k: H[:, k, 0:SEQ], 4 * i, range(6), SEQ, free)
                    for i in range(4, 10):
                        area = areas[i]
                        ring.arrived(pe, area)
                        for t in range(NT):
                            free(4 * i + t)
                            for k in range(KD):
                                last = nc.tensor.matmul(ps[:, (4 * i + t) % 6, :], H[:, k, t * P:(t + 1) * P],
                                                        ring.buf[area][:, k * 512:(k + 1) * 512],
                                                        start=(k == 0), stop=(k == KD - 1))
                            last.then_inc(ring.chunk_done, 1)

                @block.scalar
                def _(act):
                    act.wait_ge(s["link"], 2)
                    nc.scalar.activation(rows[:], rows[:], ACT.Exp).then_inc(s["exps"], 1)
                    for n in range(16):
                        act.wait_ge(ring.chunk_done, base + n + 1)
                        dst = Q[:, n, :] if n < 8 else G[:, n - 8, :]
                        nc.scalar.activation(dst, ps[:, n % 6, 0:SEQ], ACT.Silu).then_inc(s["act_read"], 1)
                    for n in range(24, 40):
                        act.wait_ge(ring.chunk_done, base + n + 1)
                        i, t = divmod(n - 24, 4)
                        nc.scalar.activation(K[:, t, i * 512:(i + 1) * 512], ps[:, n % 6, :], ACT.Sigmoid).then_inc(s["act_read"], 1)
                    for t in range(NT):
                        act.wait_ge(s["f_done"], 16)
                        act.wait_ge(s["k_done"], 16)
                        nc.scalar.activation(LF[:, t, :], LF[:, t, :], ACT.Ln).then_inc(s["ln_done"], 1)

                @block.vector
                def _(dve):
                    link = chain(dve, s["link"])
                    dve.wait_ge(s["rows_in"], 16)
                    link(nc.vector.tensor_tensor(top[:], rows[:, 0, :], rows[:, 1, :], ALU.max))
                    link(nc.vector.tensor_tensor(rows[:], rows[:], top[:].unsqueeze(1).to_broadcast([P, 2, D]), ALU.subtract))
                    dve.wait_ge(s["exps"], 1)
                    link(nc.vector.tensor_tensor(top[:], rows[:, 0, :], rows[:, 1, :], ALU.add))
                    link(nc.vector.reciprocal(top[:], top[:]))
                    link(nc.vector.tensor_tensor(rows[:, 1, :], rows[:, 1, :], top[:], ALU.mult))
                    link(nc.vector.tensor_scalar(rows[:, 0, :], rows[:, 1, :], -1.0, 1.0, ALU.mult, ALU.add))
                    for n in range(16, 24):
                        dve.wait_ge(ring.chunk_done, base + n + 1)
                        i, t = divmod(n - 16, 4)
                        nc.vector.tensor_copy(V[:, t, i * 512:(i + 1) * 512], ps[:, n % 6, :]).then_inc(s["dve_read"], 1)
                    for n in range(16):
                        i, t = divmod(n, 4)
                        cols = slice(i * 512, (i + 1) * 512)
                        feats = slice((i % 2) * 512, (i % 2 + 1) * 512)
                        dve.wait_ge(s["act_read"], 16 + n + 1)
                        nc.vector.tensor_tensor(LF[:, t, cols], K[:, t, cols], rows[:, 0, feats], ALU.mult).then_inc(s["f_scaled"], 1)
                        dve.wait_ge(s["f_scaled"], n + 1)
                        nc.vector.tensor_tensor(LF[:, t, cols], LF[:, t, cols], rows[:, 1, feats], ALU.add).then_inc(s["f_done"], 1)

                @block.gpsimd
                def _(pool):
                    for n in range(16):
                        i, t = divmod(n, 4)
                        cols = slice(i * 512, (i + 1) * 512)
                        pool.wait_ge(s["f_done"], n + 1)
                        nc.gpsimd.tensor_scalar(K[:, t, cols], LF[:, t, cols], -1.0, 1.0, ALU.mult, ALU.add).then_inc(s["k_done"], 1)
        ring.chunks += 40

    def recurrence(self, units, lf, kt, kall, q, v, v2, mids, out, context):
        nc, ps, H = self.nc, self.ps, self.H
        N = len(units)
        nt = NT if context else 2
        with ExitStack() as ctx:
            KE = self.sb(ctx, "k_end", [P, 2, nt, P])
            G = self.sb(ctx, "gcum", [P, 2, SEQ])
            Dm = self.sb(ctx, "gcum_mid", [P, 2, SEQ])
            QR = self.sb(ctx, "q_rel", [P, 2, SEQ])
            KR = self.sb(ctx, "k_rel", [P, 2, SEQ])
            E3 = self.sb(ctx, "exp_gcum", [P, 2, SEQ])
            QG = self.sb(ctx, "q_decayed", [P, 2, SEQ])
            VH = self.sb(ctx, "v_halves", [P, 2, 2, 2, P])
            AM = H[:, 4:6, SEQ:TT]

            def S(b, n):
                return H[:, 2 * b + n // 2, SEQ + (n % 2) * P:SEQ + (n % 2 + 1) * P]
            GC, KX, KT, ATT, CS, O, S0 = range(7)
            with stage(nc, "g_sum kx_sum kt_sum att_sum cs_sum o_sum g_copied d_done krel_done ke_done att_masked "
                           "s_chain o_done exp_done qrel_done qg_done vh_done zeroed") as (block, s):
                @block.tensor
                def _(pe):
                    def front(u):
                        h, d = units[u]
                        cum = self.c(("up64", "lo64")[d])
                        after, after_all = self.c(("xlo64", "xup64")[d]), self.c(("lower_x", "upper_x")[d])
                        if u >= 1:
                            pe.wait_ge(s["g_copied"], u)
                        for t in range(2):
                            last = nc.tensor.matmul(ps[:, GC, t * P:(t + 1) * P], lf(u, t), cum, start=True, stop=True)
                        last.then_inc(s["g_sum"], 1)
                        if u >= 1:
                            pe.wait_ge(s["exp_done"], 4 * (u - 1) + 1)
                        for t in range(2):
                            last = nc.tensor.matmul(ps[:, KX, t * P:(t + 1) * P], after, lf(u, t), start=True, stop=True)
                        if context:
                            first, second = (2, 3) if d == 0 else (3, 2)
                            nc.tensor.matmul(ps[:, KX, first * P:(first + 1) * P], after_all, lf(u, first), start=True, stop=False)
                            nc.tensor.matmul(ps[:, KX, first * P:(first + 1) * P], self.c("ones"), lf(u, second), start=False, stop=True)
                            last = nc.tensor.matmul(ps[:, KX, second * P:(second + 1) * P], after_all, lf(u, second),
                                                    start=True, stop=True)
                        last.then_inc(s["kx_sum"], 1)
                        if u >= 1:
                            pe.wait_ge(s["krel_done"], u)
                        for t in range(2):
                            last = nc.tensor.transpose(ps[:, KT, t * P:(t + 1) * P], kt(u, t), self.c("ident"))
                        last.then_inc(s["kt_sum"], 1)

                    def scores_states(u):
                        h, d = units[u]
                        pe.wait_ge(s["krel_done"], u + 1)
                        pe.wait_ge(s["qrel_done"], u + 1)
                        if u >= 1:
                            pe.wait_ge(s["att_masked"], u)
                            pe.wait_ge(s["s_chain"], 4 * u)
                        for t in range(2):
                            last = nc.tensor.matmul(ps[:, ATT, t * P:(t + 1) * P], KR[:, u % 2, t * P:(t + 1) * P],
                                                    QR[:, u % 2, t * P:(t + 1) * P], start=True, stop=True)
                        last.then_inc(s["att_sum"], 1)
                        pe.wait_ge(s["ke_done"], u + 1)
                        pe.wait_ge(s["vh_done"], u + 1)
                        for i, t in enumerate((2, 3) if context else ()):
                            nc.tensor.matmul(ps[:, S0, 0:P], KE[:, u % 2, t, :], v(u, t),
                                             start=(i == 0), stop=(i == 1))
                        for t in range(2):
                            last = nc.tensor.matmul(ps[:, CS, t * SEQ:(t + 1) * SEQ], KE[:, u % 2, t, :],
                                                    VH[:, u % 2, t, :, :].rearrange("p h v -> p (h v)"), start=True, stop=True)
                        last.then_inc(s["cs_sum"], 1)

                    def outputs(u):
                        h, d = units[u]
                        pe.wait_ge(s["att_masked"], u + 1)
                        pe.wait_ge(s["s_chain"], 4 * u + 4)
                        pe.wait_ge(s["qg_done"], u + 1)
                        if u >= 1:
                            pe.wait_ge(s["o_done"], u)
                        for t in range(2):
                            nc.tensor.matmul(ps[:, O, t * P:(t + 1) * P], v(u, t),
                                             AM[:, u % 2, t * P:(t + 1) * P], start=True, stop=False)
                            for half in range(2):
                                c = 2 * t + half
                                n = c if d == 0 else 3 - c
                                last = nc.tensor.matmul(ps[:, O, c * 64:(c + 1) * 64], S(u % 2, n),
                                                        QG[:, u % 2, c * 64:(c + 1) * 64], start=False, stop=(half == 1))
                        last.then_inc(s["o_sum"], 1)
                    front(0)
                    for u in range(N):
                        scores_states(u)
                        if u + 1 < N:
                            front(u + 1)
                        outputs(u)

                @block.scalar
                def _(act):
                    for u in range(N):
                        b = u % 2
                        act.wait_ge(s["kx_sum"], u + 1)
                        if u >= 2:
                            act.wait_ge(s["cs_sum"], u - 1)
                        nc.scalar.activation(KE[:, b, :, :].rearrange("p t k -> p (t k)"), ps[:, KX, 0:nt * P], ACT.Exp).then_inc(s["exp_done"], 1)
                        act.wait_ge(s["d_done"], u + 1)
                        if u >= 2:
                            act.wait_ge(s["att_sum"], u - 1)
                            act.wait_ge(s["s_chain"], 4 * (u - 1))
                            act.wait_ge(s["qg_done"], u - 1)
                        nc.scalar.activation(QR[:, b, :], Dm[:, b, :], ACT.Exp).then_inc(s["exp_done"], 1)
                        nc.scalar.activation(KR[:, b, :], Dm[:, b, :], ACT.Exp, scale=-1.0).then_inc(s["exp_done"], 1)
                        nc.scalar.activation(E3[:, b, :], G[:, b, :], ACT.Exp).then_inc(s["exp_done"], 1)

                @block.gpsimd
                def _(pool):
                    for u, (h, d) in enumerate(units):
                        b = u % 2
                        if u >= 2:
                            pool.wait_ge(s["cs_sum"], u - 1)
                        for half in range(2):
                            ins = nc.gpsimd.tensor_scalar(VH[:, b, :, half, :], v2(u),
                                                          self.c("half", 1, off=half), None, ALU.mult)
                        ins.then_inc(s["vh_done"], 1)
                        pool.wait_ge(s["exp_done"], 4 * u + 2)
                        nc.gpsimd.tensor_tensor(QR[:, b, :], QR[:, b, :], q(u), ALU.mult).then_inc(s["qrel_done"], 1)
                        pool.wait_ge(s["exp_done"], 4 * u + 4)
                        if u >= 2:
                            pool.wait_ge(s["o_sum"], u - 1)
                        nc.gpsimd.tensor_tensor(QG[:, b, :], E3[:, b, :], q(u), ALU.mult).then_inc(s["qg_done"], 1)

                @block.vector
                def _(dve):
                    def gates(u):
                        h, d = units[u]
                        b = u % 2
                        dve.wait_ge(s["g_sum"], u + 1)
                        if u >= 2:
                            dve.wait_ge(s["exp_done"], 4 * (u - 1))
                        nc.vector.tensor_copy(G[:, b, :], ps[:, GC, 0:SEQ]).then_inc(s["g_copied"], 1)
                        dve.wait_ge(s["g_copied"], u + 1)
                        g = G[:, b, :].rearrange("p (c t) -> p c t", t=64)
                        mid = mids[d]
                        nc.vector.tensor_tensor(Dm[:, b, :].rearrange("p (c t) -> p c t", t=64), g,
                                                g[:, :, mid:mid + 1].to_broadcast([P, 4, 64]), ALU.subtract).then_inc(s["d_done"], 1)
                        dve.wait_ge(s["exp_done"], 4 * u + 1)
                        nc.vector.tensor_tensor(KE[:, b, :, :], KE[:, b, :, :], kall(u),
                                                ALU.mult).then_inc(s["ke_done"], 1)
                        dve.wait_ge(s["exp_done"], 4 * u + 3)
                        dve.wait_ge(s["kt_sum"], u + 1)
                        nc.vector.tensor_tensor(KR[:, b, :], KR[:, b, :], ps[:, KT, 0:SEQ], ALU.mult).then_inc(s["krel_done"], 1)

                    def mask_and_states(u):
                        h, d = units[u]
                        b = u % 2
                        dve.wait_ge(s["att_sum"], u + 1)
                        if u >= 2:
                            dve.wait_ge(s["o_sum"], u - 1)
                        nc.vector.copy_predicated(AM[:, b, :].rearrange("p (t l) -> p t l", t=2),
                                                  self.c(("up64", "lo64")[d]).bitcast(U32).unsqueeze(1).to_broadcast([P, 2, P]),
                                                  ps[:, ATT, 0:SEQ].rearrange("p (t l) -> p t l", t=2)).then_inc(s["att_masked"], 1)
                        dve.wait_ge(s["cs_sum"], u + 1)
                        if context:
                            nc.vector.tensor_copy(S(b, 0), ps[:, S0, 0:P]).then_inc(s["s_chain"], 1)
                        else:
                            nc.vector.memset(S(b, 0), 0.0).then_inc(s["s_chain"], 1)
                        dve.wait_ge(s["exp_done"], 4 * u + 4)
                        for n in range(3):
                            c = n if d == 0 else 3 - n
                            end = c * 64 + (63 if d == 0 else 0)
                            dve.wait_ge(s["s_chain"], 4 * u + n + 1)
                            nc.vector.scalar_tensor_tensor(out=S(b, n + 1), in0=S(b, n), scalar=E3[:, b, end:end + 1],
                                                           in1=ps[:, CS, c * P:(c + 1) * P], op0=ALU.mult,
                                                           op1=ALU.add).then_inc(s["s_chain"], 1)

                    def take_outputs(u):
                        h, d = units[u]
                        dve.wait_ge(s["o_sum"], u + 1)
                        if d == 0:
                            nc.vector.tensor_copy(out(u), ps[:, O, 0:SEQ]).then_inc(s["o_done"], 1)
                        else:
                            dve.wait_ge(s["o_done"], u)
                            nc.vector.tensor_tensor(out(u), out(u), ps[:, O, 0:SEQ], ALU.add).then_inc(s["o_done"], 1)
                    nc.vector.memset(AM, 0.0).then_inc(s["zeroed"], 1)
                    dve.wait_ge(s["zeroed"], 1)
                    gates(0)
                    for u in range(N):
                        mask_and_states(u)
                        if u + 1 < N:
                            gates(u + 1)
                        take_outputs(u)

    def head_norm_gate(self, O, pairs, scale, G):
        nc, ps = self.nc, self.ps
        with ExitStack() as ctx:
            sq = self.sb(ctx, "head_squares", [P, pairs, 2, SEQ])
            root = self.sb(ctx, "head_root", [P, pairs, 2, SEQ])
            with stage(nc, "squared summed rooted inverted scaled gated") as (block, s):
                @block.scalar
                def _(act):
                    for j in range(pairs):
                        nc.scalar.activation(sq[:, j, :, :], O(j), ACT.Square).then_inc(s["squared"], 1)
                    for j in range(pairs):
                        act.wait_ge(s["summed"], j + 1)
                        nc.scalar.activation(root[:, j, :, :], ps[:, j, :].rearrange("p (h t) -> p h t", h=2), ACT.Sqrt,
                                             bias=self.eps[:, 0:1], scale=1.0 / P).then_inc(s["rooted"], 1)

                @block.tensor
                def _(pe):
                    for j in range(pairs):
                        pe.wait_ge(s["squared"], j + 1)
                        nc.tensor.matmul(ps[:, j, :], self.c("ones"), sq[:, j, :, :].rearrange("p h t -> p (h t)"),
                                         start=True, stop=True).then_inc(s["summed"], 1)

                @block.vector
                def _(dve):
                    for j in range(pairs):
                        dve.wait_ge(s["rooted"], j + 1)
                        nc.vector.reciprocal(root[:, j, :, :], root[:, j, :, :]).then_inc(s["inverted"], 1)
                        dve.wait_ge(s["inverted"], j + 1)
                        nc.vector.scalar_tensor_tensor(out=O(j), in0=O(j), scalar=scale, in1=root[:, j, :, :],
                                                       op0=ALU.mult, op1=ALU.mult).then_inc(s["scaled"], 1)
                        dve.wait_ge(s["scaled"], j + 1)
                        nc.vector.tensor_tensor(O(j), O(j), G(j), ALU.mult).then_inc(s["gated"], 1)

    def odd_mixer(self):
        with ExitStack() as ctx:
            Q = self.sb(ctx, "q", [P, 8, SEQ])
            G = self.sb(ctx, "g", [P, 8, SEQ])
            V = self.sb(ctx, "v", [P, NT, D])
            K = self.sb(ctx, "k", [P, NT, 2 * D])
            LF = self.sb(ctx, "log_f", [P, NT, 2 * D])
            self.odd_in(Q, G, V, K, LF)
            units = [(h, d) for h in range(8) for d in range(2)]

            def cols(u):
                h, d = units[u]
                return slice(d * D + h * P, d * D + (h + 1) * P)

            def head(u):
                return slice(units[u][0] * P, (units[u][0] + 1) * P)
            self.recurrence(units, lf=lambda u, t: LF[:, t, cols(u)], kt=lambda u, t: K[:, t, cols(u)],
                            kall=lambda u: K[:, :, cols(u)], q=lambda u: Q[:, units[u][0], :],
                            v=lambda u, t: V[:, t, head(u)], v2=lambda u: V[:, 0:2, head(u)], mids=(31, 32),
                            out=lambda u: self.H[:, units[u][0], 0:SEQ], context=True)
            self.head_norm_gate(lambda j: self.H[:, 2 * j:2 * j + 2, 0:SEQ], 4, self.v("hg_g"), lambda j: G[:, 2 * j:2 * j + 2, :])
        self.out_projection("AB", KD, lambda k: self.H[:, k, 0:SEQ], 1, SEQ, permuted=True)

    def feed_forward(self, n):
        nc, ring, ps, X, d = self.nc, self.ring, self.ps, self.X, self.d
        T = slice(0, SEQ)
        self.rms_norm(self.x_chunk, self.h_chunk, KD, SEQ, lambda k, c: self.v("ffn_norm2", 8 * n + k))
        base = ring.chunks
        used = {a: ring.used[a] for a in "ABCD"}
        BLOCKS, ROUNDS, AHEAD = 11, 5, 3
        row0 = BLOCKS * n
        DONE = [1, 2, 3, 4, 8, 12, 13, 14, 15, 16, 20, 24]
        KIND = [("gu", 1, i) for i in range(4)] + [("down", 0, i) for i in range(2)] \
            + [("gu", 2, i) for i in range(4)] + [("down", 1, i) for i in range(2)]
        with ExitStack() as ctx:
            xh = self.sb(ctx, "x_hi", [P, KD, SEQ], F32R)
            xl = self.sb(ctx, "x_lo", [P, KD, SEQ], F32R)
            self.split_input(SEQ, xh, xl)
            wh = self.sb(ctx, "w_hi", [P, 4, 1024], F32R)
            wl = self.sb(ctx, "w_lo", [P, 4, 1024], F32R)
            sg = self.sb(ctx, "silu_gate", [P, 2, SEQ])
            hraw = self.sb(ctx, "hidden_raw", [P, 2, SEQ])
            hh = self.sb(ctx, "hidden_hi", [P, 2, 2, SEQ], F32R)
            hl = self.sb(ctx, "hidden_lo", [P, 2, 2, SEQ], F32R)

            def raw(kind, b, i, slot):
                if kind == "gu":
                    area = "AB"[b]
                    c, what = divmod(i, 2)
                    src = ring.buf[area][:].rearrange("p (k w n) -> p k w n", k=KD, w=2)[:, :, what, c * P:(c + 1) * P]
                    return area, src, lambda w: w[:, slot, :].rearrange("p (k n) -> p k n", k=KD)
                area = "CD"[b]
                src = ring.buf[area][:].rearrange("p (k n) -> p k n", k=2)[:, :, i * 512:(i + 1) * 512]
                return area, src, lambda w: w[:, slot, :].rearrange("p (k n) -> p k n", k=2)

            with stage(nc, "hi_done lo_done silu_done hraw_done hh_done hid_done added") as (block, s):
                @block.sync
                def _(sp):
                    ring.load(sp, "A", 4, s["lo_done"])
                    with sp.Fori(0, ROUNDS - 1) as i:
                        for area, last, src in (("B", 3, d["ffn_gu"][i * 2 + (row0 + 3)]), ("C", 5, d["ffn_down"][i * 2 + (row0 + 2)]),
                                                ("A", 9, d["ffn_gu"][i * 2 + (row0 + 4)]), ("D", 11, d["ffn_down"][i * 2 + (row0 + 3)])):
                            sp.wait_ge(s["lo_done"], i * 12 + (4 + last + 1))
                            sp.dma_start(ring.buf[area][:], src).then_inc(ring.landed[area], 16)
                    for a in "ABCD":
                        ring.sent[a] += ROUNDS - 1
                    for area, last in (("B", 3), ("C", 5), ("A", 9), ("D", 11), ("C", 13)):
                        ring.load(sp, area, 4 + 12 * (ROUNDS - 1) + last + 1, s["lo_done"])

                def steps(eng, ahead, now):
                    for q in range(AHEAD):
                        ahead(-1, 8 + q)
                    for l in range(8, 12):
                        ahead(-1, l + AHEAD) if l + AHEAD < 12 else ahead(0, l + AHEAD - 12)
                        now(-1, l)

                    def one(i, last):
                        for l in range(12):
                            q = l + AHEAD
                            if q < 12:
                                ahead(i, q)
                            elif not last:
                                ahead(i + 1, q - 12)
                            elif q < 14:
                                ahead(ROUNDS, q - 12 + 4)
                            now(i, l)
                    with eng.Fori(0, ROUNDS - 1) as i:
                        one(i, False)
                    one(ROUNDS - 1, True)
                    now(ROUNDS, 4)
                    now(ROUNDS, 5)

                def place(i, l):
                    if isinstance(i, int) and i == -1:
                        return "gu", 0, l - 8, l - 8 + 1, base + l - 8 + 1, None
                    if isinstance(i, int) and i == ROUNDS:
                        n_ = 4 + 12 * ROUNDS + l - 4
                        before = base + 4 + 24 * (ROUNDS - 1) + DONE[l + 4]
                        return "down", 0, l - 4, n_ + 1, base + 4 + 24 * ROUNDS + 4 * (l - 3), before
                    kind, block_, piece = KIND[l]
                    if l >= 4:
                        before = i * 24 + (base + 4 + DONE[l - 4])
                    elif isinstance(i, int) and i == 0:
                        before = base + l + 1
                    else:
                        before = i * 24 + (base + 4 - 24 + DONE[l + 8])
                    return kind, block_ % 2, piece, i * 12 + (4 + l + 1), i * 24 + (base + 4 + DONE[l]), before

                def block_of(i, l):
                    if isinstance(i, int) and i == -1:
                        return 0
                    if isinstance(i, int) and i == ROUNDS:
                        return 2 * (BLOCKS - 1)
                    return i * 4 + 2 * KIND[l][1]

                def slot(i, l):
                    return l % 4

                @block.scalar
                def _(act):
                    def hi(i, l):
                        kind, b, piece, n_, done_, before = place(i, l)
                        if before is not None:
                            act.wait_ge(ring.chunk_done, before)
                        area, src, dst = raw(kind, b, piece, slot(i, l))
                        if piece == 0:
                            act.wait_ge(ring.landed[area], landing(i, l, area))
                        nc.scalar.activation(dst(wh), src, ACT.Copy).then_inc(s["hi_done"], 1)

                    def landing(i, l, area):
                        if isinstance(i, int) and i == -1:
                            return 16 * (used["A"] + 1)
                        return i * 16 + 16 * (used[area] + (2 if area == "A" else 1))

                    def silu(i, l):
                        kind, b, piece, n_, done_, before = place(i, l)
                        if kind == "gu" and piece % 2 == 0:
                            c = piece // 2
                            act.wait_ge(ring.chunk_done, done_)
                            if not (isinstance(i, int) and i == -1):
                                act.wait_ge(s["hraw_done"], block_of(i, l) - 1 + c)
                            nc.scalar.activation(sg[:, c, :], ps[:, c, T], ACT.Silu).then_inc(s["silu_done"], 1)
                    steps(act, hi, silu)

                @block.vector
                def _(dve):
                    def lo(i, l):
                        kind, b, piece, n_, done_, before = place(i, l)
                        dve.wait_ge(s["hi_done"], n_)
                        area, src, dst = raw(kind, b, piece, slot(i, l))
                        nc.vector.tensor_tensor(dst(wl), src, dst(wh).bitcast(F32), ALU.subtract).then_inc(s["lo_done"], 1)

                    def results(i, l):
                        kind, b, piece, n_, done_, before = place(i, l)
                        j2 = block_of(i, l)
                        if kind == "gu" and piece % 2:
                            c = piece // 2
                            dve.wait_ge(ring.chunk_done, done_)
                            dve.wait_ge(s["silu_done"], j2 + c + 1)
                            nc.vector.tensor_tensor(hraw[:, c, :], ps[:, 2 + c, T], sg[:, c, :], ALU.mult).then_inc(s["hraw_done"], 1)
                            dve.wait_ge(s["hraw_done"], j2 + c + 1)
                            nc.vector.tensor_copy(hh[:, b, c, :], hraw[:, c, :]).then_inc(s["hh_done"], 1)
                            dve.wait_ge(s["hh_done"], j2 + c + 1)
                            nc.vector.tensor_tensor(hl[:, b, c, :], hraw[:, c, :], hh[:, b, c, :].bitcast(F32),
                                                    ALU.subtract).then_inc(s["hid_done"], 1)
                        if kind == "down":
                            for m in range(4 * piece, 4 * piece + 4):
                                dve.wait_ge(ring.chunk_done, done_ - 3 + m % 4)
                                dve.wait_ge(s["added"], j2 * 4 + 1)
                                nc.vector.scalar_tensor_tensor(out=X[:, m, T], in0=ps[:, 4 + m % 4, T], scalar=0.5, in1=X[:, m, T],
                                                               op0=ALU.mult, op1=ALU.add).then_inc(s["added"], 1)
                    self.credit(nc.vector, s["added"], 2)
                    steps(dve, lo, results)

                @block.tensor
                def _(pe):
                    def nothing(i, l):
                        pass

                    def products(i, l):
                        kind, b, piece, n_, done_, before = place(i, l)
                        j2 = block_of(i, l)
                        sl = slot(i, l)
                        pe.wait_ge(s["lo_done"], n_)
                        if kind == "gu":
                            c, what = divmod(piece, 2)
                            if not (isinstance(i, int) and i == -1):
                                pe.wait_ge(s["silu_done"] if what == 0 else s["hraw_done"], j2 - 1 + c)
                            for k in range(KD):
                                w = slice(k * P, (k + 1) * P)
                                last = self.product(ps[:, 2 * what + c, T], wh[:, sl, w], wl[:, sl, w], xh[:, k, :], xl[:, k, :],
                                                    k == 0, k == KD - 1)
                            last.then_inc(ring.chunk_done, 1)
                            return
                        for m in range(4 * piece, 4 * piece + 4):
                            pe.wait_ge(s["added"], j2 * 4 + (m - 3 if m >= 4 else 0) + 1)
                            for k in range(2):
                                if m == 0:
                                    pe.wait_ge(s["hid_done"], j2 + k + 1)
                                w = slice(k * 512 + (m % 4) * P, k * 512 + (m % 4 + 1) * P)
                                last = self.product(ps[:, 4 + m % 4, T], wh[:, sl, w], wl[:, sl, w], hh[:, b, k, :], hl[:, b, k, :],
                                                    k == 0, k == 1)
                            last.then_inc(ring.chunk_done, 1)
                    steps(pe, nothing, products)
        for a, k in (("A", 6), ("B", 5), ("C", 6), ("D", 5)):
            ring.used[a] += k
        ring.chunks += 12 * BLOCKS

    def rope_tables(self, cos, sin, column):
        nc = self.nc
        MAGIC = float(1.5 * 2 ** 23)
        parts = TWO_PI_PARTS
        with ExitStack() as ctx:
            pos = self.sb(ctx, "positions", [P, SEQ], mybir.dt.int32)
            ang = self.sb(ctx, "angle", [P, SEQ])
            turns = self.sb(ctx, "turns", [P, SEQ])
            with stage(nc, "pos_in link sines") as (block, s):
                @block.sync
                def _(sp):
                    sp.dma_start(pos[:], self.d["positions"].partition_broadcast(P)).then_inc(s["pos_in"], 16)

                @block.vector
                def _(dve):
                    link = chain(dve, s["link"])
                    V = nc.vector
                    dve.wait_ge(s["pos_in"], 16)
                    link(V.tensor_copy(ang[:], pos[:]))
                    link(V.tensor_scalar(ang[:], ang[:], self.c("ropef", 1, off=column), None, ALU.mult))
                    for out, quarter in ((sin, 0.0), (cos, 0.25)):
                        link(V.tensor_scalar(turns[:], ang[:], float(1 / (2 * np.pi)), quarter, ALU.mult, ALU.add))
                        link(V.tensor_scalar(turns[:], turns[:], MAGIC, None, ALU.add))
                        link(V.tensor_scalar(turns[:], turns[:], MAGIC, None, ALU.subtract))
                        link(V.scalar_tensor_tensor(out=out, in0=turns[:], scalar=-parts[0], in1=ang[:], op0=ALU.mult, op1=ALU.add))
                        for part in parts[1:]:
                            link(V.scalar_tensor_tensor(out=out, in0=turns[:], scalar=-part, in1=out, op0=ALU.mult, op1=ALU.add))
                        if quarter:
                            link(V.tensor_scalar(out, out, float(np.float32(np.pi / 2)), None, ALU.add))
                        link(V.tensor_scalar(out, out, PI_BELOW, -PI_BELOW, ALU.min, ALU.max))

                @block.scalar
                def _(act):
                    act.wait_ge(s["link"], 2 + 7 + 8)
                    nc.scalar.activation(sin, sin, ACT.Sin).then_inc(s["sines"], 1)
                    nc.scalar.activation(cos, cos, ACT.Sin).then_inc(s["sines"], 1)

    def rotate(self, jobs, cos, sin, swap):
        nc, ps = self.nc, self.ps
        with ExitStack() as ctx:
            part = self.sb(ctx, "rotated", [P, 2, 2, SEQ])
            with stage(nc, "swapped sin_done cos_done done") as (block, s):
                def wide(t, n):
                    return t.unsqueeze(1).to_broadcast([P, n, SEQ])

                @block.tensor
                def _(pe):
                    for i, x in enumerate(jobs):
                        n = x.shape[1]
                        if i >= 2:
                            pe.wait_ge(s["sin_done"], i - 1)
                        for c in range(n):
                            last = nc.tensor.matmul(ps[:, i % 2, c * SEQ:(c + 1) * SEQ], swap, x[:, c, :], start=True, stop=True)
                        last.then_inc(s["swapped"], 1)

                @block.vector
                def _(dve):
                    for i, x in enumerate(jobs):
                        n = x.shape[1]
                        dve.wait_ge(s["swapped"], i + 1)
                        if i >= 2:
                            dve.wait_ge(s["done"], i - 1)
                        nc.vector.tensor_tensor(part[:, i % 2, 0:n, :], ps[:, i % 2, 0:n * SEQ].rearrange("p (n t) -> p n t", n=n),
                                                wide(sin, n), ALU.mult).then_inc(s["sin_done"], 1)
                        dve.wait_ge(s["cos_done"], i + 1)
                        dve.wait_ge(s["sin_done"], i + 1)
                        nc.vector.tensor_tensor(x, x, part[:, i % 2, 0:n, :], ALU.add).then_inc(s["done"], 1)

                @block.gpsimd
                def _(pool):
                    for i, x in enumerate(jobs):
                        n = x.shape[1]
                        pool.wait_ge(s["swapped"], i + 1)
                        nc.gpsimd.tensor_tensor(x, x, wide(cos, n), ALU.mult).then_inc(s["cos_done"], 1)

    def attention(self, heads, q, keys, values, scale, out, compressed=None, weights=None):
        nc, ps = self.nc, self.ps
        nb = keys(0).shape[1]
        NC = 15
        comp0 = nb * SEQ
        width = comp0 + (P if compressed else 0)
        na = nb + (1 if compressed else 0)
        units = [(h, t) for h in range(heads) for t in range(2)]
        N = len(units)
        with ExitStack() as ctx:
            PR = self.sb(ctx, "probs", [P, 2, width])
            PT = self.sb(ctx, "probs_t", [P, 2, width])
            negmax = self.sb(ctx, "neg_max", [P, 2, 4])
            total = self.sb(ctx, "total", [P, 2, 4])
            with stage(nc, "scores_done masked maxed exp_done link scaled transposed pt_copied summed o_copied") as (block, s):
                def wide(t):
                    return (t + 1) * P

                def pieces(u):
                    h, t = units[u]
                    all_ = [(b * SEQ + kt * P, values(h, b, kt)) for b in range(nb) for kt in range(t + 1)]
                    if compressed:
                        all_.append((comp0, compressed[1](h)))
                    return all_

                @block.tensor
                def _(pe):
                    def scores(u):
                        h, t = units[u]
                        if u >= 2:
                            pe.wait_ge(s["masked"], u - 1)
                        W = wide(t)
                        for b in range(nb):
                            last = nc.tensor.matmul(ps[:, u % 2, b * SEQ:b * SEQ + W], q(h)[:, t * P:(t + 1) * P],
                                                    keys(h)[:, b, 0:W], start=True, stop=True)
                        if compressed:
                            last = nc.tensor.matmul(ps[:, 2 + u % 2, 0:NC], q(h)[:, t * P:(t + 1) * P], compressed[0](h),
                                                    start=True, stop=True)
                        last.then_inc(s["scores_done"], 1)

                    def transposes(u):
                        pe.wait_ge(s["scaled"], u + 1)
                        if u >= 1:
                            pe.wait_ge(s["pt_copied"], u)
                        for i, (col, _) in enumerate(pieces(u)):
                            last = nc.tensor.transpose(ps[:, 4 + i // 4, (i % 4) * P:(i % 4 + 1) * P],
                                                       PR[:, u % 2, col:col + P], self.c("ident"))
                        last.then_inc(s["transposed"], 1)

                    def product(u):
                        h, t = units[u]
                        pe.wait_ge(s["pt_copied"], u + 1)
                        if u >= 2:
                            pe.wait_ge(s["o_copied"], u - 1)
                        lo = 64 * (h % 2)
                        js = pieces(u)
                        for i, (_, val) in enumerate(js):
                            last = nc.tensor.matmul(ps[lo:lo + 64, 6 + u % 2, 0:P], val, PT[:, u % 2, i * P:(i + 1) * P],
                                                    start=(i == 0), stop=(i == len(js) - 1))
                        last.then_inc(s["summed"], 1)
                    scores(0)
                    scores(1)
                    for u in range(N):
                        transposes(u)
                        if u + 2 < N:
                            scores(u + 2)
                        product(u)

                @block.vector
                def _(dve):
                    V = nc.vector
                    linked = [0]

                    def link(ins):
                        linked[0] += 1
                        ins.then_inc(s["link"], 1)
                        dve.wait_ge(s["link"], linked[0])

                    def mask_and_max(u):
                        h, t = units[u]
                        W, b2 = wide(t), u % 2
                        dve.wait_ge(s["scores_done"], u + 1)
                        if u >= 2:
                            dve.wait_ge(s["transposed"], u - 1)
                        pr = PR[:, b2, 0:comp0].rearrange("p (b k) -> p b k", b=nb)[:, :, 0:W]
                        sc = ps[:, u % 2, 0:comp0].rearrange("p (b k) -> p b k", b=nb)[:, :, 0:W]
                        if compressed:
                            link(V.scalar_tensor_tensor(out=PR[:, b2, comp0:comp0 + NC], in0=ps[:, 2 + u % 2, 0:NC], scalar=scale,
                                                        in1=self.c("cmp_add", NC, off=16 * t), op0=ALU.mult, op1=ALU.add))
                        V.scalar_tensor_tensor(out=pr, in0=sc, scalar=scale,
                                               in1=self.c("causal_add", W, off=P * (1 - t)).unsqueeze(1).to_broadcast([P, nb, W]),
                                               op0=ALU.mult, op1=ALU.add).then_inc(s["masked"], 1)
                        dve.wait_ge(s["masked"], u + 1)
                        if u >= 2:
                            dve.wait_ge(s["exp_done"], na * (u - 1))
                        if compressed:
                            V.tensor_reduce(negmax[:, b2, nb:nb + 1], PR[:, b2, comp0:comp0 + NC], AX.X, ALU.max, negate=True)
                        V.tensor_reduce(negmax[:, b2, 0:nb], pr, AX.X, ALU.max, negate=True).then_inc(s["maxed"], 1)

                    def normalise(u):
                        h, t = units[u]
                        W, b2 = wide(t), u % 2
                        dve.wait_ge(s["exp_done"], na * (u + 1))
                        pr = PR[:, b2, 0:comp0].rearrange("p (b k) -> p b k", b=nb)[:, :, 0:W]
                        tt = total[:, b2, 0:na]
                        if compressed:
                            pc = PR[:, b2, comp0:comp0 + NC]
                            link(V.tensor_tensor(pc, pc, self.c("cmp_mask", NC, off=16 * t), ALU.mult))
                            link(V.tensor_reduce(total[:, b2, nb:nb + 1], pc, AX.X, ALU.add))
                        link(V.tensor_scalar(tt, tt, 1e-30, None, ALU.max))
                        link(V.reciprocal(tt, tt))
                        if weights:
                            link(V.tensor_tensor(tt, tt, weights(h, t), ALU.mult))
                        if compressed:
                            V.tensor_scalar(pc, pc, total[:, b2, nb:nb + 1], None, ALU.mult)
                        V.tensor_tensor(pr, pr, total[:, b2, 0:nb].unsqueeze(2).to_broadcast([P, nb, W]), ALU.mult).then_inc(s["scaled"], 1)
                    if compressed:
                        link(V.memset(PR[:], 0.0))
                    mask_and_max(0)
                    for u in range(N):
                        if u + 1 < N:
                            mask_and_max(u + 1)
                        normalise(u)

                @block.scalar
                def _(act):
                    def exps(u):
                        h, t = units[u]
                        W, b2 = wide(t), u % 2
                        act.wait_ge(s["maxed"], u + 1)
                        if u >= 2:
                            act.wait_ge(s["scaled"], u - 1)
                        for b in range(nb):
                            pr = PR[:, b2, b * SEQ:b * SEQ + W]
                            nc.scalar.activation(pr, pr, ACT.Exp, bias=negmax[:, b2, b:b + 1],
                                                 accum_out=total[:, b2, b:b + 1]).then_inc(s["exp_done"], 1)
                        if compressed:
                            pc = PR[:, b2, comp0:comp0 + NC]
                            nc.scalar.activation(pc, pc, ACT.Exp, bias=negmax[:, b2, nb:nb + 1]).then_inc(s["exp_done"], 1)

                    def copy_transposed(u):
                        n = len(pieces(u))
                        act.wait_ge(s["transposed"], u + 1)
                        if u >= 2:
                            act.wait_ge(s["summed"], u - 1)
                        m = min(n, 4)
                        ins = nc.scalar.activation(PT[:, u % 2, 0:m * P], ps[:, 4, 0:m * P], ACT.Copy)
                        if n > 4:
                            ins = nc.scalar.activation(PT[:, u % 2, 4 * P:5 * P], ps[:, 5, 0:P], ACT.Copy)
                        ins.then_inc(s["pt_copied"], 1)

                    def copy_output(u):
                        h, t = units[u]
                        lo = 64 * (h % 2)
                        act.wait_ge(s["summed"], u + 1)
                        nc.scalar.activation(out(h)[lo:lo + 64, t * P:(t + 1) * P], ps[lo:lo + 64, 6 + u % 2, 0:P],
                                             ACT.Copy).then_inc(s["o_copied"], 1)
                    exps(0)
                    for u in range(N):
                        if u + 1 < N:
                            exps(u + 1)
                        copy_transposed(u)
                        if u >= 1:
                            copy_output(u - 1)
                    copy_output(N - 1)

    def hybrid_mixer(self):
        nc, ring, ps, H = self.nc, self.ring, self.ps, self.H
        base = ring.chunks
        GAC = 3
        with ExitStack() as ctx:
            C = self.sb(ctx, "latents", [P, 4, SEQ])
            GR = self.sb(ctx, "gla_gate", [P, 4, SEQ])
            GQ = self.sb(ctx, "gla_q", [P, 4, SEQ])
            GK = self.sb(ctx, "gla_k", [P, 2, SEQ])
            GV = self.sb(ctx, "gla_v", [P, 2, 512])
            LA = self.sb(ctx, "gla_log_a", [P, 2, SEQ])
            uq = self.sb(ctx, "w_uq", [P, 2, D])
            uk = self.sb(ctx, "w_uk", [P, D])
            uv = self.sb(ctx, "w_uv", [P, 512])
            a2 = self.sb(ctx, "w_a2", [P, SEQ])
            ba = self.sb(ctx, "gla_bias", [P, SEQ])
            mag = self.sb(ctx, "gla_mag", [P, 2, SEQ])
            low = self.sb(ctx, "gla_low", [P, 2, SEQ])
            with stage(nc, "loaded act_read dve_read a_sum link prep") as (block, s):
                areas = "BABA"

                @block.sync
                def _(sp):
                    for dst, name in ((uq[:].rearrange("p k n -> p (k n)"), "w_uq"), (uk[:], "w_uk"), (uv[:], "w_uv"), (a2[:], "w_a2")):
                        sp.dma_start(dst, self.d[name]).then_inc(s["loaded"], 16)
                    sp.dma_start(ba[:], self.d["gla_ba"].partition_broadcast(P)).then_inc(s["loaded"], 16)
                    for i, area in enumerate(areas):
                        ring.load(sp, area, base + (4 * (i + 1) if i < 3 else 14))

                @block.tensor
                def _(pe):
                    for i in range(2):
                        self.panel_products(pe, None, areas[i], KD, 512, lambda k: H[:, k, 0:SEQ], 4 * i, range(8), SEQ, lambda n: None)
                    for i in (2, 3):
                        area = areas[i]
                        ring.arrived(pe, area)
                        if i == 2:
                            for m in range(2):
                                pe.wait_ge(s["dve_read"], m + 1)
                                for k in range(KD):
                                    last = nc.tensor.matmul(ps[:, m, 0:SEQ], ring.buf[area][:, k * 512 + m * P:k * 512 + (m + 1) * P],
                                                            H[:, k, 0:SEQ], start=(k == 0), stop=(k == KD - 1))
                                last.then_inc(ring.chunk_done, 1)
                        cols = slice(SEQ, 512) if i == 2 else slice(0, 512)
                        for t in range(2):
                            bank = 2 + t if i == 2 else 4 + t
                            if i == 2:
                                pe.wait_ge(s["dve_read"], 3 + t)
                            else:
                                pe.wait_ge(s["act_read"], t + 1)
                            for k in range(KD):
                                last = nc.tensor.matmul(ps[:, bank, 0:cols.stop - cols.start], H[:, k, t * P:(t + 1) * P],
                                                        ring.buf[area][:, k * 512 + cols.start:k * 512 + cols.stop],
                                                        start=(k == 0), stop=(k == KD - 1))
                            last.then_inc(ring.chunk_done, 1)
                    pe.wait_ge(s["loaded"], 80)
                    pe.wait_ge(s["dve_read"], 4)
                    pe.wait_ge(s["act_read"], 4)
                    for t in range(2):
                        last = nc.tensor.matmul(ps[:, 6, t * SEQ:(t + 1) * SEQ], C[:, GAC, t * P:(t + 1) * P], a2[:], start=True, stop=True)
                    last.then_inc(s["a_sum"], 1)

                @block.scalar
                def _(act):
                    for m in range(4):
                        act.wait_ge(ring.chunk_done, base + 5 + m)
                        nc.scalar.activation(GR[:, m, :], ps[:, 4 + m, 0:SEQ], ACT.Silu).then_inc(s["act_read"], 1)
                    act.wait_ge(s["prep"], 1)
                    nc.scalar.activation(mag[:], mag[:], ACT.Exp).then_inc(s["prep"], 1)
                    act.wait_ge(s["prep"], 2)
                    nc.scalar.activation(mag[:], mag[:], ACT.Ln, bias=1.0).then_inc(s["prep"], 1)

                @block.vector
                def _(dve):
                    link = chain(dve, s["link"])
                    V = nc.vector
                    for m in range(4):
                        dve.wait_ge(ring.chunk_done, base + m + 1)
                        V.tensor_copy(C[:, m, :], ps[:, m, 0:SEQ]).then_inc(s["dve_read"], 1)
                    for m in range(2):
                        dve.wait_ge(ring.chunk_done, base + 9 + m)
                        for half in range(2):
                            V.tensor_scalar(GQ[:, 2 * m + half, :], ps[:, m, 0:SEQ], self.c("half", 1, off=half), 0.125,
                                            ALU.mult, ALU.mult).then_inc(s["dve_read"], 1)
                    for t in range(2):
                        dve.wait_ge(ring.chunk_done, base + 11 + t)
                        V.tensor_copy(GK[:, t, :], ps[:, 2 + t, 0:SEQ]).then_inc(s["dve_read"], 1)
                    for t in range(2):
                        dve.wait_ge(ring.chunk_done, base + 13 + t)
                        V.tensor_copy(GV[:, t, :], ps[:, 4 + t, :]).then_inc(s["dve_read"], 1)
                    dve.wait_ge(s["loaded"], 80)
                    dve.wait_ge(s["a_sum"], 1)
                    link(V.tensor_tensor(LA[:], ps[:, 6, :].rearrange("p (t n) -> p t n", t=2),
                                         ba[:].unsqueeze(1).to_broadcast([P, 2, SEQ]), ALU.add))
                    link(V.tensor_scalar(low[:], LA[:], 0.0, None, ALU.min))
                    V.scalar_tensor_tensor(out=mag[:], in0=low[:], scalar=2.0, in1=LA[:], op0=ALU.mult,
                                           op1=ALU.subtract).then_inc(s["prep"], 1)
                    dve.wait_ge(s["prep"], 3)
                    link(V.tensor_tensor(LA[:], low[:], mag[:], ALU.subtract))
                    link(V.tensor_scalar(LA[:], LA[:], 1.0 / 16.0, None, ALU.mult))
            ring.chunks += 14

            with ExitStack() as gla:
                spec = dict(units=[(h, 0) for h in range(4)], lf=lambda u, t: LA[:, t, (u // 2) * P:(u // 2 + 1) * P],
                            kt=lambda u, t: GK[:, t, (u // 2) * P:(u // 2 + 1) * P],
                            kall=lambda u: GK[:, 0:2, (u // 2) * P:(u // 2 + 1) * P],
                            q=lambda u: GQ[:, u, :], v=lambda u, t: GV[:, t, u * P:(u + 1) * P],
                            v2=lambda u: GV[:, 0:2, u * P:(u + 1) * P], mids=(63, 0), out=lambda u: H[:, 4 + u, 0:SEQ], context=False)
                self.recurrence(**spec)
            self.head_norm_gate(lambda j: H[:, 4 + 2 * j:6 + 2 * j, 0:SEQ], 2, self.v("gla_g"), lambda j: GR[:, 2 * j:2 * j + 2, :])

            cq = lambda k, t: C[:, k, t]
            self.rms_norm(cq, cq, 2, SEQ, lambda k, c: self.v("q_norm", k))
            ckv = lambda k, t: C[:, 2, t]
            self.rms_norm(ckv, ckv, 1, SEQ, lambda k, c: self.v("kv_norm"))
            Q = self.sb(ctx, "mla_q", [P, 8, SEQ])
            K = self.sb(ctx, "mla_k", [P, 8, SEQ])
            V_ = self.sb(ctx, "mla_v", [P, 2, 512])
            KR = self.sb(ctx, "mla_k_rot", [P, 1, SEQ])
            cos = self.sb(ctx, "cos", [P, SEQ])
            sin = self.sb(ctx, "sin", [P, SEQ])
            with stage(nc, "products act_read dve_read kr_done") as (block, s):
                @block.tensor
                def _(pe):
                    for h in range(8):
                        for j in range(2):
                            bank = 2 * (h % 2) + j
                            if h >= 2:
                                pe.wait_ge(s["act_read"] if j == 0 else s["dve_read"], h - 1)
                            if j == 0:
                                for k in range(2):
                                    last = nc.tensor.matmul(ps[:, bank, 0:SEQ], uq[:, k, h * P:(h + 1) * P], C[:, k, :],
                                                            start=(k == 0), stop=(k == 1))
                            else:
                                last = nc.tensor.matmul(ps[:, bank, 0:SEQ], uk[:, h * P:(h + 1) * P], C[:, 2, :], start=True, stop=True)
                            last.then_inc(s["products"], 1)
                    for t in range(2):
                        nc.tensor.matmul(ps[:, 4 + t, :], C[:, 2, t * P:(t + 1) * P], uv[:], start=True, stop=True).then_inc(s["products"], 1)

                @block.scalar
                def _(act):
                    for h in range(8):
                        act.wait_ge(s["products"], 2 * h + 1)
                        nc.scalar.activation(Q[:, h, :], ps[:, 2 * (h % 2), 0:SEQ], ACT.Copy).then_inc(s["act_read"], 1)

                @block.vector
                def _(dve):
                    nc.vector.tensor_scalar(KR[:, 0, :], C[:, GAC, :], self.c("rot_rows", 1), None, ALU.mult).then_inc(s["kr_done"], 1)
                    for h in range(8):
                        dve.wait_ge(s["products"], 2 * h + 2)
                        nc.vector.tensor_copy(K[:, h, :], ps[:, 2 * (h % 2) + 1, 0:SEQ]).then_inc(s["dve_read"], 1)
                    for t in range(2):
                        dve.wait_ge(s["products"], 17 + t)
                        nc.vector.tensor_copy(V_[:, t, :], ps[:, 4 + t, :]).then_inc(s["dve_read"], 1)
            self.rope_tables(cos[:], sin[:], 0)
            self.rotate([Q[:, 2 * j:2 * j + 2, :] for j in range(4)] + [KR[:]], cos[:], sin[:], self.c("swap_mla"))
            with stage(nc, "added") as (block, s):
                @block.vector
                def _(dve):
                    nc.vector.tensor_tensor(K[:], K[:], KR[:].to_broadcast([P, 8, SEQ]), ALU.add).then_inc(s["added"], 1)
            self.attention(8, lambda h: Q[:, h, :], lambda h: K[:, h:h + 1, :],
                           lambda h, b, kt: V_[:, kt, h * 64:(h + 1) * 64], float(np.float32(96.0) ** np.float32(-0.5)),
                           lambda h: H[:, h // 2, 0:SEQ])
        self.out_projection("BA", KD, lambda k: H[:, k, 0:SEQ], 0, SEQ, scale=1.0)

    def sparse_mixer(self):
        nc, ring, ps, H = self.nc, self.ring, self.ps, self.H
        base = ring.chunks
        areas = "BABAB"
        NC = 15
        with ExitStack() as ctx:
            Q = self.sb(ctx, "nsa_q", [P, 16, SEQ])
            K = self.sb(ctx, "nsa_k", [P, 4, SEQ])
            V = self.sb(ctx, "nsa_v", [P, 2, 512])
            KC = self.sb(ctx, "key_cmp", [P, 4, NC])
            VC = self.sb(ctx, "value_cmp", [P, 4, 64])
            GT = self.sb(ctx, "branch_gates", [P, 2, 48])
            cos = self.sb(ctx, "cos", [P, SEQ])
            sin = self.sb(ctx, "sin", [P, SEQ])
            self.rope_tables(cos[:], sin[:], 1)
            with ExitStack() as inner:
                QR = self.sb(inner, "nsa_q_raw", [P, 8, SEQ])
                wg = self.sb(inner, "w_branch_gates", [P, KD, 48])
                W1 = self.sb(inner, "w_cmp1", [P, 2, 4096])
                W2 = self.sb(inner, "w_cmp2", [P, 2, P])
                CM = self.sb(inner, "cmp_masked", [P, 2, 4, SEQ])
                with stage(nc, "w_in act_read dve_read g_sum g_done") as (block, s):
                    def dve_count(j):
                        return j - 7 if j < 12 else 4 + 2 * (j - 11)

                    @block.sync
                    def _(sp):
                        sp.dma_start(wg[:].rearrange("p k n -> p (k n)"), self.d["nsa_g"]).then_inc(s["w_in"], 16)
                        sp.dma_start(W1[:].rearrange("p b n -> p (b n)"), self.d["cmp_w1"]).then_inc(s["w_in"], 16)
                        sp.dma_start(W2[:].rearrange("p b n -> p (b n)"), self.d["cmp_w2"]).then_inc(s["w_in"], 16)
                        for i, area in enumerate(areas):
                            ring.load(sp, area, base + (4 * (i + 1) if i < 4 else 18))
                        sp.wait_ge(s["w_in"], 48)

                    @block.tensor
                    def _(pe):
                        def free(n):
                            if 6 <= n:
                                j = n - 6
                                if j < 8:
                                    pe.wait_ge(s["act_read"], j + 1)
                                else:
                                    pe.wait_ge(s["dve_read"], dve_count(j))
                        for i in range(4):
                            self.panel_products(pe, None, areas[i], KD, 512, lambda k: H[:, k, 0:SEQ], 4 * i, range(6), SEQ, free)
                        area = areas[4]
                        ring.arrived(pe, area)
                        for t in range(2):
                            free(16 + t)
                            for k in range(KD):
                                last = nc.tensor.matmul(ps[:, (16 + t) % 6, :], H[:, k, t * P:(t + 1) * P],
                                                        ring.buf[area][:, k * 512:(k + 1) * 512], start=(k == 0), stop=(k == KD - 1))
                            last.then_inc(ring.chunk_done, 1)
                        pe.wait_ge(s["w_in"], 48)
                        for t in range(2):
                            for k in range(KD):
                                last = nc.tensor.matmul(ps[:, 6, 48 * t:48 * t + 48], H[:, k, t * P:(t + 1) * P], wg[:, k, :],
                                                        start=(k == 0), stop=(k == KD - 1))
                        last.then_inc(s["g_sum"], 1)

                    @block.scalar
                    def _(act):
                        for n in range(8):
                            act.wait_ge(ring.chunk_done, base + n + 1)
                            nc.scalar.activation(QR[:, n, :], ps[:, n % 6, 0:SEQ], ACT.Copy).then_inc(s["act_read"], 1)
                        act.wait_ge(s["g_sum"], 1)
                        nc.scalar.activation(GT[:].rearrange("p t n -> p (t n)"), ps[:, 6, 0:96], ACT.Sigmoid).then_inc(s["g_done"], 1)

                    @block.vector
                    def _(dve):
                        for n in range(8, 16):
                            dve.wait_ge(ring.chunk_done, base + n + 1)
                            if n < 12:
                                branch, pair = divmod(n - 8, 2)
                                nc.vector.tensor_copy(K[:, 2 * pair + branch, :], ps[:, n % 6, 0:SEQ]).then_inc(s["dve_read"], 1)
                            else:
                                kv, pair = divmod(n - 12, 2)
                                for half in range(2):
                                    nc.vector.tensor_scalar(CM[:, kv, 2 * pair + half, :], ps[:, n % 6, 0:SEQ],
                                                            self.c("half", 1, off=half), None, ALU.mult).then_inc(s["dve_read"], 1)
                        for t in range(2):
                            dve.wait_ge(ring.chunk_done, base + 17 + t)
                            nc.vector.tensor_copy(V[:, t, :], ps[:, (16 + t) % 6, :]).then_inc(s["dve_read"], 1)
                ring.chunks += 18
                self.rotate([QR[:, 2 * j:2 * j + 2, :] for j in range(4)] + [K[:, 2 * j:2 * j + 2, :] for j in range(2)],
                            cos[:], sin[:], self.c("swap_nsa"))

                FL = self.sb(inner, "windows", [P, 2, 4, NC, 32])
                hid = self.sb(inner, "cmp_hidden", [P, 2, 4 * NC])
                kraw = self.sb(inner, "cmp_key_raw", [P, 4 * NC])
                part = self.sb(inner, "cmp_key_part", [P, 4 * NC])
                with stage(nc, "windows hidden silu_done k_sum v_sum k_copied swapped link q_masked vc_zero") as (block, s):
                    @block.vector
                    def _(dve):
                        link = chain(dve, s["link"])
                        nc.vector.memset(VC[:], 0.0).then_inc(s["vc_zero"], 1)
                        for kv in range(2):
                            pe_ = self.v(("pos_k", "pos_v")[kv], 0, 32)
                            for g in range(4):
                                x = CM[:, kv, g, :].rearrange("p (m r) -> p m r", r=16)
                                for part_ in range(2):
                                    pos = pe_[:, 16 * part_:16 * part_ + 16].unsqueeze(1).to_broadcast([P, NC, 16])
                                    o = FL[:, kv, g, :, 16 * part_:16 * part_ + 16]
                                    nc.vector.scalar_tensor_tensor(out=o, in0=pos, scalar=self.c("half", 1, off=g % 2),
                                                                   in1=x[:, part_:part_ + NC, :], op0=ALU.mult,
                                                                   op1=ALU.add).then_inc(s["windows"], 1)
                        dve.wait_ge(s["k_sum"], 1)
                        nc.vector.tensor_copy(kraw[:], ps[:, 2, 0:4 * NC]).then_inc(s["k_copied"], 1)
                        dve.wait_ge(s["swapped"], 1)
                        ends = lambda t: t.rearrange("p (m r) -> p m r", r=16)[:, 1:16, 15].unsqueeze(1).to_broadcast([P, 4, NC])
                        as_gn = lambda t: t.rearrange("p (g n) -> p g n", g=4)
                        link(nc.vector.tensor_tensor(as_gn(part[:]), as_gn(ps[:, 4, 0:4 * NC]), ends(sin[:]), ALU.mult))
                        dve.wait_ge(s["k_copied"], 1)
                        link(nc.vector.tensor_tensor(KC[:], as_gn(kraw[:]), ends(cos[:]), ALU.mult))
                        link(nc.vector.tensor_tensor(KC[:], KC[:], as_gn(part[:]), ALU.add))
                        dve.wait_ge(s["v_sum"], 1)
                        dve.wait_ge(s["vc_zero"], 1)
                        nc.vector.tensor_copy(VC[0:NC, :, :], ps[0:NC, 3, 0:256].rearrange("p (g n) -> p g n", g=4)).then_inc(s["k_copied"], 1)

                    @block.tensor
                    def _(pe):
                        for kv in range(2):
                            pe.wait_ge(s["windows"], 8 * (kv + 1))
                            for pos in range(32):
                                last = nc.tensor.matmul(ps[:, kv, 0:4 * NC], W1[:, kv, pos * P:(pos + 1) * P],
                                                        FL[:, kv, :, :, pos].rearrange("p g n -> p (g n)"), start=(pos == 0), stop=(pos == 31))
                            last.then_inc(s["hidden"], 1)
                        pe.wait_ge(s["silu_done"], 1)
                        nc.tensor.matmul(ps[:, 2, 0:4 * NC], W2[:, 0, :], hid[:, 0, :], start=True, stop=True).then_inc(s["k_sum"], 1)
                        pe.wait_ge(s["silu_done"], 2)
                        for g in range(4):
                            last = nc.tensor.matmul(ps[0:NC, 3, g * 64:(g + 1) * 64], hid[:, 1, g * NC:(g + 1) * NC], W2[:, 1, 0:64],
                                                    start=True, stop=True)
                        last.then_inc(s["v_sum"], 1)
                        pe.wait_ge(s["k_copied"], 1)
                        nc.tensor.matmul(ps[:, 4, 0:4 * NC], self.c("swap_nsa"), kraw[:], start=True, stop=True).then_inc(s["swapped"], 1)

                    @block.scalar
                    def _(act):
                        for kv in range(2):
                            act.wait_ge(s["hidden"], kv + 1)
                            nc.scalar.activation(hid[:, kv, :], ps[:, kv, 0:4 * NC], ACT.Silu).then_inc(s["silu_done"], 1)

                    @block.gpsimd
                    def _(pool):
                        for h in range(16):
                            g = h // 4
                            nc.gpsimd.tensor_scalar(Q[:, h, :], QR[:, (g // 2) * 4 + h % 4, :], self.c("half", 1, off=g % 2), None,
                                                    ALU.mult).then_inc(s["q_masked"], 1)
            self.attention(16, lambda h: Q[:, h, :], lambda h: K[:, 2 * (h // 8):2 * (h // 8) + 2, :],
                           lambda h, b, kt: V[:, kt, b * SEQ + (h // 4) * 64:b * SEQ + (h // 4 + 1) * 64], 0.125,
                           lambda h: H[:, h // 2, 0:SEQ],
                           compressed=(lambda h: KC[:, h // 4, :], lambda h: VC[:, h // 4, :]),
                           weights=lambda h, t: GT[:, t, 3 * h:3 * h + 3])
        self.out_projection("AB", KD, lambda k: H[:, k, 0:SEQ], 1, SEQ, scale=1.0)

    def finish(self):
        nc = self.nc
        self.rms_norm(self.x_chunk, self.h_chunk, KD, SEQ, lambda k, c: self.v("final_g2", k))
        with stage(nc, "stored") as (block, s):
            @block.sync
            def _(sp):
                sp.dma_start(self.out.rearrange("p (k t) -> p k t", k=KD), self.H[:, :, 0:SEQ]).then_inc(s["stored"], 16)
                sp.wait_ge(s["stored"], 16)

    def dump(self):
        with stage(self.nc, "stored") as (block, s):
            @block.sync
            def _(sp):
                sp.dma_start(self.out, self.X[:].rearrange("p k t -> p (k t)")).then_inc(s["stored"], 16)
                sp.wait_ge(s["stored"], 16)


def pack_panels(w, cols):
    k, n = w.shape
    return np.ascontiguousarray(w.reshape(k // P, P, n // cols, cols).transpose(2, 1, 0, 3)).reshape(n // cols, P, -1)


def cols_of(v):
    v = np.ascontiguousarray(v).reshape(-1, P)
    return v.T


def constants():
    c = np.zeros((P, NCONST), np.float32)
    i = np.arange(P)

    def put(name, a):
        c[:a.shape[0], CCOL[name]:CCOL[name] + a.shape[1]] = a
    blk = (i[:, None] // 64) == (i[None, :] // 64)
    put("ident", np.eye(P))
    put("ones", np.ones((P, P)))
    put("upper", i[:, None] <= i[None, :])
    put("lower", i[:, None] >= i[None, :])
    put("up64", (i[:, None] <= i[None, :]) & blk)
    put("lo64", (i[:, None] >= i[None, :]) & blk)
    put("xup64", (i[:, None] < i[None, :]) & blk)
    put("xlo64", (i[:, None] > i[None, :]) & blk)
    put("upper_x", i[:, None] < i[None, :])
    put("lower_x", i[:, None] > i[None, :])
    j = np.arange(4)
    put("tie", np.tile((j[None, :] < j[:, None]).reshape(1, 16), (P, 1)))
    put("half", np.stack([i < 64, i >= 64], 1))
    theta = np.float32(10000.0)
    freq = lambda n: np.power(theta, -np.arange(n, dtype=np.float32) * np.float32(1.0 / n)).astype(np.float32)
    rot = (i >= 64) & (i < 96)
    f = np.zeros((P, 2), np.float32)
    f[rot, 0] = np.tile(freq(16), 2)
    f[:, 1] = np.tile(freq(32), 4)
    put("ropef", f)
    put("rot_rows", rot[:, None])
    for name, starts, half in (("swap_mla", (64,), 16), ("swap_nsa", (0, 64), 32)):
        s = np.zeros((P, P), np.float32)
        for at in starts:
            for m in range(half):
                s[at + m + half, at + m] = -1.0
                s[at + m, at + m + half] = 1.0
        put(name, s)
    tri = np.where(i[None, :] <= i[:, None], 0.0, -1e30)
    put("causal_add", np.concatenate([np.zeros((P, P)), tri], 1))
    n = np.arange(16)
    seen = np.concatenate([(16 * n[None, :] + 31 <= i[:, None] + P * t) & (n < 15)[None, :] for t in range(2)], 1)
    put("cmp_mask", seen)
    put("cmp_add", np.where(seen, 0.0, -1e30))
    return c


def arrays_of(x):
    a = {}
    tok = lambda v: np.ascontiguousarray(np.asarray(v)[0].T.reshape(KD, P, SEQ).transpose(1, 0, 2))
    a["x"] = np.concatenate([tok(x["x"]), tok(x["ctx"])], 2).reshape(P, KD * TT)
    a["constants"] = constants()
    vec = {
        "norm_mix": x["norm_mix_g"], "norm_ffn": x["norm_ffn_g"], "mod_b": x["mod_b"], "conv_b": x["ssd_conv_b"],
        "conv_w": x["ssd_conv_w"], "d_skip": np.repeat(np.asarray(x["ssd_d"])[0], 64), "ssd_g": x["ssd_norm_g"],
        "cf_w": x["cf_dw_w"], "cf_b": x["cf_dw_b"], "cf_lng": x["cf_ln_g"], "cf_lnb": x["cf_ln_b"],
        "hg_lb": x["hg_lb"], "hg_g": x["hg_norm_g"], "final_g": x["final_norm_g"], "ffn_norm2": x["ffn_norm_2"],
        "mix_norm2": x["mix_norm_2"], "q_norm": x["mla_q_norm_2"], "kv_norm": x["mla_kv_norm_2"],
        "gla_g": x["gla_out_norm_2"], "final_g2": x["final_norm_2"],
        "cond": np.stack([np.asarray(x["c"])[0], np.asarray(x["c_ctx"])], 1).reshape(KD, P, 2).transpose(0, 2, 1),
    }
    v = np.zeros((P, NV), np.float32)
    for name, value in vec.items():
        c = cols_of(np.asarray(value))
        if name == "cond":
            c = c.reshape(P, KD * 2)
        v[:, VCOL[name]:VCOL[name] + c.shape[1]] = c
    for name, key in (("pos_k", "nsa_pos_k_2"), ("pos_v", "nsa_pos_v_2")):
        v[:, VCOL[name]:VCOL[name] + 32] = np.tile(np.asarray(x[key])[0].T, (2, 1))
    v[:64, VCOL["gla_ba"]:VCOL["gla_ba"] + 4] = np.asarray(x["gla_b_a_2"])[0].reshape(4, 64).T
    a["vectors"] = v
    w = np.asarray(x["mod_w"])
    a["mod_w"] = np.concatenate([pack_panels(w[i], 512) for i in range(2)])
    w = np.asarray(x["ab_w_in"])[0]
    vg = np.concatenate([w[:, 3104:4128].reshape(D, 4, 1, 256), w[:, 4128:5152].reshape(D, 4, 1, 256)], 2).reshape(D, 2048)
    a["ab_in"] = pack_panels(np.concatenate([w[:, :3072], vg], 1), 512)
    a["w_dt"] = np.ascontiguousarray(w[:, 3072:3104].reshape(KD, P, 32).transpose(1, 0, 2)).reshape(P, KD * 32)
    a["ssd_rows"] = np.concatenate([np.asarray(x["ssd_dt_bias"])[0].reshape(-1), np.asarray(x["ssd_a_log"])[0].reshape(-1)])
    a["ab_out"] = pack_panels(np.asarray(x["ab_w_out"])[0], 256)
    a["router_w"] = np.ascontiguousarray(np.asarray(x["router_w"]).reshape(KD, P, 16).transpose(1, 0, 2)).reshape(P, KD * 16)
    a["router_b"] = np.asarray(x["router_b"])
    packs = lambda w, cols: np.ascontiguousarray(
        w.reshape(-1, w.shape[-2] // P, P, w.shape[-1]).transpose(0, 2, 1, 3)).reshape(-1, P, w.shape[-2] // P * w.shape[-1])
    a["moe_gate"] = packs(np.asarray(x["moe_w_gate"]), 512)
    a["moe_up"] = packs(np.asarray(x["moe_w_up"]), 512)
    a["moe_down"] = packs(np.asarray(x["moe_w_down"]).reshape(64, 256, D), D)
    a["lb_rows"] = np.asarray(x["hg_lb"]).reshape(-1)
    a["hg_in"] = pack_panels(np.asarray(x["hg_w_in"])[0], 512)
    a["hg_out"] = pack_panels(np.asarray(x["hg_w_out"])[0], 512)
    g = np.asarray(x["ffn_w_gate_2"]).reshape(4, KD, P, 11, 1, 256)
    u = np.asarray(x["ffn_w_up_2"]).reshape(4, KD, P, 11, 1, 256)
    a["ffn_gu"] = np.concatenate([g, u], 4).transpose(0, 3, 2, 1, 4, 5).reshape(44, P, 4096)
    a["ffn_down"] = packs(np.asarray(x["ffn_w_down_2"]).reshape(44, 256, D), D)
    w = np.asarray(x["hy_w_in_2"])[0]
    pad = lambda n: np.zeros((D, n), np.float32)
    a["hy_in"] = pack_panels(np.concatenate(
        [w[:, :384], w[:, 1440:1456], pad(48), w[:, 384:416], pad(32), w[:, 1456:1968], w[:, 416:928], w[:, 928:1440]], 1), 512)
    a["hy_out"] = pack_panels(np.asarray(x["hy_w_out_2"])[0], 512)
    w = np.asarray(x["mla_w_uq_2"])[0].reshape(2, P, 8, 96)
    a["w_uq"] = np.concatenate([w, np.zeros((2, P, 8, 32), np.float32)], 3).transpose(1, 0, 2, 3).reshape(P, 2048)
    w = np.asarray(x["mla_w_ukv_2"])[0].reshape(P, 8, 2, 64)
    a["w_uk"] = np.concatenate([w[:, :, 0], np.zeros((P, 8, 64), np.float32)], 2).reshape(P, D)
    a["w_uv"] = np.ascontiguousarray(w[:, :, 1]).reshape(P, 512)
    a["w_a2"] = np.concatenate([np.asarray(x["gla_w_a2_2"])[0], np.zeros((P - 16, SEQ), np.float32)], 0)
    a["gla_ba"] = np.asarray(x["gla_b_a_2"]).reshape(-1)
    a["positions"] = np.asarray(x["positions_2"])[0]
    w1 = [np.asarray(x[n])[0].reshape(32, 64, P).transpose(1, 0, 2).reshape(64, 4096) for n in ("nsa_ck_w1_2", "nsa_cv_w1_2")]
    a["cmp_w1"] = np.concatenate([np.concatenate([w, w], 0) for w in w1], 1)
    w2 = [np.asarray(x[n])[0] for n in ("nsa_ck_w2_2", "nsa_cv_w2_2")]
    a["cmp_w2"] = np.concatenate([np.concatenate([w, w], 1) for w in w2], 1)
    w = np.asarray(x["nsa_w_in_2"])[0]
    wq = w[:, :1024].reshape(D, 2, 2, 4, 64).transpose(0, 1, 3, 2, 4).reshape(D, 1024)
    a["nsa_in"] = pack_panels(np.concatenate(
        [wq, w[:, 1536:1792], w[:, 2048:2304], w[:, 1024:1536], w[:, 1792:2048], w[:, 2304:2560]], 1), 512)
    a["nsa_g"] = np.ascontiguousarray(w[:, 2560:2608].reshape(D, 16, 3)[:, :, [1, 2, 0]].reshape(KD, P, 48).transpose(1, 0, 2)).reshape(P, KD * 48)
    a["nsa_out"] = pack_panels(np.asarray(x["nsa_w_out_2"])[0], 512)
    return a


def build(nc, d, out, stages=None):
    with ExitStack() as ctx:
        p = Program(nc, ctx, d, out)
        p.plan()
        everything(p, stages)


def everything(p, stop=None):
    p.load_inputs()
    p.modulation()
    x, h = p.x_chunk, p.h_chunk
    p.rms_norm(x, h, KD, TT, lambda k, c: p.scale_mod[:, 0, k, c:c + 1], lambda k, c: p.m(0, 0, k, c))
    p.even_mixer()
    if stop == "mix0":
        return p.dump()
    p.rms_norm(x, h, KD, TT, lambda k, c: p.scale_mod[:, 1, k, c:c + 1], lambda k, c: p.m(0, 3, k, c))
    p.experts(0, TT)
    if stop == "moe0":
        return p.dump()
    p.rms_norm(x, h, KD, TT, lambda k, c: p.scale_mod[:, 2, k, c:c + 1], lambda k, c: p.m(1, 0, k, c), permuted=True)
    p.odd_mixer()
    if stop == "mix1":
        return p.dump()
    p.rms_norm(x, h, KD, SEQ, lambda k, c: p.scale_mod[:, 3, k, c:c + 1], lambda k, c: p.m(1, 3, k, c))
    p.experts(1, SEQ)
    if stop == "moe1":
        return p.dump()
    p.rms_norm(x, x, KD, SEQ, lambda k, c: p.v("final_g", k))
    p.feed_forward(0)
    if stop == "f0a":
        return p.dump()
    p.rms_norm(x, h, KD, SEQ, lambda k, c: p.v("mix_norm2", k))
    p.hybrid_mixer()
    if stop == "m0":
        return p.dump()
    p.feed_forward(1)
    p.feed_forward(2)
    if stop == "f1a":
        return p.dump()
    p.rms_norm(x, h, KD, SEQ, lambda k, c: p.v("mix_norm2", 8 + k))
    p.sparse_mixer()
    if stop == "m1":
        return p.dump()
    p.feed_forward(3)
    p.finish()


def kernel(**inputs):
    import concourse.bacc as _bacc
    from concourse.bass_utils import run_bass_kernel_spmd as _run

    nc = _bacc.Bacc("TRN2", target_bir_lowering=False, num_devices=1)
    arrays = {f"in_{k}": np.ascontiguousarray(v) for k, v in arrays_of(inputs).items()}
    d = {k[3:]: nc.dram_tensor(k, v.shape, mybir.dt.from_np(v.dtype), kind="ExternalInput").ap() for k, v in arrays.items()}
    out = nc.dram_tensor("out", (P, KD * SEQ), F32, kind="ExternalOutput").ap()
    build(nc, d, out)
    r = _run(nc, [arrays], core_ids=[0]).results[0]["out"]
    return np.ascontiguousarray(np.asarray(r).reshape(P, KD, SEQ).transpose(2, 1, 0)).reshape(1, SEQ, D)
```
